# Optimizing a Trainium2 kernel written in Bass

```python
import jax, jax.numpy as jnp
from jax import lax
import numpy as np

D_MODEL = 1024
BATCH = 1
SEQ = 256
DEPTH = 2

N_MIXERS = 2
MIX_WIDTH = D_MODEL
MEM_TOKENS = 256
MEM_HEADS = 4
MEM_WIDTH = MIX_WIDTH // 4
MEM_HEAD_DIM = MEM_WIDTH // MEM_HEADS
MAIN_WIDTH = MIX_WIDTH - MEM_WIDTH
ML_HEADS = 4
ML_HEAD_DIM = MAIN_WIDTH // ML_HEADS
ML_CHUNK = 64
CONV_WIDTH = 4
MLA_HEADS = 6
MLA_NOPE = 128
MLA_ROPE = 64
MLA_QK = MLA_NOPE + MLA_ROPE
MLA_V = MAIN_WIDTH // MLA_HEADS
Q_LORA = 384
KV_LORA = 128
ROPE_THETA = 10000.0
Q_BLOCK = 128
D_FF = 3584
N_EXPERTS = 8
TOP_K = 2
EPS = 1e-6
ML_IN = 4 * MAIN_WIDTH + 2 * ML_HEADS + MEM_WIDTH
MLA_IN = Q_LORA + KV_LORA + MLA_ROPE + MEM_WIDTH

kernel_name = "hybrid_mlstm_mla_memory_moe"

def split_cols(t, sizes):
    idx = np.cumsum(sizes)[:-1].tolist()
    return jnp.split(t, idx, axis=-1)

def rms_norm(x, g):
    xf = x.astype(jnp.float32)
    y = xf * lax.rsqrt(jnp.mean(xf * xf, axis=-1, keepdims=True) + EPS)
    return (y * g.astype(jnp.float32)).astype(x.dtype)

def swiglu(x, w_gate, w_up, w_down):
    return (jax.nn.silu(x @ w_gate) * (x @ w_up)) @ w_down

def causal_depthwise_conv(u, w):
    C = u.shape[-1]
    return lax.conv_general_dilated(
        u, w[:, None, :].astype(u.dtype), window_strides=(1,),
        padding=[(w.shape[0] - 1, 0)], dimension_numbers=('NWC', 'WIO', 'NWC'),
        feature_group_count=C)

def rope_tail(t, positions):
    half = MLA_ROPE // 2
    inv_freq = ROPE_THETA ** (-jnp.arange(half, dtype=jnp.float32) / half)
    ang = positions.astype(jnp.float32)[..., None] * inv_freq
    cos = jnp.cos(ang)[:, :, None, :]
    sin = jnp.sin(ang)[:, :, None, :]
    t_pass, t_rot = t[..., :-MLA_ROPE], t[..., -MLA_ROPE:]
    x1 = t_rot[..., :half].astype(jnp.float32)
    x2 = t_rot[..., half:].astype(jnp.float32)
    rot = jnp.concatenate([x1 * cos - x2 * sin, x2 * cos + x1 * sin], axis=-1).astype(t.dtype)
    return jnp.concatenate([t_pass, rot], axis=-1)

def memory_attention(mq, mem_k, mem_v, q_gain, k_gain):
    B, S, _ = mq.shape
    q = rms_norm(mq.reshape(B, S, MEM_HEADS, MEM_HEAD_DIM), q_gain)
    k = rms_norm(mem_k, k_gain)
    s = jnp.einsum('bshd,bmhd->bhsm', q, k).astype(jnp.float32) * MEM_HEAD_DIM ** -0.5
    p = jax.nn.softmax(s, axis=-1).astype(mem_v.dtype)
    return jnp.einsum('bhsm,bmhd->bshd', p, mem_v).reshape(B, S, MEM_WIDTH)

def mlstm_chunkwise(q, k, v, i_pre, log_f):
    B, S, H, Dh = q.shape
    L = ML_CHUNK
    NC = S // L
    f32 = jnp.float32

    def chunks(t):
        t = t.astype(f32).reshape((B, NC, L, H) + t.shape[3:])
        return jnp.moveaxis(t, (1, 3), (0, 2))

    xs = (chunks(q), chunks(k) * Dh ** -0.5, chunks(v), chunks(i_pre), chunks(log_f))
    causal = jnp.tril(jnp.ones((L, L), dtype=bool))

    def step(carry, inp):
        C, n, m = carry
        qc, kc, vc, ig, lf = inp
        b = jnp.cumsum(lf, axis=-1)
        log_d = jnp.where(causal, b[..., :, None] - b[..., None, :] + ig[..., None, :], -jnp.inf)
        inter = b + m[..., None]
        m_row = jnp.maximum(inter, jnp.max(log_d, axis=-1))
        d = jnp.exp(log_d - m_row[..., None])
        s_inter = jnp.exp(inter - m_row)
        qk = jnp.einsum('bhld,bhsd->bhls', qc, kc) * d
        num = jnp.einsum('bhls,bhsd->bhld', qk, vc) + s_inter[..., None] * jnp.einsum('bhvk,bhlk->bhlv', C, qc)
        den = jnp.sum(qk, axis=-1) + s_inter * jnp.einsum('bhk,bhlk->bhl', n, qc)
        h = num / jnp.maximum(jnp.abs(den), jnp.exp(-m_row))[..., None]
        b_last = b[..., -1]
        g = b_last[..., None] - b + ig
        m_new = jnp.maximum(b_last + m, jnp.max(g, axis=-1))
        w = jnp.exp(g - m_new[..., None])
        decay = jnp.exp(b_last + m - m_new)
        C_new = decay[..., None, None] * C + jnp.einsum('bhs,bhsv,bhsk->bhvk', w, vc, kc)
        n_new = decay[..., None] * n + jnp.einsum('bhs,bhsk->bhk', w, kc)
        return (C_new, n_new, m_new), h

    init = (jnp.zeros((B, H, Dh, Dh), f32), jnp.zeros((B, H, Dh), f32), jnp.zeros((B, H), f32))
    _, hs = lax.scan(step, init, xs)
    return jnp.moveaxis(hs, (0, 2), (1, 3)).reshape(B, S, H, Dh).astype(q.dtype)

def causal_block_attention(q, k, v):
    B, S, H, Dq = q.shape
    qh = q.transpose(0, 2, 1, 3)
    kh = k.transpose(0, 2, 1, 3)
    vh = v.transpose(0, 2, 1, 3)
    kpos = jnp.arange(S)
    scale = Dq ** -0.5

    def block(i):
        start = i * Q_BLOCK
        qb = lax.dynamic_slice_in_dim(qh, start, Q_BLOCK, axis=2)
        s = jnp.einsum('bhqd,bhkd->bhqk', qb, kh).astype(jnp.float32) * scale
        qpos = start + jnp.arange(Q_BLOCK)
        s = jnp.where(kpos[None, :] <= qpos[:, None], s, -jnp.inf)
        p = jax.nn.softmax(s, axis=-1).astype(vh.dtype)
        return jnp.einsum('bhqk,bhkd->bqhd', p, vh)

    out = lax.map(block, jnp.arange(S // Q_BLOCK))
    return jnp.moveaxis(out, 0, 1).reshape(B, S, H, v.shape[-1])

def mlstm_layer(xn, mem_k, mem_v, w_in, conv_w, b_i, b_f, h_norm, mq_norm, mk_norm, w_out):
    B, S, _ = xn.shape
    qk, v, o, ig, fg, mq = split_cols(xn @ w_in, [2 * MAIN_WIDTH, MAIN_WIDTH, MAIN_WIDTH, ML_HEADS, ML_HEADS, MEM_WIDTH])
    qk = jax.nn.silu(causal_depthwise_conv(qk, conv_w))
    q, k = jnp.split(qk, 2, axis=-1)
    heads = lambda t: t.reshape(B, S, ML_HEADS, ML_HEAD_DIM)
    i_pre = (ig + b_i).astype(jnp.float32)
    log_f = jax.nn.log_sigmoid((fg + b_f).astype(jnp.float32))
    h_tilde = mlstm_chunkwise(heads(q), heads(k), heads(v), i_pre, log_f)
    h = rms_norm(h_tilde, h_norm) * jax.nn.sigmoid(heads(o))
    y_mem = memory_attention(mq, mem_k, mem_v, mq_norm, mk_norm)
    return jnp.concatenate([h.reshape(B, S, MAIN_WIDTH), y_mem], axis=-1) @ w_out

def mla_layer(xn, positions, mem_k, mem_v, w_in, cq_norm, ckv_norm, w_uq, w_ukv, q_norm, k_norm, mq_norm, mk_norm, w_out):
    B, S, _ = xn.shape
    c_q, c_kv, k_r, mq = split_cols(xn @ w_in, [Q_LORA, KV_LORA, MLA_ROPE, MEM_WIDTH])
    q = (rms_norm(c_q, cq_norm) @ w_uq).reshape(B, S, MLA_HEADS, MLA_QK)
    kv = (rms_norm(c_kv, ckv_norm) @ w_ukv).reshape(B, S, MLA_HEADS, MLA_NOPE + MLA_V)
    k_nope, v = jnp.split(kv, [MLA_NOPE], axis=-1)
    k = jnp.concatenate([k_nope, jnp.broadcast_to(k_r[:, :, None, :], (B, S, MLA_HEADS, MLA_ROPE))], axis=-1)
    q = rope_tail(rms_norm(q, q_norm), positions)
    k = rope_tail(rms_norm(k, k_norm), positions)
    o = causal_block_attention(q, k, v)
    y_mem = memory_attention(mq, mem_k, mem_v, mq_norm, mk_norm)
    return jnp.concatenate([o.reshape(B, S, MAIN_WIDTH), y_mem], axis=-1) @ w_out

def moe_swiglu(xn, w_router, we_gate, we_up, we_down):
    logits = (xn @ w_router).astype(jnp.float32)
    top_v, top_i = lax.top_k(logits, TOP_K)
    top_w = jax.nn.softmax(top_v, axis=-1)
    gates = jnp.sum(jax.nn.one_hot(top_i, N_EXPERTS, dtype=jnp.float32) * top_w[..., None], axis=-2)
    y = jnp.zeros_like(xn)
    for e in range(N_EXPERTS):
        y = y + gates[..., e:e + 1].astype(xn.dtype) * swiglu(xn, we_gate[e], we_up[e], we_down[e])
    return y

def setup_inputs(seed: int = 0) -> dict:
    key = jax.random.key(seed)
    ks = iter(jax.random.split(key, 48))
    f32 = jnp.float32
    nrm = lambda shape, fan_in: jax.random.normal(next(ks), shape, f32) * fan_in ** -0.5
    gain = lambda n: 1.0 + 0.02 * jax.random.normal(next(ks), (n,), f32)
    x = jax.random.normal(next(ks), (BATCH, SEQ, D_MODEL), f32)
    mem = jax.random.normal(next(ks), (BATCH, MEM_TOKENS, D_MODEL), f32)
    offset = jax.random.randint(next(ks), (BATCH, 1), 0, 1024, dtype=jnp.int32)
    positions = offset + jnp.arange(SEQ, dtype=jnp.int32)[None, :]
    return {
        "x": x, "mem": mem, "positions": positions,
        "mem_norm": gain(D_MODEL), "w_mem_kv": nrm((D_MODEL, 2 * MEM_WIDTH), D_MODEL),
        "ln_mix0": gain(D_MODEL), "w_in0": nrm((D_MODEL, ML_IN), D_MODEL),
        "conv_w0": nrm((CONV_WIDTH, 2 * MAIN_WIDTH), CONV_WIDTH),
        "b_i0": 0.1 * jax.random.normal(next(ks), (ML_HEADS,), f32),
        "b_f0": 3.0 + 0.1 * jax.random.normal(next(ks), (ML_HEADS,), f32),
        "h_norm0": gain(ML_HEAD_DIM), "mq_norm0": gain(MEM_HEAD_DIM), "mk_norm0": gain(MEM_HEAD_DIM),
        "w_out0": nrm((MIX_WIDTH, D_MODEL), MIX_WIDTH),
        "ln_ffn0": gain(D_MODEL), "w_gate0": nrm((D_MODEL, D_FF), D_MODEL),
        "w_up0": nrm((D_MODEL, D_FF), D_MODEL), "w_down0": nrm((D_FF, D_MODEL), D_FF),
        "ln_mix1": gain(D_MODEL), "w_in1": nrm((D_MODEL, MLA_IN), D_MODEL),
        "cq_norm1": gain(Q_LORA), "ckv_norm1": gain(KV_LORA),
        "w_uq1": nrm((Q_LORA, MLA_HEADS * MLA_QK), Q_LORA),
        "w_ukv1": nrm((KV_LORA, MLA_HEADS * (MLA_NOPE + MLA_V)), KV_LORA),
        "q_norm1": gain(MLA_QK), "k_norm1": gain(MLA_QK),
        "mq_norm1": gain(MEM_HEAD_DIM), "mk_norm1": gain(MEM_HEAD_DIM),
        "w_out1": nrm((MIX_WIDTH, D_MODEL), MIX_WIDTH),
        "ln_ffn1": gain(D_MODEL), "w_router1": nrm((D_MODEL, N_EXPERTS), D_MODEL),
        "we_gate1": nrm((N_EXPERTS, D_MODEL, D_FF), D_MODEL),
        "we_up1": nrm((N_EXPERTS, D_MODEL, D_FF), D_MODEL),
        "we_down1": nrm((N_EXPERTS, D_FF, D_MODEL), D_FF),
    }

def reference(x, mem, positions, mem_norm, w_mem_kv,
              ln_mix0, w_in0, conv_w0, b_i0, b_f0, h_norm0, mq_norm0, mk_norm0, w_out0,
              ln_ffn0, w_gate0, w_up0, w_down0,
              ln_mix1, w_in1, cq_norm1, ckv_norm1, w_uq1, w_ukv1, q_norm1, k_norm1, mq_norm1, mk_norm1, w_out1,
              ln_ffn1, w_router1, we_gate1, we_up1, we_down1):
    B, M, _ = mem.shape
    mem_k, mem_v = jnp.split(rms_norm(mem, mem_norm) @ w_mem_kv, 2, axis=-1)
    mem_k = mem_k.reshape(B, M, MEM_HEADS, MEM_HEAD_DIM)
    mem_v = mem_v.reshape(B, M, MEM_HEADS, MEM_HEAD_DIM)
    h = x
    for layer in range(DEPTH):
        if layer % N_MIXERS == 0:
            h = h + mlstm_layer(rms_norm(h, ln_mix0), mem_k, mem_v, w_in0, conv_w0, b_i0, b_f0,
                                h_norm0, mq_norm0, mk_norm0, w_out0)
        else:
            h = h + mla_layer(rms_norm(h, ln_mix1), positions, mem_k, mem_v, w_in1, cq_norm1, ckv_norm1,
                              w_uq1, w_ukv1, q_norm1, k_norm1, mq_norm1, mk_norm1, w_out1)
        if layer % 2 == 0:
            h = h + swiglu(rms_norm(h, ln_ffn0), w_gate0, w_up0, w_down0)
        else:
            h = h + moe_swiglu(rms_norm(h, ln_ffn1), w_router1, we_gate1, we_up1, we_down1)
    return h


_drawn_inputs = setup_inputs


def setup_inputs(seed=0):
    import zlib

    import numpy as np

    out = dict(_drawn_inputs(seed))
    spreads = {}
    factors = {'mem_norm': 3.296,
     'b_i0': 64.0,
     'mq_norm0': 8.0,
     'mk_norm0': 4.388,
     'ln_mix1': 3.004,
     'cq_norm1': 4.691,
     'ckv_norm1': 3.122,
     'q_norm1': 2.763,
     'k_norm1': 4.873,
     'mq_norm1': 8.0,
     'mk_norm1': 8.0,
     'ln_ffn1': 4.959}
    for name, (base, spread) in spreads.items():
        noise = np.random.default_rng([zlib.crc32(name.encode()), seed]).standard_normal(out[name].shape)
        drawn = base * np.exp(spread * noise) if base else spread * noise
        out[name] = __import__('jax').numpy.asarray(drawn.astype(out[name].dtype))
    for name, factor in factors.items():
        out[name] = (out[name] * factor).astype(out[name].dtype)
    return out
```

```python
from contextlib import ExitStack

import concourse.bass as bass
from concourse import mybir

F32 = mybir.dt.float32
F32R = mybir.dt.float32r
I32 = mybir.dt.int32
ALU = mybir.AluOpType
ACT = mybir.ActivationFunctionType
AX = mybir.AxisListType.X

P = 128
EPS = 1e-6
ROPE_THETA = 10000.0
NEG = -1e30
TWO_PI = (201 / 32, 2029 / 2**20, 3.0199159819e-07)
INV_2PI = 0.15915494309189535
HALF_PI = 1.5707963267948966
PI_BOUND = 3.1415925
MAGIC = 1.5 * 2**23
RSQRT_BITS = float(0x5F3759DF)

RAW_SLOTS = 6
SPLIT_SLOTS = 6
CHUNK = 2048
PIECE = CHUNK // 2


def hybrid_trunk(
    nc: bass.Bass,
    x, mem, positions, mem_norm, w_mem_kv,
    ln_mix0, w_in0, conv_w0, b_i0, b_f0, h_norm0, mq_norm0, mk_norm0, w_out0,
    ln_ffn0, w_gate0, w_up0, w_down0,
    ln_mix1, w_in1, cq_norm1, ckv_norm1, w_uq1, w_ukv1, q_norm1, k_norm1, mq_norm1, mk_norm1, w_out1,
    ln_ffn1, w_router1, we_gate1, we_up1, we_down1,
    out,
):
    _, S, D = x.shape
    TB = S // P
    KD = D // P
    MH = 4
    MEMW = w_mem_kv.shape[1] // 2
    MD = MEMW // MH
    MAIN = D - MEMW
    LH = b_i0.shape[0]
    LD = MAIN // LH
    HB = LD // 2
    QKB = 2 * MAIN // HB
    TAPS = conv_w0.shape[0]
    NOPE = 128
    ROPE = MD
    HALF = ROPE // 2
    QKD = q_norm1.shape[0]
    AH = w_uq1.shape[1] // QKD
    VD = MAIN // AH
    QL = w_uq1.shape[0]
    NE = w_router1.shape[1]
    FF = w_gate0.shape[1]
    FC = 512
    NF = FF // FC
    FB = FC // P
    NU_MAX = 3
    UNITS = NE + NU_MAX
    assert (S, D, MD, LD, AH, QL) == (256, 1024, 64, 192, 6, 384) and FF % FC == 0

    with ExitStack() as ctx:
        sem_of = {}

        def sem(name):
            if name not in sem_of:
                sem_of[name] = ctx.enter_context(nc.semaphore(name))
            return sem_of[name]

        def sb(name, shape, dt=F32, scope=ctx):
            return scope.enter_context(nc.sbuf_tensor(name, shape, dt))

        B = [ctx.enter_context(nc.psum_tensor(f"bank{i}", [P, 512], F32)) for i in range(8)]

        raw = sb("raw", [P, RAW_SLOTS, CHUNK])
        w_hi = sb("w_hi", [P, SPLIT_SLOTS, PIECE], F32R)
        w_lo = sb("w_lo", [P, SPLIT_SLOTS, PIECE], F32R)
        h = sb("h", [P, TB, D])
        xT_hi = sb("xT_hi", [P, KD, S], F32R)
        xT_lo = sb("xT_lo", [P, KD, S], F32R)
        xr = sb("xr", [P, TB, D])
        ident = sb("ident", [P, P])
        ones = sb("ones", [P, P])
        upto = sb("upto", [P, 2, P])
        before = sb("before", [P, P])
        negmask = sb("negmask", [P, 3, P])
        iota = sb("iota", [P, P])
        earlier = sb("earlier", [P, NE, NE])
        gain_rows = sb("gain_rows", [P, P])
        gains = sb("gains", [P, P])
        conv_rows = sb("conv_rows", [TAPS * QKB, HB])
        convw = sb("convw", [HB, TAPS * QKB])
        hnorm_bc = sb("hnorm_bc", [P, LD])
        qrope_bc = sb("qrope_bc", [P, ROPE])
        krope_bc = sb("krope_bc", [P, ROPE])
        gate_bias = sb("gate_bias", [LH, 2])
        pos_i = sb("pos_i", [P, TB], I32)
        w_router = sb("w_router", [P, KD, NE])
        wr_hi = sb("wr_hi", [P, KD, NE], F32R)
        wr_lo = sb("wr_lo", [P, KD, NE], F32R)
        cos = sb("cos", [P, TB, HALF])
        sin = sb("sin", [P, TB, HALF])
        stat = sb("stat", [P, 5, 40])
        kmT = sb("kmT", [P, 2, S])
        vm = sb("vm", [P, TB, MEMW])
        small = sb("small", [P, 64])

        rows, at = {}, 0
        for name, vec in (("mem", mem_norm), ("mix0", ln_mix0), ("ffn0", ln_ffn0), ("mix1", ln_mix1),
                          ("ffn1", ln_ffn1), ("cq", cq_norm1), ("ckv", ckv_norm1)):
            rows[name] = (at, vec)
            at += vec.shape[0] // P
        G_QN, G_KN, G_MQ, G_MK = at, at + 1, (at + 2, at + 3), (at + 4, at + 5)
        N_GAINS = at + 6
        G = {name: a for name, (a, _) in rows.items()}

        y = xr
        qmT = sb("qmT", [P, 2, S])
        part = ExitStack()
        with part:
            km = sb("km", [P, TB, MEMW], scope=part)
            angle = sb("angle", [P, 4, TB, HALF], scope=part)
            qk_in = sb("qk_in", [HB, 2, 4, S + TAPS - 1], scope=part)
            qkT = sb("qkT", [HB, QKB, S], scope=part)
            vA = sb("vA", [P, TB, LH, LD + 2], scope=part)
            og = sb("og", [P, TB, MAIN], scope=part)
            gm = sb("gm", [P, TB, 2 * LH + MEMW], scope=part)
            gr = sb("gr", [LH, 8, S], scope=part)
            decay = sb("decay", [P, LH, 384], scope=part)
            num = sb("num", [P, TB, LH, LD + 2], scope=part)
            headsel = sb("headsel", [LH, LH, P], scope=part)
        part = ExitStack()
        with part:
            c1 = sb("c1", [P, TB, QL + P], scope=part)
            c2 = sb("c2", [P, TB, ROPE + MEMW], scope=part)
            qS = sb("qS", [P, TB, AH, QKD], scope=part)
            kS = sb("kS", [P, TB, AH, NOPE], scope=part)
            vS = sb("vS", [P, TB, AH, VD], scope=part)
            rotq = sb("rotq", [P, TB, AH, ROPE], scope=part)
            rotk = sb("rotk", [P, TB, AH, ROPE], scope=part)
            kr = sb("kr", [P, 4, TB, ROPE], scope=part)
            scr = sb("scr", [P, AH, 384], scope=part)
            qT = sb("qT", [P, AH, S], scope=part)
            kT = sb("kT", [P, AH, S], scope=part)
            qrT = sb("qrT", [P, AH // 2, S], scope=part)
            krT = sb("krT", [P, AH // 2, S], scope=part)
        part = ExitStack()
        with part:
            aT_hi = sb("aT_hi", [P, FB, S], F32R, scope=part)
            aT_lo = sb("aT_lo", [P, FB, S], F32R, scope=part)
            silu_g = sb("silu_g", [P, FB * S], scope=part)
            act_f = sb("act_f", [P, FB * S], scope=part)
            xr_hi = sb("xr_hi", [P, TB, D], F32R, scope=part)
            xr_lo = sb("xr_lo", [P, TB, D], F32R, scope=part)
            ys_hi = sb("ys_hi", [P, D], F32R, scope=part)
            ys_lo = sb("ys_lo", [P, D], F32R, scope=part)
            onehot = sb("onehot", [P, TB, P], F32R, scope=part)
            onehotT = sb("onehotT", [P, S], F32R, scope=part)
            lg = sb("lg", [P, TB, NE], scope=part)
            rt = sb("rt", [P, 16, TB, NE], scope=part)
            cmp = sb("cmp", [P, 3, TB, NE, NE], scope=part)
            posc = sb("posc", [P, TB + 1, NE], scope=part)
            tab = sb("tab", [P, UNITS, 3, TB], scope=part)
            cur = sb("cur", [P, 3, TB], scope=part)
            over = sb("over", [P, 8, NE], scope=part)
            unit_f = sb("unit_f", [1, 4], scope=part)
            unit_i = sb("unit_i", [1, 4], I32, scope=part)
            gslot = sb("gslot", [P, 1], scope=part)
        flat = lambda t: t.rearrange("p a b c -> p (a b c)")
        flat3 = lambda t: t.rearrange("p a b -> p (a b)")
        pT = flat(qS[:, :, :, :]).rearrange("p (h c) -> p h c", h=AH)
        kmTs_0, kmTs_1 = km[:, :, :], c1[:, 0, :].rearrange("p (a s) -> p a s", a=2)
        pm_0 = lambda t, hd: (flat3(decay[:, :, :]) if t == 0 else flat3(og[:, :, :]))[:, hd * S:(hd + 1) * S]
        pmT_0 = lambda hd: (flat(num[:, :, :, :])[:, hd * 512:(hd + 1) * 512] if hd < 3 else flat(vA[:, :, :, :])[:, 0:512])
        pm_1 = lambda t, hd: flat3(scr[:, :, :])[:, (t * MH + hd) * S:(t * MH + hd + 1) * S]
        pmT_1 = lambda hd: flat(qS[:, :, :, :])[:, hd * 512:(hd + 1) * 512]

        chunks = []

        def add_chunk(view_shape, src):
            chunks.append((view_shape, src))
            return len(chunks) - 1

        def k_halves(w, c0, n):
            v = w.rearrange("(j k p) n -> j p k n", j=2, p=P)
            return [add_chunk((KD // 2, n), v[j, :, :, c0:c0 + n]) for j in range(2)]

        C_MEM = k_halves(w_mem_kv, 0, 2 * MEMW)[0]
        C_QK = len(chunks)
        for t in range(8):
            k_halves(w_in0, t * 384, 384)
        C_V = C_QK + 8
        C_GM = k_halves(w_in0, 4 * MAIN, 2 * LH + MEMW)[0]
        C_OUT0 = len(chunks)
        for t in range(2):
            k_halves(w_out0, 512 * t, 512)
        C_FFN = len(chunks)
        FFN_CHUNKS = 6 * NF
        C_IN1 = C_FFN + FFN_CHUNKS
        chunks_b = []
        first, chunks = chunks, chunks_b
        k_halves(w_in1, 0, 512)
        k_halves(w_in1, 512, 320)
        C_UQ = C_IN1 + len(chunks)
        for t in range(3):
            add_chunk((QL // P, 384), w_uq1.rearrange("(k p) n -> p k n", p=P)[:, :, 384 * t:384 * t + 384])
        C_UKV = C_IN1 + len(chunks)
        for t in range(3):
            add_chunk((2, 256), w_ukv1.rearrange("p (t a n) -> p t a n", t=3, a=2)[:, t])
        C_OUT1 = C_IN1 + len(chunks)
        for t in range(2):
            k_halves(w_out1, 512 * t, 512)
        C_MOE = C_IN1 + len(chunks)
        sizes = {i: s for i, (s, _) in enumerate(first)} | {C_IN1 + i: s for i, (s, _) in enumerate(chunks)}
        straight = {i: v for i, (_, v) in enumerate(first)} | {C_IN1 + i: v for i, (_, v) in enumerate(chunks)}
        UP, DOWN = (KD // 2, FC), (2, D)

        def view(t, slot, shape):
            k, n = shape
            return t[:, slot, 0:k * n].rearrange("p (k n) -> p k n", k=k)

        def pieces_of(shape):
            k = shape[0]
            return ((0, (k + 1) // 2), ((k + 1) // 2, k // 2))

        def raw_piece(c, shape, half):
            k0, nk = pieces_of(shape)[half]
            return view(raw, c % RAW_SLOTS, shape)[:, k0:k0 + nk, :]

        def split_piece(t, c, shape, half):
            return view(t, (2 * c + half) % SPLIT_SLOTS, (pieces_of(shape)[half][1], shape[1]))

        TERMS = ((0, 0), (0, 1), (1, 0))
        xT = (xT_hi, xT_lo)
        wS = (w_hi, w_lo)
        aT = (aT_hi, aT_lo)
        F = lambda ap: ap.bitcast(F32)

        raw_here = [sem(f"raw_here{i}") for i in range(RAW_SLOTS)]
        hi_ready, lo_ready, piece_used = sem("hi_ready"), sem("lo_ready"), sem("piece_used")
        part_done = sem("part_done")
        N_PARTS = 3

        N_ROW_DMAS = len(rows) + 2 + 8 + 1
        TILE_OUT0, TILE_IN1, TILE_OUT1 = 6, 8, 16

        def shape_of(c):
            return sizes.get(c, UP)

        block = ctx.enter_context(nc.Block())

        @block.sync
        def _(sp):
            sp.dma_start(h[:, 0, :], x.rearrange("o (b p) d -> p (o b) d", p=P)[:, 0, :]).then_inc(sem("x_here"), 16)
            sp.dma_start(h[:, 1, :], x.rearrange("o (b p) d -> p (o b) d", p=P)[:, 1, :]).then_inc(sem("x_here"), 16)
            sp.dma_start(xr[:, :, :], mem.rearrange("o (b p) d -> p (o b) d", p=P)).then_inc(sem("mem_here"), 16)

            def fetch(c, shape, src, more=0):
                if c >= RAW_SLOTS:
                    sp.wait_ge(lo_ready, 2 * (c - RAW_SLOTS + 1 + more))
                slot = c % RAW_SLOTS
                sp.dma_start(view(raw, slot, shape), src).then_inc(raw_here[slot], 16)

            def swiglu_chunks(c0, gate, up, down, more=0):
                def step(c, f, last=None, more=more):
                    for w in (gate, up):
                        for j in range(2):
                            fetch(c, UP, w(j, f), more)
                            c += 1
                    if last is not None:
                        for j in range(2):
                            fetch(c, DOWN, down(j, last), more)
                            c += 1
                step(c0, 0)
                with sp.Fori(0, NF - 1) as i:
                    step(c0 + 4, i + 1, i, more + 6 * i)
                for j in range(2):
                    fetch(c0 + 40 + j, DOWN, down(j, NF - 1), more)

            for c, src in straight.items():
                if c < C_FFN:
                    fetch(c, sizes[c], src)

            def cols(w):
                v = w.rearrange("(j k p) n -> j p k n", j=2, p=P)
                return lambda j, f: v[j, :, :, bass.ds(f * FC, FC)]

            down_v = w_down0.rearrange("(f j k p) n -> f j p k n", j=2, k=2, p=P)
            swiglu_chunks(C_FFN, cols(w_gate0), cols(w_up0),
                          lambda j, f: down_v[bass.ds(f, 1), j].rearrange("a p k n -> (a p) k n"))
            for c, src in straight.items():
                if c >= C_IN1:
                    fetch(c, sizes[c], src)

            def expert_cols(w, e):
                v = w.rearrange("e (j k p) n -> j e p k n", j=2, p=P)
                return lambda j, f: v[j, bass.ds(e, 1), :, :, bass.ds(f * FC, FC)].rearrange("a p k n -> (a p) k n")

            def expert(e, more, c0=C_MOE):
                v = we_down1.rearrange("e (f j k p) n -> j e f p k n", j=2, k=2, p=P)
                swiglu_chunks(c0, expert_cols(we_gate1, e), expert_cols(we_up1, e),
                              lambda j, f: v[j, bass.ds(e, 1), bass.ds(f, 1)].rearrange("a b p k n -> (a b p) k n"),
                              more)

            with sp.Fori(0, NE) as u:
                expert(u, FFN_CHUNKS * u)
            sp.wait_ge(sem("units_known"), 1)
            for j in range(NU_MAX):
                n_over = sp.value_load(unit_i[0:1, 3:4], min_val=0, max_val=NU_MAX)
                e = sp.value_load(unit_i[0:1, j:j + 1], min_val=0, max_val=NE - 1)
                with sp.If(n_over > j):
                    expert(e, FFN_CHUNKS * (NE + j))
            sp.wait_ge(sem("h_final"), 1)
            sp.dma_start(out.rearrange("o (b p) d -> p (o b) d", p=P), h[:, :, :]).then_inc(sem("stored"), 16)
            sp.wait_ge(sem("stored"), 16)

        @block.gpsimd
        def _(pool):
            n = 0

            def step(ins):
                nonlocal n
                n += 1
                ins.then_inc(sem("pool_step"), 1)

            def fill(t, value, pattern, base, cm, op, other):
                step(pool.memset(t, value))
                pool.wait_ge(sem("pool_step"), n)
                step(pool.affine_select(out=t, in_=t, compare_op=op, fill=other, base=base,
                                        pattern=pattern, channel_multiplier=cm))

            step(pool.memset(gain_rows[:, :], 0.0))
            step(pool.memset(ones[:, :], 1.0))
            fill(ident[:, :], 0.0, [[-1, P]], 0, 1, ALU.not_equal, 1.0)
            pool.wait_ge(sem("pool_step"), n)
            pool.iota(iota[:, :], [[1, P]], base=0, channel_multiplier=0,
                      allow_small_or_imprecise_dtypes=True).then_inc(sem("ident_ready"), 1)
            fill(upto[:, :, :], 1.0, [[0, 2], [1, P]], 0, -1, ALU.is_ge, 0.0)
            fill(before[:, :], 1.0, [[1, P]], -1, -1, ALU.is_ge, 0.0)
            step(pool.memset(negmask[:, :, :], 0.0))
            pool.wait_ge(sem("pool_step"), n)
            step(pool.affine_select(out=negmask[:, 0:3:2, :], in_=negmask[:, 0:3:2, :], compare_op=ALU.is_ge,
                                    fill=NEG, base=0, pattern=[[0, 2], [-1, P]], channel_multiplier=1))
            fill(earlier[:, :, :], 1.0, [[1, NE], [-1, NE]], -1, 0, ALU.is_ge, 0.0)
            fill(headsel[:, :, :], 0.0, [[-1, LH], [0, P]], 0, 1, ALU.not_equal, 1.0)
            step(pool.memset(vA[:, :, :, LD:LD + 2], 1.0))
            step(pool.memset(qk_in[:, :, :, 0:TAPS - 1], 0.0))
            for j in range(HALF):
                freq = float(ROPE_THETA ** (-j / HALF))
                step(pool.memset(angle[:, 0, :, j:j + 1], freq))
            pool.wait_ge(sem("pool_step"), n)
            pool.memset(small[:, 0:2], 0.0).then_inc(sem("consts_ready"), 1)

        @block.tensor
        def _(pe):
            def mm(o, a, b, start, stop, **kw):
                return pe.matmul(o, a, b, start=start, stop=stop, skip_group_check=True, **kw)

            def part_end(i):
                pe.drain().then_inc(part_done, 1)
                pe.wait_ge(part_done, N_PARTS * (i + 1))

            def transpose_rows(src, nk, first_block, bank0=0):
                for k in range(0, nk, 2):
                    for kk in (k, k + 1):
                        for t in range(TB):
                            last = pe.transpose(B[bank0 + k // 2][:, (kk - k) * S + t * P:(kk - k) * S + (t + 1) * P],
                                                src(t, kk), ident[:, :])
                    last.then_inc(sem("xT_psum"), 1)

            tiles = [0]

            def proj(parts, n, need_xT):
                t = tiles[0]
                tiles[0] += 1
                bank = [B[4 + 2 * (t % 2)], B[5 + 2 * (t % 2)]]
                if t >= 2:
                    pe.wait_ge(sem("tile_evacuated"), t - 1)
                if need_xT:
                    pe.wait_ge(sem("xT_ready"), need_xT)
                seen, total = 0, sum(len(ks) for _, _, ks in parts)
                for c, shape, ks in parts:
                    for half, (k0, nk) in enumerate(pieces_of(shape)):
                        pe.wait_ge(lo_ready, 2 * c + half + 1)
                        w = [split_piece(x, c, shape, half) for x in wS]
                        for i, k in enumerate(ks[k0:k0 + nk]):
                            for tb in range(TB):
                                for a, b in TERMS:
                                    last = mm(bank[tb][:, 0:n], xT[a][:, k, tb * P:(tb + 1) * P], w[b][:, i, :],
                                              start=(seen == 0 and (a, b) == (0, 0)),
                                              stop=(seen == total - 1 and (a, b) == TERMS[-1]))
                            seen += 1
                        last.then_inc(piece_used, 1)

            def proj_one_k(c, k):
                t = tiles[0]
                tiles[0] += 1
                pe.wait_ge(sem("tile_evacuated"), t - 1)
                for half in range(2):
                    pe.wait_ge(lo_ready, 2 * c + half + 1)
                    w = [split_piece(x, c, (2, 256), half) for x in wS]
                    for tb in range(TB):
                        for a, b in TERMS:
                            last = mm(B[4 + 2 * (t % 2) + tb][:, half * 256:(half + 1) * 256],
                                      xT[a][:, k, tb * P:(tb + 1) * P], w[b][:, 0, :], (a, b) == (0, 0), (a, b) == TERMS[-1])
                    last.then_inc(piece_used, 1)

            def full(c, n):
                return [(c, (KD // 2, n), range(0, 4)), (c + 1, (KD // 2, n), range(4, 8))]

            pe.wait_ge(sem("ident_ready"), 1)
            pe.wait_ge(sem("rows_here"), 16 * N_ROW_DMAS)
            pe.transpose(B[0][:, 0:P], gain_rows[:, :], ident[:, :])
            pe.transpose(B[1][0:HB, 0:TAPS * QKB], conv_rows[:, :], ident[0:TAPS * QKB, 0:TAPS * QKB]).then_inc(
                sem("gains_psum"), 1)
            pe.wait_ge(sem("gains_ready"), 2)

            pe.wait_ge(sem("rows_normed"), 2)
            transpose_rows(lambda t, k: xr[:, t, k * P:(k + 1) * P], KD, 0)
            proj(full(C_MEM, 512), 512, 4)
            pe.wait_ge(sem("km_normed"), 1)
            for pair in range(2):
                for t in range(TB):
                    last = pe.transpose(B[0][:, pair * S + t * P:pair * S + (t + 1) * P],
                                        km[:, t, pair * P:(pair + 1) * P], ident[:, :])
            last.then_inc(sem("kmT_psum"), 1)
            part_end(0)

            pe.wait_ge(sem("rows_normed"), 4)
            transpose_rows(lambda t, k: xr[:, t, k * P:(k + 1) * P], KD, 4)
            pe.wait_ge(sem("xT_ready"), 8)
            for t in range(4):
                if t >= 2:
                    pe.wait_ge(sem("qk_copied"), t - 1)
                for j in range(2):
                    c = C_QK + 2 * t + j
                    for half in range(2):
                        pe.wait_ge(lo_ready, 2 * c + half + 1)
                        w = [split_piece(x, c, (4, 384), half) for x in wS]
                        for q in range(4):
                            dst = B[2 * (t % 2) + q // 2][0:HB, (q % 2) * S:(q % 2 + 1) * S]
                            for i in range(2):
                                k = 4 * j + 2 * half + i
                                for a, b in TERMS:
                                    last = mm(dst, w[a][:, i, q * HB:(q + 1) * HB], xT[b][:, k, :],
                                              start=(k == 0 and q % 2 == 0 and (a, b) == (0, 0)),
                                              stop=(k == KD - 1 and (a, b) == TERMS[-1]))
                        last.then_inc(piece_used, 1)
            for t in range(4):
                proj(full(C_V + 2 * t, 384), 384, 0)
            proj(full(C_GM, 264), 264, 0)
            pe.wait_ge(sem("tile_evacuated"), 6)
            for g in range(2):
                for t in range(TB):
                    last = pe.transpose(B[0][0:LH, g * S + t * P:g * S + (t + 1) * P],
                                        gm[:, t, g * LH:(g + 1) * LH], ident[:, :])
            last.then_inc(sem("gates_psum"), 1)
            for pair in range(2):
                for t in range(TB):
                    last = pe.transpose(B[1][:, pair * S + t * P:pair * S + (t + 1) * P],
                                        gm[:, t, 2 * LH + pair * P:2 * LH + (pair + 1) * P], ident[:, :])
            last.then_inc(sem("qmT_psum"), 1)
            pe.wait_ge(sem("gate_rows_ready"), 1)
            for g, row in enumerate((3, 5)):
                for t in range(TB):
                    last = pe.transpose(B[0][:, (g * TB + t) * LH:(g * TB + t + 1) * LH],
                                        gr[:, row, t * P:(t + 1) * P], ident[0:LH, 0:LH])
            last.then_inc(sem("gate_cols_psum"), 1)
            for hd in range(LH):
                last = mm(B[2 + hd // 2][:, (hd % 2) * S:(hd % 2 + 1) * S], headsel[:, hd, :], gr[:, 4, :], True, True)
            last.then_inc(sem("peak_psum"), 1)
            part_end(1)

            for hd in range(LH):
                bank = B[4 + hd]
                for sbk in range(TB):
                    cols = slice(0, S) if sbk == 0 else slice(S, S + P)
                    for i in range(2):
                        last = mm(bank[:, cols], qkT[:, QKB // 2 + 2 * hd + i, sbk * P:(sbk + 1) * P],
                                  qkT[:, 2 * hd + i, sbk * P:S], i == 0, i == 1)
                last.then_inc(sem("mscores_psum"), 1)
            for hd in range(LH):
                pe.wait_ge(sem("mweights_ready"), hd + 1)
                bank = B[hd]
                mm(bank[:, 0:LD + 1], decay[:, hd, 0:P], vA[:, 0, hd, 0:LD + 1], True, True)
                mm(bank[:, S:S + LD + 1], decay[:, hd, P:S], vA[:, 0, hd, 0:LD + 1], True, False)
                mm(bank[:, S:S + LD + 1], decay[:, hd, S:S + P], vA[:, 1, hd, 0:LD + 1], False, True).then_inc(
                    sem("mnum_psum"), 1)
            part_end(2)

            def memory_attention(layer, qmT, kmTs, pm, pmT):
                pe.wait_ge(sem("mem_ops_ready"), 2 * (layer + 1))
                for t in range(TB):
                    for hd in range(MH):
                        r = slice(MD * (hd % 2), MD * (hd % 2) + MD)
                        last = mm(B[4 + 2 * t + hd % 2][:, (hd // 2) * S:(hd // 2 + 1) * S],
                                  qmT[r, hd // 2, t * P:(t + 1) * P], kmTs[r, hd // 2, :], True, True)
                last.then_inc(sem("mem_scores"), 1)
                for hd in range(MH):
                    pe.wait_ge(sem("mem_probs"), MH * layer + hd + 1)
                    for t in range(TB):
                        for mb in range(2):
                            last = pe.transpose(B[hd][:, (t * 2 + mb) * P:(t * 2 + mb + 1) * P],
                                                pm(t, hd)[:, mb * P:(mb + 1) * P], ident[:, :])
                    last.then_inc(sem("mem_pT_psum"), 1)
                for hd in range(MH):
                    pe.wait_ge(sem("mem_pT"), MH * layer + hd + 1)
                    for t in range(TB):
                        for mb in range(2):
                            last = mm(B[4][:, (t * MH + hd) * MD:(t * MH + hd + 1) * MD],
                                      pmT(hd)[:, (t * 2 + mb) * P:(t * 2 + mb + 1) * P],
                                      vm[:, mb, hd * MD:(hd + 1) * MD], mb == 0, mb == 1)
                last.then_inc(sem("mem_out_psum"), 1)

            memory_attention(0, qmT, kmTs_0, pm_0, pmT_0)
            part_end(3)
            transpose_rows(lambda t, k: y[:, t, k * P:(k + 1) * P], KD, 8)
            for t in range(2):
                proj(full(C_OUT0 + 2 * t, 512), 512, 12)
            part_end(4)

            pe.wait_ge(sem("rows_normed"), 6)
            transpose_rows(lambda t, k: xr[:, t, k * P:(k + 1) * P], KD, 12)
            pe.wait_ge(sem("xT_ready"), 16)

            def ffn_in(c, which, more):
                for j in range(4):
                    pe.wait_ge(lo_ready, 2 * c + j + 1 + 2 * more)
                    w = [split_piece(x, c + j // 2, UP, j % 2) for x in wS]
                    for q in range(FB):
                        dst = B[2 * which + q // 2][:, (q % 2) * S:(q % 2 + 1) * S]
                        for i in range(2):
                            k = 2 * j + i
                            for a, b in TERMS:
                                last = mm(dst, w[a][:, i, q * P:(q + 1) * P], xT[b][:, k, :],
                                          start=(k == 0 and q % 2 == 0 and (a, b) == (0, 0)),
                                          stop=(k == KD - 1 and (a, b) == TERMS[-1]))
                    last.then_inc(piece_used, 1)

            def ffn_down(c, more, start, stop):
                for j in range(4):
                    pe.wait_ge(lo_ready, 2 * c + j + 1 + 2 * more)
                    w = [split_piece(x, c + j // 2, DOWN, j % 2) for x in wS]
                    for t in range(TB):
                        for half in range(2):
                            for a, b in TERMS:
                                last = mm(B[4 + 2 * t + half][:, :], aT[a][:, j, t * P:(t + 1) * P],
                                          w[b][:, 0, half * 512:(half + 1) * 512],
                                          start=(start and j == 0 and (a, b) == (0, 0)),
                                          stop=(stop and j == 3 and (a, b) == TERMS[-1]))
                    last.then_inc(piece_used, 1)

            ffn_in(C_FFN, 0, 0)
            ffn_in(C_FFN + 2, 1, 0)

            def ffn_step(i, n, start):
                c, more = C_FFN + 4, 6 * i
                pe.wait_ge(sem("silu_done"), n + 1)
                ffn_in(c, 0, more)
                pe.wait_ge(sem("act_done"), n + 1)
                ffn_in(c + 2, 1, more)
                pe.wait_ge(sem("aT_ready"), n + 1)
                ffn_down(c + 4, more, start, False)

            ffn_step(0, 0, True)
            with pe.Fori(1, NF - 1) as i:
                ffn_step(i, i, False)
            pe.wait_ge(sem("aT_ready"), NF)
            ffn_down(C_FFN + 40, 0, False, True)
            part_end(5)

            pe.wait_ge(sem("rows_normed"), 8)
            transpose_rows(lambda t, k: xr[:, t, k * P:(k + 1) * P], KD, 16)
            proj(full(C_IN1, 512), 512, 20)
            proj(full(C_IN1 + 2, 320), 320, 0)
            pe.wait_ge(sem("lora_normed"), 1)
            transpose_rows(lambda t, k: c1[:, t, k * P:(k + 1) * P], 4, 20)
            for t in range(3):
                proj([(C_UQ + t, (3, 384), range(3))], 384, 22)
            for t in range(3):
                proj_one_k(C_UKV + t, 3)
            part_end(6)

            pe.wait_ge(sem("q_ready"), 1)
            for b in range(3):
                for hd in (2 * b, 2 * b + 1):
                    for t in range(TB):
                        last = pe.transpose(B[b][:, (hd % 2) * S + t * P:(hd % 2) * S + (t + 1) * P],
                                            qS[:, t, hd, 0:NOPE], ident[:, :])
                last.then_inc(sem("headsT_psum"), 1)

            def pairs_turned(src, b0):
                for j in range(3):
                    for t in range(TB):
                        last = pe.transpose(B[b0 + j // 2][:, (j % 2) * S + t * P:(j % 2) * S + (t + 1) * P],
                                            src[:, t, 2 * j:2 * j + 2, :].rearrange("p h d -> p (h d)"), ident[:, :])
                    if j:
                        last.then_inc(sem("headsT_psum"), 1)

            pairs_turned(rotq, 3)
            pe.wait_ge(sem("k_ready"), 1)
            for b in range(3):
                for hd in (2 * b, 2 * b + 1):
                    for t in range(TB):
                        last = pe.transpose(B[5 + b][:, (hd % 2) * S + t * P:(hd % 2) * S + (t + 1) * P],
                                            kS[:, t, hd, :], ident[:, :])
                last.then_inc(sem("headsT_psum"), 1)
            pe.wait_ge(sem("headsT_ready"), 2)
            pairs_turned(rotk, 0)
            pe.wait_ge(sem("headsT_ready"), 10)
            for hd in range(AH):
                r = slice(ROPE * (hd % 2), ROPE * (hd % 2) + ROPE)
                for t in range(TB):
                    dst = B[hd][:, 0:P] if t == 0 else B[hd][:, P:P + S]
                    q, k = slice(t * P, (t + 1) * P), slice(0, (t + 1) * P)
                    mm(dst, qT[:, hd, q], kT[:, hd, k], True, False)
                    last = mm(dst, qrT[r, hd // 2, q], krT[r, hd // 2, k], False, True)
                last.then_inc(sem("scores_psum"), 1)
            for hd in range(AH):
                pe.wait_ge(sem("probs_ready"), hd + 1)
                for i in range(3):
                    last = pe.transpose(B[(6 + hd) % 8][:, i * P:(i + 1) * P], scr[:, hd, i * P:(i + 1) * P], ident[:, :])
                last.then_inc(sem("pT_psum"), 1)
            pe.wait_ge(sem("pT_ready"), AH)
            for t in range(TB):
                for hd in range(AH):
                    bank, col = (B[4 + t], hd * VD) if hd < 4 else (B[6], (t * 2 + hd - 4) * VD)
                    if t == 0:
                        last = mm(bank[:, col:col + VD], pT[:, hd, 0:P], vS[:, 0, hd, :], True, True)
                    else:
                        mm(bank[:, col:col + VD], pT[:, hd, P:S], vS[:, 0, hd, :], True, False)
                        last = mm(bank[:, col:col + VD], pT[:, hd, S:S + P], vS[:, 1, hd, :], False, True)
            last.then_inc(sem("heads_psum"), 1)
            for pair in range(2):
                for t in range(TB):
                    last = pe.transpose(B[7][:, pair * S + t * P:pair * S + (t + 1) * P],
                                        c2[:, t, ROPE + pair * P:ROPE + (pair + 1) * P], ident[:, :])
            last.then_inc(sem("qmT_psum"), 1)
            part_end(7)
            memory_attention(1, qmT, kmTs_1, pm_1, pmT_1)
            part_end(8)
            transpose_rows(lambda t, k: y[:, t, k * P:(k + 1) * P], KD, 22)
            for t in range(2):
                proj(full(C_OUT1 + 2 * t, 512), 512, 26)
            part_end(9)

            pe.wait_ge(sem("rows_normed"), 10)
            transpose_rows(lambda t, k: xr[:, t, k * P:(k + 1) * P], KD, 26)
            pe.wait_ge(sem("xT_ready"), 30)
            wr = (wr_hi, wr_lo)
            for t in range(TB):
                for k in range(KD):
                    for a, b in TERMS:
                        last = mm(B[4][:, t * NE:(t + 1) * NE], xT[a][:, k, t * P:(t + 1) * P], wr[b][:, k, :],
                                  k == 0 and (a, b) == (0, 0), k == KD - 1 and (a, b) == TERMS[-1])
            last.then_inc(sem("logits_psum"), 1)
            pe.wait_ge(sem("routed"), 1)
            mask = rt[:, 5]
            mm(B[5][:, 0:NE], before[:, :], mask[:, 0, :], True, True)
            mm(B[5][:, NE:2 * NE], ones[:, :], mask[:, 0, :], True, False)
            mm(B[5][:, NE:2 * NE], before[:, :], mask[:, 1, :], False, True)
            mm(B[5][:, 2 * NE:3 * NE], ones[:, :], mask[:, 0, :], True, False)
            mm(B[5][:, 2 * NE:3 * NE], ones[:, :], mask[:, 1, :], False, True).then_inc(sem("slots_psum"), 1)
            part_end(10)

            def gather(u):
                pe.wait_ge(sem("onehot_ready"), u + 1)
                for k in range(KD):
                    n = 0
                    for rows_x in (xr_hi, xr_lo):
                        for t in range(TB):
                            last = mm(B[k // 4][:, (k % 4) * P:(k % 4 + 1) * P], rows_x[:, t, k * P:(k + 1) * P],
                                      onehot[:, t, :], n == 0, n == 3)
                            n += 1
                    if k % 4 == 3:
                        last.then_inc(sem("gather_psum"), 1)

            def turn(u):
                for t in range(TB):
                    mm(B[3][:, S:S + 1], F(onehot[:, t, :]), cur[:, 2, t:t + 1], t == 0, t == TB - 1)
                for t in range(TB):
                    last = pe.transpose(B[3][:, t * P:(t + 1) * P], F(onehot[:, t, :]), ident[:, :])
                last.then_inc(sem("turn_psum"), 1)

            def e_in(c, which, more):
                for j in range(4):
                    pe.wait_ge(lo_ready, 2 * c + j + 1 + 2 * more)
                    w = [split_piece(x, c + j // 2, UP, j % 2) for x in wS]
                    for i in range(2):
                        k = 2 * j + i
                        for a, b in TERMS:
                            last = mm(B[which][:, :], xT[a][:, k, 0:P], w[b][:, i, :],
                                      start=(k == 0 and (a, b) == (0, 0)), stop=(k == KD - 1 and (a, b) == TERMS[-1]))
                    last.then_inc(piece_used, 1)

            def e_turn(n):
                pe.wait_ge(sem("eact_done"), n + 1)
                for q in range(FB):
                    last = pe.transpose(B[2][:, q * P:(q + 1) * P], act_f[:, q * P:(q + 1) * P], ident[:, :])
                last.then_inc(sem("eaT_psum"), 1)

            def e_down(c, more, n, start, stop):
                pe.wait_ge(sem("eaT_ready"), n + 1)
                for j in range(4):
                    pe.wait_ge(lo_ready, 2 * c + j + 1 + 2 * more)
                    w = [split_piece(x, c + j // 2, DOWN, j % 2) for x in wS]
                    for half in range(2):
                        for a, b in TERMS:
                            last = mm(B[4 + half][:, :], aT[a][:, j, 0:P], w[b][:, 0, half * 512:(half + 1) * 512],
                                      start=(start and j == 0 and (a, b) == (0, 0)),
                                      stop=(stop and j == 3 and (a, b) == TERMS[-1]))
                    last.then_inc(piece_used, 1)

            def back(u):
                pe.wait_ge(sem("ys_ready"), 2 * u + 2)
                for t in range(TB):
                    for half in range(2):
                        if t:
                            pe.wait_ge(sem("h_added"), 4 * u + half + 1)
                        for n, ys in enumerate((ys_hi, ys_lo)):
                            last = mm(B[6 + half][:, :], onehotT[:, t * P:(t + 1) * P],
                                      ys[:, half * 512:(half + 1) * 512], n == 0, n == 1)
                        last.then_inc(sem("back_psum"), 1)

            def start_unit(u):
                gather(u)
                pe.wait_ge(sem("gather_ready"), 2 * u + 2)
                e_in(C_MOE, 0, FFN_CHUNKS * u)

            def unit(u, last=False):
                more, n0 = FFN_CHUNKS * u, NF * u
                e_in(C_MOE + 2, 1, more)

                def e_step(i, start):
                    c, m = C_MOE + 4, more + 6 * i
                    pe.wait_ge(sem("esilu_done"), n0 + i + 1)
                    e_in(c, 0, m)
                    e_turn(n0 + i)
                    e_in(c + 2, 1, m)
                    e_down(c + 4, m, n0 + i, start, False)

                e_step(0, True)
                with pe.Fori(1, NF - 1) as i:
                    e_step(i, False)
                e_turn(n0 + NF - 1)
                if not last:
                    gather(u + 1)
                e_down(C_MOE + 40, more, n0 + NF - 1, False, True)
                if not last:
                    pe.wait_ge(sem("gather_ready"), 2 * u + 4)
                    e_in(C_MOE + FFN_CHUNKS, 0, more)
                back(u)
                if not last:
                    turn(u + 1)

            start_unit(0)
            turn(0)
            with pe.Fori(0, NE - 1) as u:
                unit(u)
            unit(NE - 1, last=True)
            pe.wait_ge(sem("units_known"), 1)
            for j in range(NU_MAX):
                n_over = pe.value_load(unit_i[0:1, 3:4], min_val=0, max_val=NU_MAX)
                with pe.If(n_over > j):
                    start_unit(NE + j)
                    turn(NE + j)
                    unit(NE + j, last=True)

        @block.scalar
        def _(act):
            n_dma = 0
            act.wait_ge(sem("pool_step"), 1)
            for name, (a, vec) in rows.items():
                nk = vec.shape[0] // P
                act.dma_start(gain_rows[a:a + nk, :], vec.rearrange("(k p) -> k p", p=P)).then_inc(sem("rows_here"), 16)
                n_dma += 1
            for g, vec in ((G_QN, q_norm1), (G_KN, k_norm1)):
                act.dma_start(gain_rows[g:g + 1, :], vec.rearrange("(o n) -> o n", o=1)[:, 0:NOPE]).then_inc(
                    sem("rows_here"), 16)
                n_dma += 1
            for g, vec in ((G_MQ[0], mq_norm0), (G_MQ[1], mq_norm1), (G_MK[0], mk_norm0), (G_MK[1], mk_norm1)):
                for r in range(2):
                    act.dma_start(gain_rows[g:g + 1, r * MD:(r + 1) * MD], vec.rearrange("(o n) -> o n", o=1)).then_inc(
                        sem("rows_here"), 16)
                    n_dma += 1
            act.dma_start(conv_rows[:, :], conv_w0.rearrange("t (b p) -> (t b) p", p=HB)).then_inc(sem("rows_here"), 16)
            n_dma += 1
            assert n_dma == N_ROW_DMAS
            act.dma_start(hnorm_bc[:, :], h_norm0.partition_broadcast(P)).then_inc(
                sem("bc_here"), 16)
            act.dma_start(qrope_bc[:, :], q_norm1[NOPE:QKD].partition_broadcast(P)).then_inc(
                sem("bc_here"), 16)
            act.dma_start(krope_bc[:, :], k_norm1[NOPE:QKD].partition_broadcast(P)).then_inc(
                sem("bc_here"), 16)
            act.dma_start(gate_bias[:, 0:1], b_i0.rearrange("(n o) -> n o", o=1)).then_inc(sem("bc_here"), 16)
            act.dma_start(gate_bias[:, 1:2], b_f0.rearrange("(n o) -> n o", o=1)).then_inc(sem("bc_here"), 16)
            act.dma_start(pos_i[:, :], positions.rearrange("o (b p) -> p (o b)", p=P),
                          allow_slow_non_contiguous=True).then_inc(sem("bc_here"), 16)
            act.dma_start(w_router[:, :, :], w_router1.rearrange("(k p) e -> p k e", p=P)).then_inc(sem("bc_here"), 16)

            steps = [0]

            def step(ins):
                steps[0] += 1
                ins.then_inc(sem("act_step"), 1)

            def settle():
                act.wait_ge(sem("act_step"), steps[0])

            def part_end(i):
                act.drain().then_inc(part_done, 1)
                act.wait_ge(part_done, N_PARTS * (i + 1))

            done = [0]

            def split_high(p, shape, more=0, lap=0):
                c, half = p // 2, p % 2
                if half == 0:
                    act.wait_ge(raw_here[c % RAW_SLOTS], 16 * (c // RAW_SLOTS + 1) + 16 * lap)
                if p >= SPLIT_SLOTS:
                    act.wait_ge(piece_used, p - SPLIT_SLOTS + 1 + 2 * more)
                act.activation(split_piece(w_hi, c, shape, half), raw_piece(c, shape, half), ACT.Copy).then_inc(hi_ready, 1)

            def splits_to(p):
                while done[0] <= p:
                    split_high(done[0], shape_of(done[0] // 2))
                    done[0] += 1

            def norm_rows(src, i):
                for t in range(TB):
                    junk = flat3(og[:, :, :])[:, 0:D] if i == 0 else xr[:, t, :]
                    if i == 0 and t:
                        settle()
                    ins = act.activation(junk, src[:, t, :], ACT.Square, accum_out=stat[:, 0, t:t + 1])
                    if i == 0 and t == 0:
                        step(ins)
                ins.then_inc(sem("sumsq_ready"), 1)

            def high_T(nk, base, gain, lookahead=None, bank0=0):
                for b in range(nk // 2):
                    act.wait_ge(sem("xT_psum"), base + b + 1)
                    for kk in range(2):
                        k = 2 * b + kk
                        ins = act.activation(xT_hi[:, k, :], B[bank0 + b][:, kk * S:(kk + 1) * S], ACT.Copy,
                                             scale=1.0 if gain is None else gains[:, gain + k:gain + k + 1])
                    ins.then_inc(sem("xT_hi_ready"), 1)

            act.wait_ge(sem("mem_here"), 16)
            norm_rows(xr, 0)
            act.wait_ge(sem("gains_psum"), 1)
            act.activation(gains[:, :], B[0][:, 0:P], ACT.Copy).then_inc(sem("gains_ready"), 1)
            act.activation(convw[:, :], B[1][0:HB, 0:TAPS * QKB], ACT.Copy).then_inc(sem("gains_ready"), 1)
            splits_to(2 * (C_MEM + 2) + 1)
            act.wait_ge(sem("gains_ready"), 2)
            high_T(KD, 0, G["mem"])
            act.wait_ge(piece_used, 2 * (C_MEM + 2))
            for t in range(TB):
                act.activation(vm[:, t, :], B[4 + t][:, MEMW:2 * MEMW], ACT.Copy).then_inc(sem("vm_copied"), 1)
            act.wait_ge(sem("kmT_psum"), 1)
            act.activation(kmT[:, :, :].rearrange("p a s -> p (a s)"), B[0][:, :], ACT.Copy).then_inc(sem("kmT_ready"), 1)
            part_end(0)

            act.wait_ge(sem("x_here"), 32)
            norm_rows(h, 1)
            splits_to(2 * (C_QK + 1) + 1)
            high_T(KD, 4, G["mix0"])
            for t in range(4):
                splits_to(2 * (C_QK + 2 * t + 3) + 1)
                act.wait_ge(piece_used, 2 * (C_QK + 2 * t + 2))
                if t >= 2:
                    act.wait_ge(sem("conv_done"), t - 1)
                for b in range(2):
                    ins = act.activation(qk_in[:, t % 2, 2 * b:2 * b + 2, TAPS - 1:],
                                         B[2 * (t % 2) + b][0:HB, :].rearrange("p (q s) -> p q s", q=2), ACT.Copy)
                ins.then_inc(sem("qk_copied"), 1)
            for t in range(2):
                splits_to(2 * (C_V + 2 * t + 3) + 1)
                act.wait_ge(piece_used, 2 * (C_V + 2 * t + 2))
                for tb in range(TB):
                    ins = act.activation(vA[:, tb, 2 * t:2 * t + 2, 0:LD],
                                         B[4 + 2 * ((t + 1) % 2) + tb][:, 0:384].rearrange("p (h d) -> p h d", h=2), ACT.Copy)
                ins.then_inc(sem("tile_evacuated"), 1)
            for t in range(2):
                splits_to(2 * (C_V + 4 + 2 * t + 3) + 1)
                act.wait_ge(piece_used, 2 * (C_V + 4 + 2 * t + 2))
                for tb in range(TB):
                    ins = act.activation(og[:, tb, 384 * t:384 * t + 384], B[4 + 2 * ((t + 1) % 2) + tb][:, 0:384], ACT.Sigmoid)
                ins.then_inc(sem("tile_evacuated"), 1)
            splits_to(2 * (C_OUT0 + 1) + 1)
            act.wait_ge(piece_used, 2 * (C_GM + 2))
            for tb in range(TB):
                ins = act.activation(gm[:, tb, :], B[6 + tb][:, 0:264], ACT.Copy)
            ins.then_inc(sem("tile_evacuated"), 1)
            for q in range(4):
                act.wait_ge(sem("conv_done"), q + 1)
                act.activation(qkT[:, 4 * q:4 * q + 4, :], qkT[:, 4 * q:4 * q + 4, :], ACT.Silu).then_inc(sem("qk_silu"), 1)
            act.wait_ge(sem("angles_ready"), 1)
            act.activation(sin[:, :, :], angle[:, 2, :, :], ACT.Sin).then_inc(sem("rope_ready"), 1)
            act.activation(cos[:, :, :], angle[:, 3, :, :], ACT.Sin).then_inc(sem("rope_ready"), 1)
            act.wait_ge(sem("gate_abs"), 1)
            step(act.activation(gr[:, 1, :], gr[:, 1, :], ACT.Exp, scale=-1.0))
            settle()
            act.activation(gr[:, 1, :], gr[:, 1, :], ACT.Ln, bias=1.0).then_inc(sem("gate_ln"), 1)
            act.wait_ge(sem("gate_m"), 1)
            act.activation(gr[:, 5, :], gr[:, 5, :], ACT.Exp, scale=-1.0).then_inc(sem("gate_rows_ready"), 1)
            part_end(1)

            for hd in range(LH):
                act.wait_ge(sem("decay_exp"), hd + 1)
                act.activation(decay[:, hd, :], decay[:, hd, :], ACT.Exp, scale=-1.0).then_inc(sem("decay_ready"), 1)
            for hd in range(LH):
                act.wait_ge(sem("mnum_psum"), hd + 1)
                act.activation(num[:, :, hd, 0:LD + 1],
                               B[hd][:, :].rearrange("p (t n) -> p t n", t=TB)[:, :, 0:LD + 1], ACT.Copy).then_inc(
                    sem("num_copied"), 1)
            part_end(2)

            def memory_attention(layer, pm, pmT):
                act.wait_ge(sem("mem_bias"), layer + 1)
                for hd in range(MH):
                    for t in range(TB):
                        c = t * MH + hd
                        ins = act.activation(pm(t, hd), B[4 + 2 * t + hd % 2][:, (hd // 2) * S:(hd // 2 + 1) * S], ACT.Exp,
                                             bias=small[:, 8 + c:9 + c], scale=small[:, c:c + 1],
                                             accum_out=small[:, 16 + c:17 + c])
                    ins.then_inc(sem("mem_probs"), 1)
                for hd in range(MH):
                    act.wait_ge(sem("mem_pT_psum"), MH * layer + hd + 1)
                    act.activation(pmT(hd), B[hd][:, :], ACT.Copy).then_inc(sem("mem_pT"), 1)

            memory_attention(0, pm_0, pmT_0)
            part_end(3)
            high_T(KD, 8, None)
            for t in range(2):
                splits_to(2 * (C_OUT0 + 2 * t + 3 if t == 0 else C_FFN + 1) + 1)
            part_end(4)

            norm_rows(h, 2)
            high_T(KD, 12, G["ffn0"])

            def silu_gate(c, more, n):
                act.wait_ge(piece_used, 2 * (c + more))
                if not isinstance(n, int) or n > 0:
                    act.wait_ge(sem("act_done"), n)
                for b in range(2):
                    ins = act.activation(silu_g[:, b * 512:(b + 1) * 512], B[b][:, :], ACT.Silu)
                ins.then_inc(sem("silu_done"), 1)

            def high_act(c, more, n):
                act.wait_ge(sem("act_done"), n + 1)
                act.wait_ge(piece_used, 2 * (c + more))
                act.activation(aT_hi[:, :, :].rearrange("p q s -> p (q s)"), act_f[:, :], ACT.Copy).then_inc(
                    sem("aT_hi_ready"), 1)

            def ffn_body(i, next_shape):
                c, more = C_FFN + 4, 6 * i

                def pieces(a, b):
                    for j in range(a, b):
                        split_high(2 * c + j, DOWN if 8 <= j < 12 else UP if j < 8 else next_shape, more, i)

                pieces(4, 6)
                high_act(c, more, i)
                pieces(6, 9)
                silu_gate(c + 2, more, i + 1)
                pieces(9, 16)

            p0 = 2 * C_FFN
            for j in (4, 5):
                split_high(p0 + j, UP)
            silu_gate(C_FFN + 2, 0, 0)
            for j in range(6, 12):
                split_high(p0 + j, UP)
            with act.Fori(0, NF - 2) as i:
                ffn_body(i, UP)
            ffn_body(NF - 2, DOWN)
            high_act(C_FFN + 40, 0, NF - 1)
            done[0] = 2 * C_IN1
            splits_to(2 * (C_IN1 + 1) + 1)
            part_end(5)

            norm_rows(h, 3)
            high_T(KD, 16, G["mix1"])
            splits_to(2 * (C_IN1 + 3) + 1)
            act.wait_ge(piece_used, 2 * (C_IN1 + 2))
            for tb in range(TB):
                ins = act.activation(c1[:, tb, :], B[4 + 2 * (TILE_IN1 % 2) + tb][:, :], ACT.Copy)
            ins.then_inc(sem("tile_evacuated"), 1)
            splits_to(2 * (C_UQ + 1) + 1)
            act.wait_ge(piece_used, 2 * (C_IN1 + 4))
            for tb in range(TB):
                ins = act.activation(c2[:, tb, :], B[4 + 2 * ((TILE_IN1 + 1) % 2) + tb][:, 0:320], ACT.Copy)
            ins.then_inc(sem("tile_evacuated"), 1)
            high_T(4, 20, G["cq"])
            splits_to(2 * (C_UQ + 2) + 1)
            for t in range(3):
                act.wait_ge(piece_used, 2 * (C_UQ + t + 1))
                for tb in range(TB):
                    ins = act.activation(qS[:, tb, 2 * t:2 * t + 2, :].rearrange("p h d -> p (h d)"),
                                         B[4 + 2 * ((TILE_IN1 + 2 + t) % 2) + tb][:, 0:384], ACT.Copy)
                ins.then_inc(sem("tile_evacuated"), 1)
                splits_to(2 * (C_UQ + 3 + t) + 1)
            for t in range(3):
                act.wait_ge(piece_used, 2 * (C_UKV + t + 1))
                for tb in range(TB):
                    src = B[4 + 2 * ((TILE_IN1 + 5 + t) % 2) + tb][:, :].rearrange("p (h d) -> p h d", h=2)
                    act.activation(kS[:, tb, 2 * t:2 * t + 2, :], src[:, :, 0:NOPE], ACT.Copy)
                    ins = act.activation(vS[:, tb, 2 * t:2 * t + 2, :], src[:, :, NOPE:], ACT.Copy)
                ins.then_inc(sem("tile_evacuated"), 1)
            part_end(6)

            for b in range(3):
                act.wait_ge(sem("headsT_psum"), b + 1)
                act.activation(qT[:, 2 * b:2 * b + 2, :].rearrange("p h s -> p (h s)"), B[b][:, :], ACT.Copy,
                               scale=small[:, 60:61]).then_inc(sem("headsT_ready"), 1)

            def pairs(dst, b0, n):
                act.wait_ge(sem("headsT_psum"), n + 1)
                act.activation(dst[:, 0:2, :].rearrange("p h s -> p (h s)"), B[b0][:, :], ACT.Copy).then_inc(
                    sem("headsT_ready"), 1)
                act.wait_ge(sem("headsT_psum"), n + 2)
                act.activation(dst[:, 2, :], B[b0 + 1][:, 0:S], ACT.Copy).then_inc(sem("headsT_ready"), 1)

            pairs(qrT, 3, 3)
            for b in range(3):
                act.wait_ge(sem("headsT_psum"), 5 + b + 1)
                act.activation(kT[:, 2 * b:2 * b + 2, :].rearrange("p h s -> p (h s)"), B[5 + b][:, :], ACT.Copy).then_inc(
                    sem("headsT_ready"), 1)
            pairs(krT, 0, 8)
            act.wait_ge(sem("score_bias"), 1)
            for hd in range(AH):
                for t in range(TB):
                    c = t * AH + hd
                    part_s = scr[:, hd, 0:P] if t == 0 else scr[:, hd, P:P + S]
                    ins = act.activation(part_s, part_s, ACT.Exp, bias=small[:, 12 + c:13 + c], scale=small[:, c:c + 1],
                                         accum_out=small[:, 24 + c:25 + c])
                ins.then_inc(sem("probs_ready"), 1)
            for hd in range(AH):
                act.wait_ge(sem("pT_psum"), hd + 1)
                act.activation(pT[:, hd, :], B[(6 + hd) % 8][:, 0:384], ACT.Copy).then_inc(sem("pT_ready"), 1)
            part_end(7)
            memory_attention(1, pm_1, pmT_1)
            part_end(8)
            high_T(KD, 22, None)
            splits_to(2 * (C_MOE + 1) + 1)
            part_end(9)

            norm_rows(h, 4)
            high_T(KD, 26, G["ffn1"])
            act.wait_ge(sem("rows_normed"), 10)
            for t in range(TB):
                act.activation(xr_hi[:, t, :], xr[:, t, :], ACT.Copy).then_inc(sem("xr_hi_ready"), 1)
            act.wait_ge(sem("top_diff"), 1)
            act.activation(rt[:, 8, :, 0:1], rt[:, 7, :, 0:1], ACT.Exp).then_inc(sem("top_exp"), 1)
            part_end(10)

            def gathered(u):
                for b in range(2):
                    act.wait_ge(sem("gather_psum"), 2 * u + b + 1)
                    for kk in range(4):
                        k = 4 * b + kk
                        ins = act.activation(xT_hi[:, k, 0:P], B[b][:, kk * P:(kk + 1) * P], ACT.Copy,
                                             scale=gains[:, G["ffn1"] + k:G["ffn1"] + k + 1])
                    ins.then_inc(sem("gather_hi"), 1)

            def e_silu(c, more, n):
                act.wait_ge(piece_used, 2 * (c + more))
                if n is not None:
                    act.wait_ge(sem("eact_done"), n)
                act.activation(silu_g[:, 0:FC], B[0][:, :], ACT.Silu).then_inc(sem("esilu_done"), 1)

            def e_high(n):
                act.wait_ge(sem("eaT_psum"), n + 1)
                act.activation(aT_hi[:, :, 0:P], B[2][:, :].rearrange("p (q s) -> p q s", q=FB), ACT.Copy).then_inc(
                    sem("eaT_hi"), 1)

            def unit(u, last=False):
                more, lap, n0, p0 = FFN_CHUNKS * u, NF * u, NF * u, 2 * C_MOE

                for j in (4, 5):
                    split_high(p0 + j, UP, more, lap)
                e_silu(C_MOE + 2, more, None)
                for j in (6, 7):
                    split_high(p0 + j, UP, more, lap)
                act.wait_ge(sem("turn_psum"), u + 1)
                act.activation(onehotT[:, :], B[3][:, 0:S], ACT.Copy)
                act.activation(gslot[:, :], B[3][:, S:S + 1], ACT.Copy).then_inc(sem("turned"), 1)
                for j in range(8, 12):
                    split_high(p0 + j, UP, more, lap)

                def e_step(i, next_shape):
                    c, m, lp = C_MOE + 4, more + 6 * i, lap + i

                    def pieces(a, b):
                        for j in range(a, b):
                            split_high(2 * c + j, DOWN if 8 <= j < 12 else UP if j < 8 else next_shape, m, lp)

                    pieces(4, 9)
                    e_high(n0 + i)
                    e_silu(c + 2, m, n0 + i + 1)
                    pieces(9, 16)

                with act.Fori(0, NF - 2) as i:
                    e_step(i, UP)
                e_step(NF - 2, DOWN)
                e_high(n0 + NF - 1)
                if not last:
                    for j in (0, 1):
                        split_high(p0 + 2 * FFN_CHUNKS + j, UP, more, lap)
                    gathered(u + 1)
                    for j in (2, 3):
                        split_high(p0 + 2 * FFN_CHUNKS + j, UP, more, lap)
                act.wait_ge(piece_used, 2 * (C_MOE + FFN_CHUNKS + more))
                for half in range(2):
                    act.activation(ys_hi[:, half * 512:(half + 1) * 512], B[4 + half][:, :], ACT.Copy,
                                   scale=gslot[:, 0:1]).then_inc(sem("ys_hi"), 1)

            gathered(0)
            with act.Fori(0, NE - 1) as u:
                unit(u)
            unit(NE - 1, last=True)
            act.wait_ge(sem("units_known"), 1)
            for j in range(NU_MAX):
                n_over = act.value_load(unit_i[0:1, 3:4], min_val=0, max_val=NU_MAX)
                with act.If(n_over > j):
                    for i in range(4):
                        split_high(2 * C_MOE + i, UP, FFN_CHUNKS * (NE + j), NF * (NE + j))
                    gathered(NE + j)
                    unit(NE + j, last=True)

        @block.vector
        def _(dve):
            steps = [0]

            def step(ins):
                steps[0] += 1
                ins.then_inc(sem("dve_step"), 1)

            def settle():
                dve.wait_ge(sem("dve_step"), steps[0])

            def chain(ins):
                step(ins)
                settle()

            def part_end(i):
                dve.drain().then_inc(part_done, 1)
                dve.wait_ge(part_done, N_PARTS * (i + 1))

            done = [0]

            def split_low(p, shape, more=0):
                c, half = p // 2, p % 2
                dve.wait_ge(hi_ready, p + 1 + 2 * more)
                dve.tensor_tensor(split_piece(w_lo, c, shape, half), raw_piece(c, shape, half),
                                  F(split_piece(w_hi, c, shape, half)), ALU.subtract).then_inc(lo_ready, 1)

            def splits_to(p):
                while done[0] <= p:
                    split_low(done[0], shape_of(done[0] // 2))
                    done[0] += 1

            def rsqrt(n):
                v, t, r = stat[:, 1, 0:n], stat[:, 2, 0:n], stat[:, 4, 0:n]
                chain(dve.tensor_scalar(t.bitcast(I32), v.bitcast(I32), 1, None, ALU.logical_shift_right))
                chain(dve.tensor_scalar(r.bitcast(I32), t.bitcast(I32), -1.0, RSQRT_BITS, ALU.mult, ALU.add))
                for _ in range(3):
                    chain(dve.tensor_tensor(t, r, r, ALU.mult))
                    chain(dve.tensor_tensor(t, t, v, ALU.mult))
                    chain(dve.tensor_scalar(t, t, -0.5, 1.5, ALU.mult, ALU.add))
                    chain(dve.tensor_tensor(r, t, r, ALU.mult))

            def variance(n, width, c0=0):
                chain(dve.tensor_scalar(stat[:, 1, c0:c0 + n], stat[:, 0, c0:c0 + n], 1.0 / width, EPS, ALU.mult, ALU.add))

            def norm_rows(src, i):
                dve.wait_ge(sem("sumsq_ready"), i + 1)
                variance(TB, D)
                rsqrt(TB)
                for t in range(TB):
                    dve.tensor_scalar(xr[:, t, :], src[:, t, :], stat[:, 4, t:t + 1], None, ALU.mult).then_inc(
                        sem("rows_normed"), 1)

            def low_T(nk, base, gain, bank0=0):
                for b in range(nk // 2):
                    dve.wait_ge(sem("xT_hi_ready"), base + b + 1)
                    for kk in range(2):
                        k = 2 * b + kk
                        ins = dve.scalar_tensor_tensor(
                            out=xT_lo[:, k, :], in0=B[bank0 + b][:, kk * S:(kk + 1) * S],
                            scalar=1.0 if gain is None else gains[:, gain + k:gain + k + 1],
                            in1=F(xT_hi[:, k, :]), op0=ALU.mult, op1=ALU.subtract)
                    ins.then_inc(sem("xT_ready"), 1)

            dve.wait_ge(sem("consts_ready"), 1)
            dve.wait_ge(sem("bc_here"), 16 * 7)
            chain(dve.tensor_copy(small[:, 0:TB], pos_i[:, :]))
            for t in range(TB):
                step(dve.tensor_scalar(angle[:, 0, t, :], angle[:, 0, t, :], small[:, t:t + 1], None, ALU.mult))
            settle()
            for i, shift in ((2, 0.0), (3, 0.25)):
                chain(dve.tensor_scalar(angle[:, 1], angle[:, 0], INV_2PI, shift, ALU.mult, ALU.add))
                chain(dve.tensor_scalar(angle[:, 1], angle[:, 1], MAGIC, None, ALU.add))
                chain(dve.tensor_scalar(angle[:, 1], angle[:, 1], MAGIC, None, ALU.subtract))
                chain(dve.scalar_tensor_tensor(out=angle[:, i], in0=angle[:, 1], scalar=-TWO_PI[0], in1=angle[:, 0],
                                               op0=ALU.mult, op1=ALU.add))
                for part_c in TWO_PI[1:]:
                    chain(dve.scalar_tensor_tensor(out=angle[:, i], in0=angle[:, 1], scalar=-part_c, in1=angle[:, i],
                                                   op0=ALU.mult, op1=ALU.add))
                if shift:
                    chain(dve.tensor_scalar(angle[:, i], angle[:, i], HALF_PI, None, ALU.add))
                chain(dve.tensor_scalar(angle[:, i], angle[:, i], PI_BOUND, -PI_BOUND, ALU.min, ALU.max))
            chain(dve.tensor_copy(wr_hi[:, :, :], w_router[:, :, :]))
            dve.tensor_tensor(wr_lo[:, :, :], w_router[:, :, :], F(wr_hi[:, :, :]), ALU.subtract).then_inc(
                sem("angles_ready"), 1)

            norm_rows(xr, 0)
            dve.wait_ge(sem("gains_ready"), 2)
            splits_to(2 * (C_MEM + 2) + 1)
            low_T(KD, 0, G["mem"])
            dve.wait_ge(piece_used, 2 * (C_MEM + 2))
            dve.wait_ge(sem("vm_copied"), TB)
            for t in range(TB):
                ins = dve.tensor_copy(km[:, t, :], B[4 + t][:, 0:MEMW])
            ins.then_inc(sem("tile_evacuated"), 1)
            dve.wait_ge(sem("tile_evacuated"), 1)

            def head_sums(src, dst, scratch):
                chain(dve.tensor_tensor(scratch, src, src, ALU.mult))
                chain(dve.tensor_reduce(dst, scratch, AX, ALU.add))

            head_sums(km[:, :, :].rearrange("p t (h d) -> p (t h) d", h=MH), stat[:, 0, 0:TB * MH],
                      og[:, 0, 0:TB * MEMW].rearrange("p (n d) -> p n d", n=TB * MH))
            variance(TB * MH, MD)
            rsqrt(TB * MH)
            kmv = km[:, :, :].rearrange("p t (h d) -> p (t h) d", h=MH)
            dve.tensor_tensor(kmv, kmv, stat[:, 4, 0:TB * MH].unsqueeze(2).to_broadcast([P, TB * MH, MD]),
                              ALU.mult).then_inc(sem("km_normed"), 1)
            dve.wait_ge(sem("km_normed"), 1)
            part_end(0)

            norm_rows(h, 1)
            splits_to(2 * (C_QK + 1) + 1)
            low_T(KD, 4, G["mix0"])
            for t in range(4):
                splits_to(2 * (C_QK + 2 * t + 3) + 1)
                dve.wait_ge(sem("qk_copied"), t + 1)
                for tap in range(TAPS - 1, -1, -1):
                    if tap < TAPS - 1:
                        settle()
                    for q in range(4):
                        b = 4 * t + q
                        u = qk_in[:, t % 2, q, tap:tap + S]
                        wcol = convw[:, tap * QKB + b:tap * QKB + b + 1]
                        if tap == TAPS - 1:
                            step(dve.tensor_scalar(qkT[:, b, :], u, wcol, None, ALU.mult))
                        else:
                            ins = dve.scalar_tensor_tensor(out=qkT[:, b, :], in0=u, scalar=wcol, in1=qkT[:, b, :],
                                                           op0=ALU.mult, op1=ALU.add)
                            if tap == 0 and q == 3:
                                ins.then_inc(sem("conv_done"), 1)
                            else:
                                step(ins)
            splits_to(2 * (C_GM + 1) + 1)
            dve.wait_ge(sem("tile_evacuated"), 5)
            step(dve.tensor_tensor(og[:, :, :].rearrange("p t (h d) -> p (t h) d", h=LH),
                                   og[:, :, :].rearrange("p t (h d) -> p (t h) d", h=LH),
                                   hnorm_bc[:, :].unsqueeze(1).to_broadcast([P, TB * LH, LD]), ALU.mult))
            splits_to(2 * (C_OUT0 + 1) + 1)
            dve.wait_ge(sem("gates_psum"), 1)
            step(dve.tensor_scalar(gr[:, 0, :], B[0][0:LH, 0:S], gate_bias[:, 0:1], None, ALU.add))
            chain(dve.tensor_scalar(gr[:, 2, :], B[0][0:LH, S:2 * S], gate_bias[:, 1:2], None, ALU.add))
            dve.scalar_tensor_tensor(out=gr[:, 1, :], in0=gr[:, 2, :], scalar=-1.0, in1=gr[:, 2, :], op0=ALU.mult,
                                     op1=ALU.max).then_inc(sem("gate_abs"), 1)
            step(dve.tensor_scalar(gr[:, 2, :], gr[:, 2, :], 0.0, None, ALU.min))
            dve.wait_ge(sem("qmT_psum"), 1)
            step(dve.tensor_copy(qmT[:, :, :].rearrange("p a s -> p (a s)"), B[1][:, :]))
            dve.wait_ge(sem("gate_ln"), 1)
            settle()
            chain(dve.tensor_tensor(gr[:, 2, :], gr[:, 2, :], gr[:, 1, :], ALU.subtract))
            dve.wait_ge(sem("consts_ready"), 1)
            chain(dve.memset(gr[:, 7, :], 1.0))
            chain(dve.tensor_tensor_scan(gr[:, 6, :], gr[:, 7, :], gr[:, 2, :], 0.0, ALU.mult, ALU.add))
            chain(dve.tensor_tensor(gr[:, 3, :], gr[:, 0, :], gr[:, 6, :], ALU.subtract))
            chain(dve.tensor_tensor_scan(gr[:, 4, :], gr[:, 7, :], gr[:, 3, :], 0.0, ALU.mult, ALU.max))
            dve.tensor_tensor(gr[:, 5, :], gr[:, 6, :], gr[:, 4, :], ALU.add).then_inc(sem("gate_m"), 1)
            dve.wait_ge(sem("gate_cols_psum"), 1)
            chain(dve.tensor_copy(small[:, 0:2 * TB * LH], B[0][:, 0:2 * TB * LH]))
            part_end(1)

            for hd in range(LH):
                peak = B[2 + hd // 2][:, (hd % 2) * S:(hd % 2 + 1) * S]
                step(dve.tensor_scalar(decay[:, hd, 0:S], peak, small[:, hd:hd + 1], 0.0, ALU.subtract, ALU.max))
                dve.tensor_scalar(decay[:, hd, S:S + P], peak[:, P:S], small[:, LH + hd:LH + hd + 1], 0.0, ALU.subtract,
                                  ALU.max).then_inc(sem("decay_exp"), 1)
            for hd in range(LH):
                dve.wait_ge(sem("decay_ready"), hd + 1)
                diag = decay[:, hd, :].rearrange("p (b c) -> p b c", b=3)[:, 0:3:2, :]
                chain(dve.tensor_tensor(diag, diag, upto[:, :, :], ALU.mult))
                dve.wait_ge(sem("mscores_psum"), hd + 1)
                dve.scalar_tensor_tensor(out=decay[:, hd, :], in0=B[4 + hd][:, 0:384], scalar=float(LD) ** -0.5,
                                         in1=decay[:, hd, :], op0=ALU.mult, op1=ALU.mult).then_inc(
                    sem("mweights_ready"), 1)
            step(dve.tensor_tensor(small[:, 40:41], gains[:, G_MQ[0]:G_MQ[0] + 1], gains[:, G_MK[0]:G_MK[0] + 1], ALU.mult))
            qm = gm[:, :, 2 * LH:].rearrange("p t (h d) -> p t h d", h=MH)
            sqm = km[:, :, :].rearrange("p t (h d) -> p t h d", h=MH)
            chain(dve.tensor_tensor(sqm, qm, qm, ALU.mult))
            chain(dve.tensor_reduce(stat[:, 0, 8:16].rearrange("p (t h) -> p t h", t=TB), sqm, AX, ALU.add))
            variance(8, MD, 8)
            dve.tensor_scalar(kmTs_0, kmT[:, :, :], small[:, 40:41], float(MD) ** -0.5, ALU.mult, ALU.mult).then_inc(
                sem("mem_ops_ready"), 1)
            dve.wait_ge(sem("num_copied"), LH)
            den = num[:, :, :, LD]
            rec = small[:, 16:24].rearrange("p (t h) -> p t h", t=TB)
            chain(dve.scalar_tensor_tensor(out=rec, in0=den, scalar=-1.0, in1=den, op0=ALU.mult, op1=ALU.max))
            chain(dve.tensor_tensor(rec, rec, small[:, 8:16].rearrange("p (t h) -> p t h", t=TB), ALU.max))
            chain(dve.reciprocal(rec, rec))
            sqn = decay[:, :, :].rearrange("p h (a d) -> p (h a) d", d=LD)
            nv = num[:, :, :, 0:LD].rearrange("p t h d -> p (t h) d")
            chain(dve.tensor_tensor(sqn, nv, rec.rearrange("p t h -> p (t h)").unsqueeze(2).to_broadcast([P, TB * LH, LD]),
                                    ALU.mult))
            chain(dve.tensor_copy(nv, sqn))
            chain(dve.tensor_tensor(sqn, nv, nv, ALU.mult))
            chain(dve.tensor_reduce(stat[:, 0, 0:8], sqn, AX, ALU.add))
            variance(8, LD)
            rsqrt(16)
            ogv = og[:, :, :].rearrange("p t (h d) -> p t h d", h=LH)
            for t in range(TB):
                for hd in range(LH):
                    c = t * LH + hd
                    step(dve.scalar_tensor_tensor(out=y[:, t, hd * LD:(hd + 1) * LD], in0=num[:, t, hd, 0:LD],
                                                  scalar=stat[:, 4, c:c + 1], in1=ogv[:, t, hd, :], op0=ALU.mult,
                                                  op1=ALU.mult))
            settle()
            part_end(2)

            def memory_attention(layer, rq):
                dve.tensor_copy(small[:, 0:8], rq).then_inc(sem("mem_ops_ready"), 1)
                dve.wait_ge(sem("mem_ops_ready"), 2 * (layer + 1))
                dve.wait_ge(sem("mem_scores"), layer + 1)
                for t in range(TB):
                    for odd in range(2):
                        step(dve.tensor_reduce(small[:, 8 + t * MH + odd:8 + t * MH + odd + 3:2],
                                               B[4 + 2 * t + odd][:, :].rearrange("p (a s) -> p a s", a=2), AX, ALU.max))
                settle()
                dve.scalar_tensor_tensor(out=small[:, 8:16], in0=small[:, 8:16], scalar=-1.0, in1=small[:, 0:8],
                                         op0=ALU.mult, op1=ALU.mult).then_inc(sem("mem_bias"), 1)
                dve.wait_ge(sem("mem_probs"), MH * (layer + 1))
                chain(dve.reciprocal(small[:, 24:32], small[:, 16:24]))
                dve.wait_ge(sem("mem_out_psum"), layer + 1)
                chain(dve.tensor_tensor(
                    y[:, :, MAIN:].rearrange("p t (h d) -> p t h d", h=MH),
                    B[4][:, :].rearrange("p (t h d) -> p t h d", t=TB, h=MH),
                    small[:, 24:32].rearrange("p (t h) -> p t h", t=TB).unsqueeze(3).to_broadcast([P, TB, MH, MD]),
                    ALU.mult))

            memory_attention(0, stat[:, 4, 8:16])
            part_end(3)
            low_T(KD, 8, None)

            def add_tile(t, c, half):
                dve.wait_ge(piece_used, 2 * (c + 2))
                for tb in range(TB):
                    ins = dve.tensor_tensor(h[:, tb, half * 512:(half + 1) * 512], B[4 + 2 * (t % 2) + tb][:, :],
                                            h[:, tb, half * 512:(half + 1) * 512], ALU.add)
                ins.then_inc(sem("tile_evacuated"), 1)

            splits_to(2 * (C_OUT0 + 3) + 1)
            add_tile(TILE_OUT0, C_OUT0, 0)
            splits_to(2 * (C_FFN + 1) + 1)
            add_tile(TILE_OUT0 + 1, C_OUT0 + 2, 1)
            part_end(4)

            norm_rows(h, 2)
            low_T(KD, 12, G["ffn0"])

            def product(c, more, n, first=False):
                dve.wait_ge(sem("silu_done"), n + 1)
                dve.wait_ge(piece_used, 2 * (c + more))
                if not first:
                    dve.wait_ge(sem("aT_ready"), n)
                for b in range(2):
                    ins = dve.tensor_tensor(act_f[:, b * 512:(b + 1) * 512], B[2 + b][:, :],
                                            silu_g[:, b * 512:(b + 1) * 512], ALU.mult)
                ins.then_inc(sem("act_done"), 1)

            def low_act(n):
                dve.wait_ge(sem("aT_hi_ready"), n + 1)
                dve.tensor_tensor(aT_lo[:, :, :].rearrange("p q s -> p (q s)"), act_f[:, :],
                                  F(aT_hi[:, :, :]).rearrange("p q s -> p (q s)"), ALU.subtract).then_inc(sem("aT_ready"), 1)

            def ffn_body(i, next_shape):
                c, more = C_FFN + 4, 6 * i

                def pieces(a, b):
                    for j in range(a, b):
                        split_low(2 * c + j, DOWN if 8 <= j < 12 else UP if j < 8 else next_shape, more)

                pieces(4, 6)
                low_act(i)
                pieces(6, 13)
                product(c + 4, more, i + 1)
                pieces(13, 16)

            p0 = 2 * C_FFN
            for j in range(4, 8):
                split_low(p0 + j, UP)
            product(C_FFN + 4, 0, 0, first=True)
            for j in range(8, 12):
                split_low(p0 + j, UP)
            with dve.Fori(0, NF - 2) as i:
                ffn_body(i, UP)
            ffn_body(NF - 2, DOWN)
            low_act(NF - 1)
            done[0] = 2 * C_IN1
            splits_to(2 * (C_IN1 + 1) + 1)
            dve.wait_ge(piece_used, 2 * C_IN1)
            for t in range(TB):
                for half in range(2):
                    step(dve.tensor_tensor(h[:, t, half * 512:(half + 1) * 512], B[4 + 2 * t + half][:, :],
                                           h[:, t, half * 512:(half + 1) * 512], ALU.add))
            part_end(5)

            norm_rows(h, 3)
            low_T(KD, 16, G["mix1"])
            splits_to(2 * (C_UQ + 1) + 1)
            dve.wait_ge(sem("tile_evacuated"), TILE_IN1 + 1)
            lora = scr[:, 0:4, :].rearrange("p a b -> p (a b)")[:, 0:TB * 512].rearrange("p (t n) -> p t n", t=TB)
            chain(dve.tensor_tensor(lora, c1[:, :, :], c1[:, :, :], ALU.mult))
            step(dve.tensor_reduce(stat[:, 0, 0:TB], lora[:, :, 0:QL], AX, ALU.add))
            chain(dve.tensor_reduce(stat[:, 0, TB:2 * TB], lora[:, :, QL:], AX, ALU.add))
            variance(TB, QL, 0)
            variance(TB, P, TB)
            rsqrt(2 * TB)
            for t in range(TB):
                step(dve.tensor_scalar(c1[:, t, 0:QL], c1[:, t, 0:QL], stat[:, 4, t:t + 1], None, ALU.mult))
                ins = dve.tensor_scalar(c1[:, t, QL:], c1[:, t, QL:], stat[:, 4, TB + t:TB + t + 1], None, ALU.mult)
                if t == TB - 1:
                    ins.then_inc(sem("lora_normed"), 1)
            low_T(4, 20, G["cq"])
            step(dve.tensor_tensor(small[:, 60:61], gains[:, G_QN:G_QN + 1], gains[:, G_KN:G_KN + 1], ALU.mult))
            dve.wait_ge(sem("tile_evacuated"), TILE_IN1 + 2)
            dve.wait_ge(sem("rope_ready"), 2)
            k_r = c2[:, :, 0:ROPE]
            step(dve.tensor_tensor(kr[:, 0], k_r, k_r, ALU.mult))
            chain(dve.tensor_tensor(kr[:, 1], k_r, krope_bc[:, :].unsqueeze(1).to_broadcast([P, TB, ROPE]), ALU.mult))
            step(dve.tensor_reduce(stat[:, 0, 32:34], kr[:, 0], AX, ALU.add))

            def halves(ap):
                return (ap[:, :, 0:HALF], ap[:, :, HALF:ROPE]) if len(ap.shape) == 3 else (
                    ap[:, :, :, 0:HALF], ap[:, :, :, HALF:ROPE])

            def rotate(dst, src, t1, t2, c, s):
                (a, b), (da, db) = halves(src), halves(dst)
                step(dve.tensor_tensor(t1, a, c, ALU.mult))
                chain(dve.tensor_tensor(t2, b, s, ALU.mult))
                chain(dve.tensor_tensor(da, t1, t2, ALU.subtract))
                step(dve.tensor_tensor(t1, b, c, ALU.mult))
                chain(dve.tensor_tensor(t2, a, s, ALU.mult))
                return dve.tensor_tensor(db, t1, t2, ALU.add)

            step(rotate(kr[:, 2], kr[:, 1], kr[:, 3, :, 0:HALF], kr[:, 3, :, HALF:], cos[:, :, :], sin[:, :, :]))
            for t in range(4):
                splits_to(2 * (C_UQ + 2 + t) + 1)
            dve.wait_ge(sem("tile_evacuated"), TILE_IN1 + 8)
            H12 = TB * AH
            sq = scr[:, :, :].rearrange("p a b -> p (a b)")
            qv = qS[:, :, :, :].rearrange("p t h d -> p (t h) d")
            kv = kS[:, :, :, :].rearrange("p t h d -> p (t h) d")
            q2 = sq[:, 0:H12 * QKD].rearrange("p (h d) -> p h d", h=H12)
            chain(dve.tensor_tensor(q2, qv, qv, ALU.mult))
            chain(dve.tensor_reduce(stat[:, 0, 0:H12], q2, AX, ALU.add))
            k2 = sq[:, 0:H12 * NOPE].rearrange("p (h d) -> p h d", h=H12)
            chain(dve.tensor_tensor(k2, kv, kv, ALU.mult))
            chain(dve.tensor_reduce(stat[:, 0, H12:2 * H12], k2, AX, ALU.add))
            kss = stat[:, 0, H12:2 * H12].rearrange("p (t h) -> p t h", t=TB)
            chain(dve.tensor_tensor(kss, kss, stat[:, 0, 32:34].unsqueeze(2).to_broadcast([P, TB, AH]), ALU.add))
            mq_v = c2[:, :, ROPE:].rearrange("p t (h d) -> p t h d", h=MH)
            m2 = sq[:, 0:TB * MEMW].rearrange("p (t h d) -> p t h d", t=TB, h=MH)
            chain(dve.tensor_tensor(m2, mq_v, mq_v, ALU.mult))
            chain(dve.tensor_reduce(stat[:, 0, 24:32].rearrange("p (t h) -> p t h", t=TB), m2, AX, ALU.add))
            variance(24, QKD, 0)
            variance(8, MD, 24)
            part_end(6)
            chain(dve.tensor_tensor(rotq[:, :, :, :].rearrange("p t h d -> p (t h) d"), qv[:, :, NOPE:],
                                    qrope_bc[:, :].unsqueeze(1).to_broadcast([P, H12, ROPE]), ALU.mult))
            q0 = sq[:, 0:H12 * ROPE].rearrange("p (t h d) -> p t h d", t=TB, h=AH)
            chain(dve.tensor_copy(q0, rotq[:, :, :, :]))
            cb = cos[:, :, :].unsqueeze(2).to_broadcast([P, TB, AH, HALF])
            sbb = sin[:, :, :].unsqueeze(2).to_broadcast([P, TB, AH, HALF])
            t1, t2 = (sq[:, (2 + i) * H12 * HALF:(3 + i) * H12 * HALF].rearrange("p (t h d) -> p t h d", t=TB, h=AH)
                      for i in range(2))
            rotate(rotq[:, :, :, :], q0, t1, t2, cb, sbb).then_inc(sem("q_ready"), 1)
            rsqrt(32)
            rk = stat[:, 4, H12:2 * H12]
            step(dve.tensor_tensor(kv, kv, rk.unsqueeze(2).to_broadcast([P, H12, NOPE]), ALU.mult))
            rkv = rk.rearrange("p (t h) -> p t h", t=TB)
            for t in range(TB):
                step(dve.tensor_tensor(rotk[:, t], kr[:, 2, t, :].unsqueeze(1).to_broadcast([P, AH, ROPE]),
                                       rkv[:, t].unsqueeze(2).to_broadcast([P, AH, ROPE]), ALU.mult))
            settle()
            dve.tensor_scalar(small[:, 0:H12], stat[:, 4, 0:H12], float(QKD) ** -0.5, None, ALU.mult).then_inc(
                sem("k_ready"), 1)
            for hd in range(AH):
                dve.wait_ge(sem("scores_psum"), hd + 1)
                step(dve.tensor_tensor(scr[:, hd, :].rearrange("p (b c) -> p b c", b=3),
                                       B[hd][:, 0:384].rearrange("p (b c) -> p b c", b=3), negmask[:, :, :], ALU.add))
            settle()
            step(dve.tensor_reduce(small[:, 12:18], scr[:, :, 0:P], AX, ALU.max))
            chain(dve.tensor_reduce(small[:, 18:24], scr[:, :, P:P + S], AX, ALU.max))
            dve.wait_ge(sem("k_ready"), 1)
            dve.scalar_tensor_tensor(out=small[:, 12:24], in0=small[:, 12:24], scalar=-1.0, in1=small[:, 0:12],
                                     op0=ALU.mult, op1=ALU.mult).then_inc(sem("score_bias"), 1)
            dve.wait_ge(sem("probs_ready"), AH)
            chain(dve.reciprocal(small[:, 36:48], small[:, 24:36]))
            dve.wait_ge(sem("heads_psum"), 1)
            rs = small[:, 36:48].rearrange("p (t h) -> p t h", t=TB)
            for t in range(TB):
                step(dve.tensor_tensor(y[:, t, 0:4 * VD].rearrange("p (h d) -> p h d", h=4),
                                       B[4 + t][:, :].rearrange("p (h d) -> p h d", h=4),
                                       rs[:, t, 0:4].unsqueeze(2).to_broadcast([P, 4, VD]), ALU.mult))
                step(dve.tensor_tensor(y[:, t, 4 * VD:MAIN].rearrange("p (h d) -> p h d", h=2),
                                       B[6][:, t * 2 * VD:(t + 1) * 2 * VD].rearrange("p (h d) -> p h d", h=2),
                                       rs[:, t, 4:6].unsqueeze(2).to_broadcast([P, 2, VD]), ALU.mult))
            settle()
            dve.wait_ge(sem("qmT_psum"), 2)
            step(dve.tensor_copy(qmT[:, :, :].rearrange("p a s -> p (a s)"), B[7][:, :]))
            chain(dve.tensor_tensor(small[:, 61:62], gains[:, G_MQ[1]:G_MQ[1] + 1], gains[:, G_MK[1]:G_MK[1] + 1], ALU.mult))
            dve.tensor_scalar(kmTs_1, kmT[:, :, :], small[:, 61:62], float(MD) ** -0.5, ALU.mult, ALU.mult).then_inc(
                sem("mem_ops_ready"), 1)
            part_end(7)
            memory_attention(1, stat[:, 4, 24:32])
            part_end(8)
            low_T(KD, 22, None)
            splits_to(2 * (C_OUT1 + 3) + 1)
            add_tile(TILE_OUT1, C_OUT1, 0)
            splits_to(2 * (C_MOE + 1) + 1)
            add_tile(TILE_OUT1 + 1, C_OUT1 + 2, 1)
            part_end(9)

            norm_rows(h, 4)
            low_T(KD, 26, G["ffn1"])
            for t in range(TB):
                dve.wait_ge(sem("xr_hi_ready"), t + 1)
                step(dve.tensor_tensor(xr_lo[:, t, :], xr[:, t, :], F(xr_hi[:, t, :]), ALU.subtract))
            dve.wait_ge(sem("logits_psum"), 1)
            chain(dve.tensor_copy(lg[:, :, :].rearrange("p t e -> p (t e)"), B[4][:, 0:TB * NE]))
            for t in range(TB):
                own = lg[:, t, :].unsqueeze(2).to_broadcast([P, NE, NE])
                other = lg[:, t, :].unsqueeze(1).to_broadcast([P, NE, NE])
                step(dve.tensor_tensor(cmp[:, 0, t], other, own, ALU.is_gt))
                step(dve.tensor_tensor(cmp[:, 1, t], other, own, ALU.is_equal))
            settle()
            for t in range(TB):
                step(dve.tensor_tensor(cmp[:, 1, t], cmp[:, 1, t], earlier[:, :, :], ALU.mult))
            settle()
            chain(dve.tensor_tensor(cmp[:, 2], cmp[:, 0], cmp[:, 1], ALU.add))
            chain(dve.tensor_reduce(rt[:, 0], cmp[:, 2], AX, ALU.add))
            step(dve.tensor_scalar(rt[:, 1], rt[:, 0], 0.0, None, ALU.is_equal))
            step(dve.tensor_scalar(rt[:, 2], rt[:, 0], 1.0, None, ALU.is_equal))
            settle()
            step(dve.tensor_tensor(rt[:, 3], rt[:, 1], lg[:, :, :], ALU.mult))
            step(dve.tensor_tensor(rt[:, 4], rt[:, 2], lg[:, :, :], ALU.mult))
            dve.tensor_tensor(rt[:, 5], rt[:, 1], rt[:, 2], ALU.add).then_inc(sem("routed"), 1)
            settle()
            chain(dve.tensor_tensor(rt[:, 6], rt[:, 4], rt[:, 3], ALU.subtract))
            dve.tensor_reduce(rt[:, 7, :, 0], rt[:, 6], AX, ALU.add).then_inc(sem("top_diff"), 1)
            dve.wait_ge(sem("top_exp"), 1)
            chain(dve.tensor_scalar(rt[:, 9, :, 0:1], rt[:, 8, :, 0:1], 1.0, None, ALU.add))
            chain(dve.reciprocal(rt[:, 9, :, 0:1], rt[:, 9, :, 0:1]))
            chain(dve.tensor_tensor(rt[:, 10, :, 0:1], rt[:, 8, :, 0:1], rt[:, 9, :, 0:1], ALU.mult))
            for t in range(TB):
                step(dve.tensor_scalar(rt[:, 11, t, :], rt[:, 1, t, :], rt[:, 9, t, 0:1], None, ALU.mult))
            settle()
            for t in range(TB):
                step(dve.scalar_tensor_tensor(out=rt[:, 12, t, :], in0=rt[:, 2, t, :], scalar=rt[:, 10, t, 0:1],
                                              in1=rt[:, 11, t, :], op0=ALU.mult, op1=ALU.add))
            dve.wait_ge(sem("slots_psum"), 1)
            chain(dve.tensor_copy(posc[:, :, :].rearrange("p t e -> p (t e)"), B[5][:, 0:3 * NE]))
            for n, src in enumerate((posc[:, 0:TB, :], rt[:, 5], rt[:, 12])):
                step(dve.tensor_copy(tab[:, 0:NE, n, :].rearrange("p e t -> p t e"), src))
            def mark(u):
                dve.tensor_copy(cur[:, :, :].unsqueeze(1), tab[:, bass.ds(u, 1), :, :]).then_inc(sem("cur_ready"), 1)
                dve.wait_ge(sem("cur_ready"), u + 1)
                for t in range(TB):
                    ins = dve.tensor_scalar(onehot[:, t, :], iota[:, :], cur[:, 0, t:t + 1], cur[:, 1, t:t + 1],
                                            ALU.is_equal, ALU.mult)
                ins.then_inc(sem("onehot_ready"), 1)

            settle()
            mark(0)
            chain(dve.tensor_scalar(over[:, 0, :], posc[:, TB, :], float(P), None, ALU.is_gt))
            chain(dve.tensor_tensor_scan(over[:, 1, :], ones[:, 0:NE], over[:, 0, :], 0.0, ALU.mult, ALU.add))
            step(dve.tensor_scalar(rt[:, 13], posc[:, 0:TB, :], -float(P), None, ALU.add))
            step(dve.tensor_copy(unit_f[:, 3:4], over[0:1, 1, NE - 1:NE]))
            for j in range(NU_MAX):
                chain(dve.tensor_scalar(over[:, 2, :], over[:, 1, :], float(j + 1), None, ALU.is_equal))
                chain(dve.tensor_tensor(over[:, 2, :], over[:, 2, :], over[:, 0, :], ALU.mult))
                sel = over[:, 2, :].unsqueeze(1).to_broadcast([P, TB, NE])
                for n, src in enumerate((rt[:, 13], rt[:, 5], rt[:, 12])):
                    chain(dve.tensor_tensor(rt[:, 14], src, sel, ALU.mult))
                    chain(dve.tensor_reduce(tab[:, NE + j, n, :], rt[:, 14], AX, ALU.add))
                chain(dve.tensor_tensor(over[:, 3, :], over[:, 2, :], iota[:, 0:NE], ALU.mult))
                chain(dve.tensor_reduce(unit_f[:, j:j + 1], over[0:1, 3, :], AX, ALU.add))
            dve.tensor_copy(unit_i[:, :], unit_f[:, :]).then_inc(sem("units_known"), 1)
            part_end(10)

            def gathered(u):
                for b in range(2):
                    dve.wait_ge(sem("gather_hi"), 2 * u + b + 1)
                    for kk in range(4):
                        k = 4 * b + kk
                        ins = dve.scalar_tensor_tensor(
                            out=xT_lo[:, k, 0:P], in0=B[b][:, kk * P:(kk + 1) * P],
                            scalar=gains[:, G["ffn1"] + k:G["ffn1"] + k + 1], in1=F(xT_hi[:, k, 0:P]),
                            op0=ALU.mult, op1=ALU.subtract)
                    ins.then_inc(sem("gather_ready"), 1)

            def scaled(u):
                dve.wait_ge(sem("turned"), u + 1)
                for half in range(2):
                    dve.wait_ge(sem("ys_hi"), 2 * u + half + 1)
                    dve.scalar_tensor_tensor(out=ys_lo[:, half * 512:(half + 1) * 512], in0=B[4 + half][:, :],
                                             scalar=gslot[:, 0:1], in1=F(ys_hi[:, half * 512:(half + 1) * 512]),
                                             op0=ALU.mult, op1=ALU.subtract).then_inc(sem("ys_ready"), 1)

            def added(u):
                for t in range(TB):
                    for half in range(2):
                        dve.wait_ge(sem("back_psum"), 4 * u + 2 * t + half + 1)
                        dve.tensor_tensor(h[:, t, half * 512:(half + 1) * 512], B[6 + half][:, :],
                                          h[:, t, half * 512:(half + 1) * 512], ALU.add).then_inc(sem("h_added"), 1)

            def e_product(c, more, n):
                dve.wait_ge(sem("esilu_done"), n + 1)
                dve.wait_ge(piece_used, 2 * (c + more))
                dve.tensor_tensor(act_f[:, 0:FC], B[1][:, :], silu_g[:, 0:FC], ALU.mult).then_inc(sem("eact_done"), 1)

            def e_low(n):
                dve.wait_ge(sem("eaT_hi"), n + 1)
                dve.tensor_tensor(aT_lo[:, :, 0:P], B[2][:, :].rearrange("p (q s) -> p q s", q=FB),
                                  F(aT_hi[:, :, 0:P]), ALU.subtract).then_inc(sem("eaT_ready"), 1)

            def unit(u, last=False):
                more, n0, p0 = FFN_CHUNKS * u, NF * u, 2 * C_MOE

                for j in (6, 7):
                    split_low(p0 + j, UP, more)
                e_product(C_MOE + 4, more, n0)
                for j in range(8, 12):
                    split_low(p0 + j, UP, more)

                def e_step(i, next_shape):
                    c, m = C_MOE + 4, more + 6 * i

                    def pieces(a, b):
                        for j in range(a, b):
                            split_low(2 * c + j, DOWN if 8 <= j < 12 else UP if j < 8 else next_shape, m)

                    pieces(4, 9)
                    e_low(n0 + i)
                    pieces(9, 12)
                    e_product(c + 4, m, n0 + i + 1)
                    pieces(12, 16)

                with dve.Fori(0, NF - 2) as i:
                    e_step(i, UP)
                if not last:
                    mark(u + 1)
                e_step(NF - 2, DOWN)
                e_low(n0 + NF - 1)
                if last:
                    scaled(u)
                    added(u)
                    return
                for j in (0, 1):
                    split_low(p0 + 2 * FFN_CHUNKS + j, UP, more)
                gathered(u + 1)
                for j in (2, 3):
                    split_low(p0 + 2 * FFN_CHUNKS + j, UP, more)
                scaled(u)
                for j in (4, 5):
                    split_low(p0 + 2 * FFN_CHUNKS + j, UP, more)
                added(u)

            gathered(0)
            for j in (4, 5):
                split_low(2 * C_MOE + j, UP)
            with dve.Fori(0, NE - 1) as u:
                unit(u)
            unit(NE - 1, last=True)
            for j in range(NU_MAX):
                n_over = dve.value_load(unit_i[0:1, 3:4], min_val=0, max_val=NU_MAX)
                with dve.If(n_over > j):
                    mark(NE + j)
                    more = FFN_CHUNKS * (NE + j)
                    for i in range(4):
                        split_low(2 * C_MOE + i, UP, more)
                    gathered(NE + j)
                    for i in (4, 5):
                        split_low(2 * C_MOE + i, UP, more)
                    unit(NE + j, last=True)
            dve.drain().then_inc(sem("h_final"), 1)


_INS = [
    "x", "mem", "positions", "mem_norm", "w_mem_kv",
    "ln_mix0", "w_in0", "conv_w0", "b_i0", "b_f0", "h_norm0", "mq_norm0", "mk_norm0", "w_out0",
    "ln_ffn0", "w_gate0", "w_up0", "w_down0",
    "ln_mix1", "w_in1", "cq_norm1", "ckv_norm1", "w_uq1", "w_ukv1", "q_norm1", "k_norm1", "mq_norm1", "mk_norm1", "w_out1",
    "ln_ffn1", "w_router1", "we_gate1", "we_up1", "we_down1",
]


def kernel(**inputs):
    import numpy as _np
    import concourse.bacc as _bacc
    from concourse import mybir as _mybir
    from concourse.bass_utils import run_bass_kernel_spmd as _run

    nc = _bacc.Bacc("TRN2", target_bir_lowering=False, num_devices=1)
    arrays, args = {}, []
    for name in _INS:
        a = _np.ascontiguousarray(inputs[name])
        arrays[f"in_{name}_dram"] = a
        args.append(nc.dram_tensor(f"in_{name}_dram", a.shape, _mybir.dt.from_np(a.dtype), kind="ExternalInput").ap())
    shape = tuple(inputs["x"].shape)
    args.append(nc.dram_tensor("out_0_dram", shape, _mybir.dt.float32, kind="ExternalOutput").ap())
    hybrid_trunk(nc, *args)
    r = _run(nc, [arrays], core_ids=[0])
    return r.results[0]["out_0_dram"]
```

```python
from contextlib import ExitStack

import concourse.bass as bass
from concourse import mybir

F32 = mybir.dt.float32
F32R = mybir.dt.float32r
I32 = mybir.dt.int32
ALU = mybir.AluOpType
ACT = mybir.ActivationFunctionType
AX = mybir.AxisListType.X

P = 128
EPS = 1e-6
ROPE_THETA = 10000.0
NEG = -1e30
TWO_PI = (201 / 32, 2029 / 2**20, 3.0199159819e-07)
INV_2PI = 0.15915494309189535
HALF_PI = 1.5707963267948966
PI_BOUND = 3.1415925
MAGIC = 1.5 * 2**23
RSQRT_BITS = float(0x5F3759DF)

RAW_SLOTS = 6
SPLIT_SLOTS = 6
CHUNK = 2048
PIECE = CHUNK // 2


def hybrid_trunk(
    nc: bass.Bass,
    x, mem, positions, mem_norm, w_mem_kv,
    ln_mix0, w_in0, conv_w0, b_i0, b_f0, h_norm0, mq_norm0, mk_norm0, w_out0,
    ln_ffn0, w_gate0, w_up0, w_down0,
    ln_mix1, w_in1, cq_norm1, ckv_norm1, w_uq1, w_ukv1, q_norm1, k_norm1, mq_norm1, mk_norm1, w_out1,
    ln_ffn1, w_router1, we_gate1, we_up1, we_down1,
    out,
):
    _, S, D = x.shape
    TB = S // P
    KD = D // P
    MH = 4
    MEMW = w_mem_kv.shape[1] // 2
    MD = MEMW // MH
    MAIN = D - MEMW
    LH = b_i0.shape[0]
    LD = MAIN // LH
    HB = LD // 2
    QKB = 2 * MAIN // HB
    TAPS = conv_w0.shape[0]
    NOPE = 128
    ROPE = MD
    HALF = ROPE // 2
    QKD = q_norm1.shape[0]
    AH = w_uq1.shape[1] // QKD
    VD = MAIN // AH
    QL = w_uq1.shape[0]
    NE = w_router1.shape[1]
    FF = w_gate0.shape[1]
    FC = 512
    NF = FF // FC
    FB = FC // P
    NU_MAX = 3
    UNITS = NE + NU_MAX
    assert (S, D, MD, LD, AH, QL) == (256, 1024, 64, 192, 6, 384) and FF % FC == 0

    with ExitStack() as ctx:
        sem_of = {}

        def sem(name):
            if name not in sem_of:
                sem_of[name] = ctx.enter_context(nc.semaphore(name))
            return sem_of[name]

        def sb(name, shape, dt=F32, scope=ctx):
            return scope.enter_context(nc.sbuf_tensor(name, shape, dt))

        B = [ctx.enter_context(nc.psum_tensor(f"bank{i}", [P, 512], F32)) for i in range(8)]

        raw = sb("raw", [P, RAW_SLOTS, CHUNK])
        w_hi = sb("w_hi", [P, SPLIT_SLOTS, PIECE], F32R)
        w_lo = sb("w_lo", [P, SPLIT_SLOTS, PIECE], F32R)
        h = sb("h", [P, TB, D])
        xT_hi = sb("xT_hi", [P, KD, S], F32R)
        xT_lo = sb("xT_lo", [P, KD, S], F32R)
        xr = sb("xr", [P, TB, D])
        ident = sb("ident", [P, P])
        ones = sb("ones", [P, P])
        upto = sb("upto", [P, 2, P])
        before = sb("before", [P, P])
        negmask = sb("negmask", [P, 3, P])
        iota = sb("iota", [P, P])
        earlier = sb("earlier", [P, NE, NE])
        gain_rows = sb("gain_rows", [P, P])
        gains = sb("gains", [P, P])
        conv_rows = sb("conv_rows", [TAPS * QKB, HB])
        convw = sb("convw", [HB, TAPS * QKB])
        hnorm_bc = sb("hnorm_bc", [P, LD])
        qrope_bc = sb("qrope_bc", [P, ROPE])
        krope_bc = sb("krope_bc", [P, ROPE])
        gate_bias = sb("gate_bias", [LH, 2])
        pos_i = sb("pos_i", [P, TB], I32)
        w_router = sb("w_router", [P, KD, NE])
        wr_hi = sb("wr_hi", [P, KD, NE], F32R)
        wr_lo = sb("wr_lo", [P, KD, NE], F32R)
        cos = sb("cos", [P, TB, HALF])
        sin = sb("sin", [P, TB, HALF])
        stat = sb("stat", [P, 5, 40])
        kmT = sb("kmT", [P, 2, S])
        vm = sb("vm", [P, TB, MEMW])
        small = sb("small", [P, 64])
        msmall = sb("msmall", [P, 4, TB * MH])

        rows, at = {}, 0
        for name, vec in (("mem", mem_norm), ("mix0", ln_mix0), ("ffn0", ln_ffn0), ("mix1", ln_mix1),
                          ("ffn1", ln_ffn1), ("cq", cq_norm1), ("ckv", ckv_norm1)):
            rows[name] = (at, vec)
            at += vec.shape[0] // P
        G_QN, G_KN, G_MQ, G_MK = at, at + 1, (at + 2, at + 3), (at + 4, at + 5)
        G = {name: a for name, (a, _) in rows.items()}

        y = xr
        qmT = sb("qmT", [P, 2, S])
        part = ExitStack()
        with part:
            km = sb("km", [P, TB, MEMW], scope=part)
            angle = sb("angle", [P, 4, TB, HALF], scope=part)
            qk_in = sb("qk_in", [HB, 2, 4, S + TAPS - 1], scope=part)
            qkT = sb("qkT", [HB, QKB, S], scope=part)
            vA = sb("vA", [P, TB, LH, LD + 2], scope=part)
            og = sb("og", [P, TB, MAIN], scope=part)
            gm = sb("gm", [P, TB, 2 * LH + MEMW], scope=part)
            gr = sb("gr", [LH, 8, S], scope=part)
            decay = sb("decay", [P, LH, 384], scope=part)
            late = sb("late", [P, D], scope=part)
            headsel = sb("headsel", [LH, LH, P], scope=part)
        part = ExitStack()
        with part:
            c1 = sb("c1", [P, TB, QL + P], scope=part)
            c2 = sb("c2", [P, TB, ROPE + MEMW], scope=part)
            qS = sb("qS", [P, TB, AH, QKD], scope=part)
            kS = sb("kS", [P, TB, AH, NOPE], scope=part)
            vS = sb("vS", [P, TB, AH, VD], scope=part)
            rotq = sb("rotq", [P, TB, AH, ROPE], scope=part)
            rotk = sb("rotk", [P, TB, AH, ROPE], scope=part)
            kr = sb("kr", [P, 4, TB, ROPE], scope=part)
            scr = sb("scr", [P, AH, 384], scope=part)
            qT = sb("qT", [P, AH, S], scope=part)
            kT = sb("kT", [P, AH, S], scope=part)
            qrT = sb("qrT", [P, AH // 2, S], scope=part)
            krT = sb("krT", [P, AH // 2, S], scope=part)
        part = ExitStack()
        with part:
            aT_hi = sb("aT_hi", [P, FB, S], F32R, scope=part)
            aT_lo = sb("aT_lo", [P, FB, S], F32R, scope=part)
            silu_g = sb("silu_g", [P, FB * S], scope=part)
            act_f = sb("act_f", [P, FB * S], scope=part)
            xr_hi = sb("xr_hi", [P, TB, D], F32R, scope=part)
            xr_lo = sb("xr_lo", [P, TB, D], F32R, scope=part)
            ys_hi = sb("ys_hi", [P, D], F32R, scope=part)
            ys_lo = sb("ys_lo", [P, D], F32R, scope=part)
            onehot = sb("onehot", [P, TB, P], F32R, scope=part)
            onehotT = sb("onehotT", [P, S], F32R, scope=part)
            lgT = sb("lgT", [NE, S], scope=part)
            lg = sb("lg", [P, TB, NE], scope=part)
            rt = sb("rt", [P, 16, TB, NE], scope=part)
            cmp = sb("cmp", [P, 3, TB, NE, NE], scope=part)
            posc = sb("posc", [P, TB + 1, NE], scope=part)
            tab = sb("tab", [P, UNITS, 3, TB], scope=part)
            cur = sb("cur", [P, 3, TB], scope=part)
            over = sb("over", [P, 8, NE], scope=part)
            unit_f = sb("unit_f", [1, 4], scope=part)
            unit_i = sb("unit_i", [1, 4], I32, scope=part)
            gslot = sb("gslot", [P, 1], scope=part)
        flat = lambda t: t.rearrange("p a b c -> p (a b c)")
        flat3 = lambda t: t.rearrange("p a b -> p (a b)")
        pT = flat(qS[:, :, :, :]).rearrange("p (h c) -> p h c", h=AH)
        mem_rows = (flat3(decay[:, :, :])[:, 0:D], late[:, :])
        kmTs_0, kmTs_1 = km[:, :, :], c1[:, 0, :].rearrange("p (a s) -> p a s", a=2)
        pm = lambda t, hd: flat3(xr[:, :, :])[:, (t * MH + hd) * S:(t * MH + hd + 1) * S]
        pmT_0 = lambda hd: flat3(og[:, :, :])[:, hd * 512:(hd + 1) * 512] if hd < 3 else late[:, 0:512]
        pmT_1 = lambda hd: flat3(qT[:, :, :])[:, hd * 512:(hd + 1) * 512] if hd < 3 else flat3(kT[:, :, :])[:, 0:512]

        chunks = []

        def add_chunk(view_shape, src):
            chunks.append((view_shape, src))
            return len(chunks) - 1

        def k_halves(w, c0, n):
            v = w.rearrange("(j k p) n -> j p k n", j=2, p=P)
            return [add_chunk((KD // 2, n), v[j, :, :, c0:c0 + n]) for j in range(2)]

        C_MEM = k_halves(w_mem_kv, 0, 2 * MEMW)[0]
        C_GM = k_halves(w_in0, 4 * MAIN, 2 * LH + MEMW)[0]
        C_QK = len(chunks)
        for t in range(8):
            k_halves(w_in0, t * 384, 384)
        C_V = C_QK + 8
        C_OUT0 = len(chunks)
        for t in range(2):
            k_halves(w_out0, 512 * t, 512)
        C_FFN = len(chunks)
        FFN_CHUNKS = 6 * NF
        C_IN1 = C_FFN + FFN_CHUNKS
        chunks_b = []
        first, chunks = chunks, chunks_b
        k_halves(w_in1, 0, 512)
        k_halves(w_in1, 512, 320)
        C_UQ = C_IN1 + len(chunks)
        for t in range(3):
            add_chunk((QL // P, 384), w_uq1.rearrange("(k p) n -> p k n", p=P)[:, :, 384 * t:384 * t + 384])
        C_UKV = C_IN1 + len(chunks)
        for t in range(3):
            add_chunk((2, 256), w_ukv1.rearrange("p (t a n) -> p t a n", t=3, a=2)[:, t])
        C_OUT1 = C_IN1 + len(chunks)
        for t in range(2):
            k_halves(w_out1, 512 * t, 512)
        C_MOE = C_IN1 + len(chunks)
        sizes = {i: s for i, (s, _) in enumerate(first)} | {C_IN1 + i: s for i, (s, _) in enumerate(chunks)}
        straight = {i: v for i, (_, v) in enumerate(first)} | {C_IN1 + i: v for i, (_, v) in enumerate(chunks)}
        UP, DOWN = (KD // 2, FC), (2, D)

        def view(t, slot, shape):
            k, n = shape
            return t[:, slot, 0:k * n].rearrange("p (k n) -> p k n", k=k)

        def pieces_of(shape):
            k = shape[0]
            return ((0, (k + 1) // 2), ((k + 1) // 2, k // 2))

        def raw_piece(c, shape, half):
            k0, nk = pieces_of(shape)[half]
            return view(raw, c % RAW_SLOTS, shape)[:, k0:k0 + nk, :]

        def split_piece(t, c, shape, half):
            return view(t, (2 * c + half) % SPLIT_SLOTS, (pieces_of(shape)[half][1], shape[1]))

        TERMS = ((0, 0), (0, 1), (1, 0))
        xT = (xT_hi, xT_lo)
        wS = (w_hi, w_lo)
        aT = (aT_hi, aT_lo)
        F = lambda ap: ap.bitcast(F32)

        raw_here = [sem(f"raw_here{i}") for i in range(RAW_SLOTS)]
        hi_ready, lo_ready, piece_used = sem("hi_ready"), sem("lo_ready"), sem("piece_used")

        N_ROW_DMAS = len(rows) + 2 + 4 + 1
        TILE_OUT0, TILE_IN1, TILE_OUT1 = 5, 7, 15
        tile_bank = lambda t, tb: B[4 + 2 * (t % 2) + tb]

        def copied(t):
            return t + 1 if t <= TILE_OUT0 else t


        def shape_of(c):
            return sizes.get(c, UP)

        block = ctx.enter_context(nc.Block())

        @block.sync
        def _(sp):
            for t in range(TB):
                sp.dma_start(mem_rows[t], mem.rearrange("o (b p) d -> p (o b) d", p=P)[:, t, :]).then_inc(sem("mem_here"), 16)
            for t in range(TB):
                sp.dma_start(h[:, t, :], x.rearrange("o (b p) d -> p (o b) d", p=P)[:, t, :]).then_inc(sem("x_here"), 16)
            n_dma = 0
            sp.wait_ge(sem("pool_step"), 1)
            for name, (a, vec) in rows.items():
                nk = vec.shape[0] // P
                sp.dma_start(gain_rows[a:a + nk, :], vec.rearrange("(k p) -> k p", p=P)).then_inc(sem("rows_here"), 16)
                n_dma += 1
            for g, vec in ((G_QN, q_norm1), (G_KN, k_norm1)):
                sp.dma_start(gain_rows[g:g + 1, :], vec.rearrange("(o n) -> o n", o=1)[:, 0:NOPE]).then_inc(
                    sem("rows_here"), 16)
                n_dma += 1
            for g, vec in ((G_MQ[0], mq_norm0), (G_MQ[1], mq_norm1), (G_MK[0], mk_norm0), (G_MK[1], mk_norm1)):
                sp.dma_start(gain_rows[g:g + 1, :].rearrange("o (r d) -> o r d", r=2),
                             vec.rearrange("(o r d) -> o r d", o=1, r=1).to_broadcast([1, 2, MD])).then_inc(sem("rows_here"), 16)
                n_dma += 1
            sp.dma_start(conv_rows[:, :], conv_w0.rearrange("t (b p) -> (t b) p", p=HB)).then_inc(sem("rows_here"), 16)
            n_dma += 1
            assert n_dma == N_ROW_DMAS
            sp.dma_start(gate_bias[:, 0:1], b_i0.rearrange("(n o) -> n o", o=1)).then_inc(sem("bias_here"), 16)
            sp.dma_start(gate_bias[:, 1:2], b_f0.rearrange("(n o) -> n o", o=1)).then_inc(sem("bias_here"), 16)
            sp.dma_start(hnorm_bc[:, :], h_norm0.partition_broadcast(P)).then_inc(sem("bias_here"), 16)

            def fetch(c, shape, src, more=0):
                if c >= RAW_SLOTS:
                    sp.wait_ge(lo_ready, 2 * (c - RAW_SLOTS + 1 + more))
                slot = c % RAW_SLOTS
                sp.dma_start(view(raw, slot, shape), src).then_inc(raw_here[slot], 16)

            def swiglu_chunks(c0, gate, up, down, more=0):
                def step(c, f, last=None, more=more):
                    for w in (gate, up):
                        for j in range(2):
                            fetch(c, UP, w(j, f), more)
                            c += 1
                    if last is not None:
                        for j in range(2):
                            fetch(c, DOWN, down(j, last), more)
                            c += 1
                step(c0, 0)
                with sp.Fori(0, NF - 1) as i:
                    step(c0 + 4, i + 1, i, more + 6 * i)
                for j in range(2):
                    fetch(c0 + 40 + j, DOWN, down(j, NF - 1), more)

            for c, src in straight.items():
                if c < C_FFN:
                    fetch(c, sizes[c], src)
                    if c == RAW_SLOTS - 1:
                        sp.dma_start(qrope_bc[:, :], q_norm1[NOPE:QKD].partition_broadcast(P)).then_inc(
                            sem("tables_here"), 16)
                        sp.dma_start(krope_bc[:, :], k_norm1[NOPE:QKD].partition_broadcast(P)).then_inc(
                            sem("tables_here"), 16)
                        sp.dma_start(pos_i[:, :], positions.rearrange("o (b p) -> p (o b)", p=P),
                                     allow_slow_non_contiguous=True).then_inc(sem("tables_here"), 16)
                        sp.dma_start(w_router[:, :, :], w_router1.rearrange("(k p) e -> p k e", p=P)).then_inc(
                            sem("tables_here"), 16)

            def cols(w):
                v = w.rearrange("(j k p) n -> j p k n", j=2, p=P)
                return lambda j, f: v[j, :, :, bass.ds(f * FC, FC)]

            down_v = w_down0.rearrange("(f j k p) n -> f j p k n", j=2, k=2, p=P)
            swiglu_chunks(C_FFN, cols(w_gate0), cols(w_up0),
                          lambda j, f: down_v[bass.ds(f, 1), j].rearrange("a p k n -> (a p) k n"))
            for c, src in straight.items():
                if c >= C_IN1:
                    fetch(c, sizes[c], src)

            def expert_cols(w, e):
                v = w.rearrange("e (j k p) n -> j e p k n", j=2, p=P)
                return lambda j, f: v[j, bass.ds(e, 1), :, :, bass.ds(f * FC, FC)].rearrange("a p k n -> (a p) k n")

            def expert(e, more, c0=C_MOE):
                v = we_down1.rearrange("e (f j k p) n -> j e f p k n", j=2, k=2, p=P)
                swiglu_chunks(c0, expert_cols(we_gate1, e), expert_cols(we_up1, e),
                              lambda j, f: v[j, bass.ds(e, 1), bass.ds(f, 1)].rearrange("a b p k n -> (a b p) k n"),
                              more)

            with sp.Fori(0, NE) as u:
                expert(u, FFN_CHUNKS * u)
            sp.wait_ge(sem("units_known"), 1)
            for j in range(NU_MAX):
                n_over = sp.value_load(unit_i[0:1, 3:4], min_val=0, max_val=NU_MAX)
                e = sp.value_load(unit_i[0:1, j:j + 1], min_val=0, max_val=NE - 1)
                with sp.If(n_over > j):
                    expert(e, FFN_CHUNKS * (NE + j))
            sp.wait_ge(sem("h_final"), 1)
            sp.dma_start(out.rearrange("o (b p) d -> p (o b) d", p=P), h[:, :, :]).then_inc(sem("stored"), 16)
            sp.wait_ge(sem("stored"), 16)

        @block.gpsimd
        def _(pool):
            n = 0

            def step(ins):
                nonlocal n
                n += 1
                ins.then_inc(sem("pool_step"), 1)

            def fill(t, value, pattern, base, cm, op, other):
                step(pool.memset(t, value))
                pool.wait_ge(sem("pool_step"), n)
                step(pool.affine_select(out=t, in_=t, compare_op=op, fill=other, base=base,
                                        pattern=pattern, channel_multiplier=cm))

            step(pool.memset(gain_rows[:, :], 0.0))
            step(pool.memset(ones[:, :], 1.0))
            fill(ident[:, :], 0.0, [[-1, P]], 0, 1, ALU.not_equal, 1.0)
            pool.wait_ge(sem("pool_step"), n)
            pool.iota(iota[:, :], [[1, P]], base=0, channel_multiplier=0,
                      allow_small_or_imprecise_dtypes=True).then_inc(sem("ident_ready"), 1)
            fill(upto[:, :, :], 1.0, [[0, 2], [1, P]], 0, -1, ALU.is_ge, 0.0)
            fill(before[:, :], 1.0, [[1, P]], -1, -1, ALU.is_ge, 0.0)
            step(pool.memset(negmask[:, :, :], 0.0))
            pool.wait_ge(sem("pool_step"), n)
            step(pool.affine_select(out=negmask[:, 0:3:2, :], in_=negmask[:, 0:3:2, :], compare_op=ALU.is_ge,
                                    fill=NEG, base=0, pattern=[[0, 2], [-1, P]], channel_multiplier=1))
            fill(earlier[:, :, :], 1.0, [[1, NE], [-1, NE]], -1, 0, ALU.is_ge, 0.0)
            fill(headsel[:, :, :], 0.0, [[-1, LH], [0, P]], 0, 1, ALU.not_equal, 1.0)
            step(pool.memset(vA[:, :, :, LD:LD + 2], 1.0))
            step(pool.memset(qk_in[:, :, :, 0:TAPS - 1], 0.0))
            for j in range(HALF):
                freq = float(ROPE_THETA ** (-j / HALF))
                step(pool.memset(angle[:, 0, :, j:j + 1], freq))
            pool.wait_ge(sem("pool_step"), n)
            pool.memset(small[:, 0:2], 0.0).then_inc(sem("consts_ready"), 1)

        @block.tensor
        def _(pe):
            def mm(o, a, b, start, stop, **kw):
                return pe.matmul(o, a, b, start=start, stop=stop, skip_group_check=True, **kw)

            def transpose_rows(src, nk, bank0=0, normed=None):
                for t in range(TB):
                    if normed is not None:
                        pe.wait_ge(sem("rows_normed"), normed + t + 1)
                    for k in range(0, nk, 2):
                        for kk in (k, k + 1):
                            last = pe.transpose(B[bank0 + k // 2][:, (kk - k) * S + t * P:(kk - k) * S + (t + 1) * P],
                                                src(t, kk), ident[:, :])
                        if t == TB - 1:
                            last.then_inc(sem("xT_psum"), 1)

            tiles = [0]

            def columns(parts, n, bank, ready=None, between=None, rows_first=False):
                seen, total = 0, sum(len(ks) for _, _, ks in parts)
                def product(w, i, k, tb, first, stop):
                    for a, b in TERMS:
                        last = mm(bank[tb][:, 0:n], xT[a][:, k, tb * P:(tb + 1) * P], w[b][:, i, :],
                                  start=(first and (a, b) == (0, 0)), stop=(stop and (a, b) == TERMS[-1]))
                    return last

                for j, (c, shape, ks) in enumerate(parts):
                    if j == 1 and between:
                        between()
                    if rows_first and j == len(parts) - 1:
                        pe.wait_ge(lo_ready, 2 * c + 2)
                        for tb in range(TB):
                            for half, (k0, nk) in enumerate(pieces_of(shape)):
                                w = [split_piece(x, c, shape, half) for x in wS]
                                for i, k in enumerate(ks[k0:k0 + nk]):
                                    last = product(w, i, k, tb, False, k == ks[-1])
                                if tb == TB - 1:
                                    last.then_inc(piece_used, 1)
                                elif half == 1:
                                    last.then_inc(sem("first_rows"), 1)
                        continue
                    for half, (k0, nk) in enumerate(pieces_of(shape)):
                        if ready is not None:
                            pe.wait_ge(sem("xT_ready"), ready + ks[k0] // 2 + 1)
                        pe.wait_ge(lo_ready, 2 * c + half + 1)
                        w = [split_piece(x, c, shape, half) for x in wS]
                        for i, k in enumerate(ks[k0:k0 + nk]):
                            for tb in range(TB):
                                last = product(w, i, k, tb, seen == 0, seen == total - 1)
                            seen += 1
                        last.then_inc(piece_used, 1)

            def proj(parts, n, ready=None, between=None, rows_first=False):
                t = tiles[0]
                tiles[0] += 1
                if t >= 2:
                    pe.wait_ge(sem("tile_evacuated"), copied(t - 2))
                columns(parts, n, [tile_bank(t, tb) for tb in range(TB)], ready, between, rows_first)

            def proj_one_k(c, k):
                t = tiles[0]
                tiles[0] += 1
                pe.wait_ge(sem("tile_evacuated"), copied(t - 2))
                for half in range(2):
                    pe.wait_ge(lo_ready, 2 * c + half + 1)
                    w = [split_piece(x, c, (2, 256), half) for x in wS]
                    for tb in range(TB):
                        for a, b in TERMS:
                            last = mm(tile_bank(t, tb)[:, half * 256:(half + 1) * 256],
                                      xT[a][:, k, tb * P:(tb + 1) * P], w[b][:, 0, :], (a, b) == (0, 0), (a, b) == TERMS[-1])
                    last.then_inc(piece_used, 1)

            def full(c, n):
                return [(c, (KD // 2, n), range(0, 4)), (c + 1, (KD // 2, n), range(4, 8))]

            pe.wait_ge(sem("ident_ready"), 1)
            pe.wait_ge(sem("rows_here"), 16 * N_ROW_DMAS)
            pe.transpose(B[4][:, 0:P], gain_rows[:, :], ident[:, :])
            pe.transpose(B[5][0:HB, 0:TAPS * QKB], conv_rows[:, :], ident[0:TAPS * QKB, 0:TAPS * QKB]).then_inc(
                sem("gains_psum"), 1)

            transpose_rows(lambda t, k: mem_rows[t][:, k * P:(k + 1) * P], KD, normed=0)
            pe.wait_ge(sem("gains_ready"), 2)
            transpose_rows(lambda t, k: xr[:, t, k * P:(k + 1) * P], KD, bank0=4, normed=TB)

            pe.wait_ge(sem("xT_ready"), 2)
            columns(full(C_MEM, 512), 512, B[0:2], ready=0)
            pe.wait_ge(sem("xT_ready"), 6)
            proj(full(C_GM, 264), 264, ready=4)

            def gates_turned():
                pe.wait_ge(sem("tile_evacuated"), 1)
                for g in range(2):
                    for t in range(TB):
                        last = pe.transpose(B[6][0:LH, g * S + t * P:g * S + (t + 1) * P],
                                            gm[:, t, g * LH:(g + 1) * LH], ident[:, :])
                last.then_inc(sem("gates_psum"), 1)
                for pair in range(2):
                    for t in range(TB):
                        last = pe.transpose(B[7][:, pair * S + t * P:pair * S + (t + 1) * P],
                                            gm[:, t, 2 * LH + pair * P:2 * LH + (pair + 1) * P], ident[:, :])
                last.then_inc(sem("qmT_psum"), 1)

            def keys_turned():
                pe.wait_ge(sem("km_normed"), 1)
                for pair in range(2):
                    for t in range(TB):
                        last = pe.transpose(B[4][:, pair * S + t * P:pair * S + (t + 1) * P],
                                            km[:, t, pair * P:(pair + 1) * P], ident[:, :])
                last.then_inc(sem("kmT_psum"), 1)

            def peaks():
                pe.wait_ge(sem("gate_rows_ready"), 1)
                for g, row in enumerate((3, 5)):
                    for t in range(TB):
                        last = pe.transpose(B[5][:, (g * TB + t) * LH:(g * TB + t + 1) * LH],
                                            gr[:, row, t * P:(t + 1) * P], ident[0:LH, 0:LH])
                last.then_inc(sem("gate_cols_psum"), 1)
                for hd in range(LH):
                    last = mm(B[6 + hd // 2][:, (hd % 2) * S:(hd % 2 + 1) * S], headsel[:, hd, :], gr[:, 4, :], True, True)
                last.then_inc(sem("peak_psum"), 1)

            pe.wait_ge(sem("mem_copied"), 1)
            for t in range(4):
                if t >= 2:
                    pe.wait_ge(sem("qk_copied"), t - 1)
                for j in range(2):
                    c = C_QK + 2 * t + j
                    for half in range(2):
                        pe.wait_ge(lo_ready, 2 * c + half + 1)
                        w = [split_piece(x, c, (4, 384), half) for x in wS]
                        for q in range(4):
                            dst = B[2 * (t % 2) + q // 2][0:HB, (q % 2) * S:(q % 2 + 1) * S]
                            for i in range(2):
                                k = 4 * j + 2 * half + i
                                for a, b in TERMS:
                                    last = mm(dst, w[a][:, i, q * HB:(q + 1) * HB], xT[b][:, k, :],
                                              start=(k == 0 and q % 2 == 0 and (a, b) == (0, 0)),
                                              stop=(k == KD - 1 and (a, b) == TERMS[-1]))
                        last.then_inc(piece_used, 1)
                    if (t, j) == (0, 0):
                        gates_turned()
                    if (t, j) == (1, 0):
                        keys_turned()
                    if (t, j) == (1, 1):
                        peaks()

            def mem_scores(layer, kmTs):
                pe.wait_ge(sem("mem_ops_ready"), layer + 1)
                for hd in range(MH):
                    r = slice(MD * (hd % 2), MD * (hd % 2) + MD)
                    for t in range(TB):
                        last = mm(B[hd][:, t * S:(t + 1) * S], qmT[r, hd // 2, t * P:(t + 1) * P],
                                  kmTs[r, hd // 2, :], True, True)
                    last.then_inc(sem("mem_scores"), 1)

            def mem_turned(layer):
                for hd in range(MH):
                    pe.wait_ge(sem("mem_probs"), MH * layer + hd + 1)
                    for t in range(TB):
                        for mb in range(2):
                            last = pe.transpose(B[hd][:, (t * 2 + mb) * P:(t * 2 + mb + 1) * P],
                                                pm(t, hd)[:, mb * P:(mb + 1) * P], ident[:, :])
                    last.then_inc(sem("mem_pT_psum"), 1)

            def mem_sums(layer, pmT):
                for hd in range(MH):
                    pe.wait_ge(sem("mem_pT"), MH * layer + hd + 1)
                    for t in range(TB):
                        for mb in range(2):
                            last = mm(B[0][:, (t * MH + hd) * MD:(t * MH + hd + 1) * MD],
                                      pmT(hd)[:, (t * 2 + mb) * P:(t * 2 + mb + 1) * P],
                                      vm[:, mb, hd * MD:(hd + 1) * MD], mb == 0, mb == 1)
                last.then_inc(sem("mem_out_psum"), 1)

            def head_scores():
                pe.wait_ge(sem("mem_added"), 1)
                for hd in range(LH):
                    pe.wait_ge(sem("qk_silu"), 3 + hd // 2)
                    for sbk in range(TB):
                        cols = slice(0, S) if sbk == 0 else slice(S, S + P)
                        for i in range(2):
                            last = mm(B[hd][:, cols], qkT[:, QKB // 2 + 2 * hd + i, sbk * P:(sbk + 1) * P],
                                      qkT[:, 2 * hd + i, sbk * P:S], i == 0, i == 1)
                    last.then_inc(sem("mscores_psum"), 1)

            def head_sums():
                for hd in range(LH):
                    pe.wait_ge(sem("mweights_ready"), hd + 1)
                    bank = B[hd]
                    mm(bank[:, 0:LD + 1], decay[:, hd, 0:P], vA[:, 0, hd, 0:LD + 1], True, True)
                    mm(bank[:, S:S + LD + 1], decay[:, hd, P:S], vA[:, 0, hd, 0:LD + 1], True, False)
                    mm(bank[:, S:S + LD + 1], decay[:, hd, S:S + P], vA[:, 1, hd, 0:LD + 1], False, True).then_inc(
                        sem("mnum_psum"), 1)

            pe.wait_ge(sem("decay_exp"), LH)
            pe.wait_ge(sem("qk_copied"), 4)
            proj(full(C_V, 384), 384, between=lambda: mem_scores(0, kmTs_0))
            pe.wait_ge(sem("kmT_ready"), 1)
            proj(full(C_V + 2, 384), 384, between=lambda: mem_turned(0))
            mem_sums(0, pmT_0)
            proj(full(C_V + 4, 384), 384, between=head_scores)
            pe.wait_ge(sem("tile_evacuated"), 3)
            head_sums()
            proj(full(C_V + 6, 384), 384)
            pe.wait_ge(sem("y_ready"), 1)
            transpose_rows(lambda t, k: y[:, t, k * P:(k + 1) * P], KD)
            for t in range(2):
                proj(full(C_OUT0 + 2 * t, 512), 512, ready=8, rows_first=t == 1)

            transpose_rows(lambda t, k: xr[:, t, k * P:(k + 1) * P], KD, normed=2 * TB)

            def ffn_in(c, which, more, ready=None):
                for j in range(4):
                    if ready is not None:
                        pe.wait_ge(sem("xT_ready"), ready + max(j + 1, 2))
                    pe.wait_ge(lo_ready, 2 * c + j + 1 + 2 * more)
                    w = [split_piece(x, c + j // 2, UP, j % 2) for x in wS]
                    for q in range(FB):
                        dst = B[2 * which + q // 2][:, (q % 2) * S:(q % 2 + 1) * S]
                        for i in range(2):
                            k = 2 * j + i
                            for a, b in TERMS:
                                last = mm(dst, w[a][:, i, q * P:(q + 1) * P], xT[b][:, k, :],
                                          start=(k == 0 and q % 2 == 0 and (a, b) == (0, 0)),
                                          stop=(k == KD - 1 and (a, b) == TERMS[-1]))
                    last.then_inc(piece_used, 1)

            def ffn_down(c, more, start):
                for j in range(4):
                    pe.wait_ge(lo_ready, 2 * c + j + 1 + 2 * more)
                    w = [split_piece(x, c + j // 2, DOWN, j % 2) for x in wS]
                    for t in range(TB):
                        for half in range(2):
                            for a, b in TERMS:
                                last = mm(B[4 + 2 * t + half][:, :], aT[a][:, j, t * P:(t + 1) * P],
                                          w[b][:, 0, half * 512:(half + 1) * 512],
                                          start=(start and j == 0 and (a, b) == (0, 0)), stop=False)
                    last.then_inc(piece_used, 1)

            ffn_in(C_FFN, 0, 0, ready=12)
            ffn_in(C_FFN + 2, 1, 0)

            def ffn_step(i, n, start):
                c, more = C_FFN + 4, 6 * i
                pe.wait_ge(sem("silu_done"), n + 1)
                ffn_in(c, 0, more)
                pe.wait_ge(sem("act_done"), n + 1)
                ffn_in(c + 2, 1, more)
                pe.wait_ge(sem("aT_ready"), n + 1)
                ffn_down(c + 4, more, start)

            ffn_step(0, 0, True)
            with pe.Fori(1, NF - 1) as i:
                ffn_step(i, i, False)
            pe.wait_ge(sem("aT_ready"), NF)
            c = C_FFN + 40
            pe.wait_ge(lo_ready, 2 * c + 4)
            for t in range(TB):
                for half in range(2):
                    for j in range(4):
                        w = [split_piece(x, c + j // 2, DOWN, j % 2) for x in wS]
                        for a, b in TERMS:
                            last = mm(B[4 + 2 * t + half][:, :], aT[a][:, j, t * P:(t + 1) * P],
                                      w[b][:, 0, half * 512:(half + 1) * 512], False, j == 3 and (a, b) == TERMS[-1])
                        if (t, half) == (TB - 1, 1):
                            last.then_inc(piece_used, 1)
                    if (t, half) != (TB - 1, 1):
                        last.then_inc(sem("ffn_out"), 1)

            transpose_rows(lambda t, k: xr[:, t, k * P:(k + 1) * P], KD, normed=3 * TB)
            proj(full(C_IN1, 512), 512, ready=16)
            proj(full(C_IN1 + 2, 320), 320)
            pe.wait_ge(sem("lora_normed"), 1)
            transpose_rows(lambda t, k: c1[:, t, k * P:(k + 1) * P], 4)

            def uq(t):
                proj([(C_UQ + t, (3, 384), range(3))], 384, ready=20)

            uq(0)
            pe.wait_ge(sem("tile_evacuated"), copied(TILE_IN1 + 1))
            for pair in range(2):
                for t in range(TB):
                    last = pe.transpose(B[2][:, pair * S + t * P:pair * S + (t + 1) * P],
                                        c2[:, t, ROPE + pair * P:ROPE + (pair + 1) * P], ident[:, :])
            last.then_inc(sem("qmT_psum"), 1)
            uq(1)
            mem_scores(1, kmTs_1)
            uq(2)
            for t in range(3):
                proj_one_k(C_UKV + t, 3)
            mem_turned(1)
            mem_sums(1, pmT_1)

            pe.wait_ge(sem("q_ready"), 1)
            pe.wait_ge(sem("mem_added"), 2)
            pe.wait_ge(sem("tile_evacuated"), copied(TILE_IN1 + 7))
            for b in range(3):
                for hd in (2 * b, 2 * b + 1):
                    for t in range(TB):
                        last = pe.transpose(B[b][:, (hd % 2) * S + t * P:(hd % 2) * S + (t + 1) * P],
                                            qS[:, t, hd, 0:NOPE], ident[:, :])
                last.then_inc(sem("headsT_psum"), 1)

            def pairs_turned(src, b0):
                for j in range(3):
                    for t in range(TB):
                        last = pe.transpose(B[b0 + j // 2][:, (j % 2) * S + t * P:(j % 2) * S + (t + 1) * P],
                                            src[:, t, 2 * j:2 * j + 2, :].rearrange("p h d -> p (h d)"), ident[:, :])
                    if j:
                        last.then_inc(sem("headsT_psum"), 1)

            pairs_turned(rotq, 3)
            pe.wait_ge(sem("k_ready"), 1)
            for b in range(3):
                for hd in (2 * b, 2 * b + 1):
                    for t in range(TB):
                        last = pe.transpose(B[5 + b][:, (hd % 2) * S + t * P:(hd % 2) * S + (t + 1) * P],
                                            kS[:, t, hd, :], ident[:, :])
                last.then_inc(sem("headsT_psum"), 1)
            pe.wait_ge(sem("headsT_ready"), 2)
            pairs_turned(rotk, 0)
            pe.wait_ge(sem("headsT_ready"), 10)
            for hd in range(AH):
                r = slice(ROPE * (hd % 2), ROPE * (hd % 2) + ROPE)
                for t in range(TB):
                    dst = B[hd][:, 0:P] if t == 0 else B[hd][:, P:P + S]
                    q, k = slice(t * P, (t + 1) * P), slice(0, (t + 1) * P)
                    mm(dst, qT[:, hd, q], kT[:, hd, k], True, False)
                    last = mm(dst, qrT[r, hd // 2, q], krT[r, hd // 2, k], False, True)
                last.then_inc(sem("scores_psum"), 1)
            for hd in range(AH):
                pe.wait_ge(sem("probs_ready"), hd + 1)
                for i in range(3):
                    last = pe.transpose(B[(6 + hd) % 8][:, i * P:(i + 1) * P], scr[:, hd, i * P:(i + 1) * P], ident[:, :])
                last.then_inc(sem("pT_psum"), 1)
            for hd in range(AH):
                pe.wait_ge(sem("pT_ready"), hd + 1)
                for t in range(TB):
                    bank, col = (B[4 + t], hd * VD) if hd < 4 else (B[6], (t * 2 + hd - 4) * VD)
                    if t == 0:
                        last = mm(bank[:, col:col + VD], pT[:, hd, 0:P], vS[:, 0, hd, :], True, True)
                    else:
                        mm(bank[:, col:col + VD], pT[:, hd, P:S], vS[:, 0, hd, :], True, False)
                        last = mm(bank[:, col:col + VD], pT[:, hd, S:S + P], vS[:, 1, hd, :], False, True)
            last.then_inc(sem("heads_psum"), 1)
            pe.wait_ge(sem("heads_out"), TB)
            transpose_rows(lambda t, k: y[:, t, k * P:(k + 1) * P], KD)
            for t in range(2):
                proj(full(C_OUT1 + 2 * t, 512), 512, ready=22, rows_first=t == 1)

            transpose_rows(lambda t, k: xr[:, t, k * P:(k + 1) * P], KD, normed=4 * TB)
            wr = (wr_hi, wr_lo)
            for k in range(KD):
                if k % 2 == 0:
                    pe.wait_ge(sem("xT_ready"), 26 + k // 2 + 1)
                for a, b in TERMS:
                    last = mm(B[4][0:NE, 0:S], wr[a][:, k, :], xT[b][:, k, :],
                              k == 0 and (a, b) == (0, 0), k == KD - 1 and (a, b) == TERMS[-1])
            last.then_inc(sem("logits_psum"), 1)
            pe.wait_ge(sem("logits_copied"), 1)
            for t in range(TB):
                last = pe.transpose(B[5][:, S + t * NE:S + (t + 1) * NE], lgT[:, t * P:(t + 1) * P], ident[0:NE, 0:NE])
            last.then_inc(sem("logits_psum"), 1)
            pe.wait_ge(sem("routed"), 1)
            mask = rt[:, 5]
            mm(B[5][:, 0:NE], before[:, :], mask[:, 0, :], True, True)
            mm(B[5][:, NE:2 * NE], ones[:, :], mask[:, 0, :], True, False)
            mm(B[5][:, NE:2 * NE], before[:, :], mask[:, 1, :], False, True)
            mm(B[5][:, 2 * NE:3 * NE], ones[:, :], mask[:, 0, :], True, False)
            mm(B[5][:, 2 * NE:3 * NE], ones[:, :], mask[:, 1, :], False, True).then_inc(sem("slots_psum"), 1)

            def gather(u):
                pe.wait_ge(sem("onehot_ready"), u + 1)
                for k in range(KD):
                    n = 0
                    for rows_x in (xr_hi, xr_lo):
                        for t in range(TB):
                            last = mm(B[k // 4][:, (k % 4) * P:(k % 4 + 1) * P], rows_x[:, t, k * P:(k + 1) * P],
                                      onehot[:, t, :], n == 0, n == 3)
                            n += 1
                    if k % 4 == 3:
                        last.then_inc(sem("gather_psum"), 1)

            def turn(u):
                for t in range(TB):
                    mm(B[3][:, S:S + 1], F(onehot[:, t, :]), cur[:, 2, t:t + 1], t == 0, t == TB - 1)
                for t in range(TB):
                    last = pe.transpose(B[3][:, t * P:(t + 1) * P], F(onehot[:, t, :]), ident[:, :])
                last.then_inc(sem("turn_psum"), 1)

            def e_in(c, which, more):
                for j in range(4):
                    pe.wait_ge(lo_ready, 2 * c + j + 1 + 2 * more)
                    w = [split_piece(x, c + j // 2, UP, j % 2) for x in wS]
                    for i in range(2):
                        k = 2 * j + i
                        for a, b in TERMS:
                            last = mm(B[which][:, :], xT[a][:, k, 0:P], w[b][:, i, :],
                                      start=(k == 0 and (a, b) == (0, 0)), stop=(k == KD - 1 and (a, b) == TERMS[-1]))
                    last.then_inc(piece_used, 1)

            def e_turn(n):
                pe.wait_ge(sem("eact_done"), n + 1)
                for q in range(FB):
                    last = pe.transpose(B[2][:, q * P:(q + 1) * P], act_f[:, q * P:(q + 1) * P], ident[:, :])
                last.then_inc(sem("eaT_psum"), 1)

            def e_down(c, more, n, start, stop):
                pe.wait_ge(sem("eaT_ready"), n + 1)
                for j in range(4):
                    pe.wait_ge(lo_ready, 2 * c + j + 1 + 2 * more)
                    w = [split_piece(x, c + j // 2, DOWN, j % 2) for x in wS]
                    for half in range(2):
                        for a, b in TERMS:
                            last = mm(B[4 + half][:, :], aT[a][:, j, 0:P], w[b][:, 0, half * 512:(half + 1) * 512],
                                      start=(start and j == 0 and (a, b) == (0, 0)),
                                      stop=(stop and j == 3 and (a, b) == TERMS[-1]))
                    last.then_inc(piece_used, 1)

            def back(u):
                pe.wait_ge(sem("ys_ready"), 2 * u + 2)
                for t in range(TB):
                    for half in range(2):
                        if t:
                            pe.wait_ge(sem("h_added"), 4 * u + half + 1)
                        for n, ys in enumerate((ys_hi, ys_lo)):
                            last = mm(B[6 + half][:, :], onehotT[:, t * P:(t + 1) * P],
                                      ys[:, half * 512:(half + 1) * 512], n == 0, n == 1)
                        last.then_inc(sem("back_psum"), 1)

            def start_unit(u):
                gather(u)
                pe.wait_ge(sem("gather_ready"), 2 * u + 2)
                e_in(C_MOE, 0, FFN_CHUNKS * u)

            def unit(u, last=False):
                more, n0 = FFN_CHUNKS * u, NF * u
                e_in(C_MOE + 2, 1, more)

                def e_step(i, start):
                    c, m = C_MOE + 4, more + 6 * i
                    pe.wait_ge(sem("esilu_done"), n0 + i + 1)
                    e_in(c, 0, m)
                    e_turn(n0 + i)
                    e_in(c + 2, 1, m)
                    e_down(c + 4, m, n0 + i, start, False)

                e_step(0, True)
                with pe.Fori(1, NF - 1) as i:
                    e_step(i, False)
                e_turn(n0 + NF - 1)
                if not last:
                    gather(u + 1)
                e_down(C_MOE + 40, more, n0 + NF - 1, False, True)
                if not last:
                    pe.wait_ge(sem("gather_ready"), 2 * u + 4)
                    e_in(C_MOE + FFN_CHUNKS, 0, more)
                back(u)
                if not last:
                    turn(u + 1)

            start_unit(0)
            turn(0)
            with pe.Fori(0, NE - 1) as u:
                unit(u)
            unit(NE - 1, last=True)
            pe.wait_ge(sem("units_known"), 1)
            for j in range(NU_MAX):
                n_over = pe.value_load(unit_i[0:1, 3:4], min_val=0, max_val=NU_MAX)
                with pe.If(n_over > j):
                    start_unit(NE + j)
                    turn(NE + j)
                    unit(NE + j, last=True)

        @block.scalar
        def _(act):
            steps = [0]

            def step(ins):
                steps[0] += 1
                ins.then_inc(sem("act_step"), 1)

            def settle():
                act.wait_ge(sem("act_step"), steps[0])

            done = [0]

            def split_high(p, shape, more=0, lap=0):
                c, half = p // 2, p % 2
                if half == 0:
                    act.wait_ge(raw_here[c % RAW_SLOTS], 16 * (c // RAW_SLOTS + 1) + 16 * lap)
                if p >= SPLIT_SLOTS:
                    act.wait_ge(piece_used, p - SPLIT_SLOTS + 1 + 2 * more)
                act.activation(split_piece(w_hi, c, shape, half), raw_piece(c, shape, half), ACT.Copy).then_inc(hi_ready, 1)

            def splits_to(p):
                while done[0] <= p:
                    split_high(done[0], shape_of(done[0] // 2))
                    done[0] += 1

            def sumsq(rows_t, col, junk):
                return act.activation(junk, rows_t, ACT.Square, accum_out=stat[:, 0, col:col + 1])

            def norm_rows(halves_there):
                name, counts = halves_there
                for half in range(2):
                    for t in range(TB):
                        if half == 0:
                            act.wait_ge(sem(name), counts[t])
                        else:
                            rows_added[0] += 1
                            act.wait_ge(sem("rows_added"), rows_added[0])
                        r = slice(half * 512, (half + 1) * 512)
                        sumsq(h[:, t, r], 2 * t + half, xr[:, t, r]).then_inc(sem("sumsq_ready"), 1)

            rows_added = [0]

            def high_T(nk, base, gain, bank0=0, after=None):
                for b in range(nk // 2):
                    act.wait_ge(sem("xT_psum"), base + b + 1)
                    if after is not None:
                        act.wait_ge(piece_used, after + b + 1)
                    for kk in range(2):
                        k = 2 * b + kk
                        ins = act.activation(xT_hi[:, k, :], B[bank0 + b][:, kk * S:(kk + 1) * S], ACT.Copy,
                                             scale=1.0 if gain is None else gains[:, gain + k:gain + k + 1])
                    ins.then_inc(sem("xT_hi_ready"), 1)

            def whole(c):
                act.wait_ge(piece_used, 2 * c)

            act.wait_ge(sem("ident_ready"), 1)
            act.activation(small[:, 63:64], iota[:, 0:1], ACT.Square)
            for t in range(TB):
                act.wait_ge(sem("mem_here"), 16 * TB)
                sumsq(mem_rows[t], t, flat3(xT_hi[:, :, :])[:, t * D:(t + 1) * D]).then_inc(sem("sumsq_ready"), 1)
            for t in range(TB):
                act.wait_ge(sem("x_here"), 16 * TB)
                sumsq(h[:, t, :], TB + t, xr[:, t, :]).then_inc(sem("sumsq_ready"), 1)
            act.wait_ge(sem("gains_psum"), 1)
            act.activation(gains[:, :], B[4][:, 0:P], ACT.Copy).then_inc(sem("gains_ready"), 1)
            act.activation(convw[:, :], B[5][0:HB, 0:TAPS * QKB], ACT.Copy).then_inc(sem("gains_ready"), 1)
            act.wait_ge(sem("gains_ready"), 2)
            high_T(KD, 0, G["mem"])
            splits_to(2 * C_GM + 1)
            high_T(KD, 4, G["mix0"], bank0=4, after=0)
            splits_to(2 * C_GM + 3)
            whole(C_MEM + 2)
            for t in range(TB):
                act.activation(vm[:, t, :], B[t][:, MEMW:2 * MEMW], ACT.Copy).then_inc(sem("vm_copied"), 1)
            splits_to(2 * C_QK + 1)
            whole(C_GM + 2)
            for tb in range(TB):
                ins = act.activation(gm[:, tb, :], tile_bank(0, tb)[:, 0:264], ACT.Copy)
            ins.then_inc(sem("tile_evacuated"), 1)

            def qk_out(t):
                whole(C_QK + 2 * t + 2)
                if t >= 2:
                    act.wait_ge(sem("conv_done"), t - 1)
                for b in range(2):
                    act.activation(qk_in[:, t % 2, 2 * b:2 * b + 2, TAPS - 1:],
                                   B[2 * (t % 2) + b][0:HB, :].rearrange("p (q s) -> p q s", q=2), ACT.Copy)
                for q in range(4):
                    b = 4 * t + q
                    w = (TAPS - 1) * QKB + b
                    ins = act.activation(qkT[:, b, :], B[2 * (t % 2) + q // 2][0:HB, (q % 2) * S:(q % 2 + 1) * S], ACT.Copy,
                                         scale=convw[:, w:w + 1])
                ins.then_inc(sem("qk_copied"), 1)

            splits_to(2 * C_QK + 7)
            act.wait_ge(sem("gate_abs"), 1)
            step(act.activation(gr[:, 1, :], gr[:, 1, :], ACT.Exp, scale=-1.0))
            settle()
            act.activation(gr[:, 1, :], gr[:, 1, :], ACT.Ln, bias=1.0).then_inc(sem("gate_ln"), 1)
            qk_out(0)
            splits_to(2 * C_QK + 9)
            act.wait_ge(sem("gate_m"), 1)
            act.activation(gr[:, 5, :], gr[:, 5, :], ACT.Exp, scale=-1.0).then_inc(sem("gate_rows_ready"), 1)
            splits_to(2 * C_QK + 11)
            act.wait_ge(sem("kmT_psum"), 1)
            act.activation(kmT[:, :, :].rearrange("p a s -> p (a s)"), B[4][:, :], ACT.Copy).then_inc(sem("kmT_ready"), 1)
            qk_out(1)
            splits_to(2 * C_QK + 15)
            for hd in range(LH):
                act.wait_ge(sem("decay_exp"), hd + 1)
                act.activation(decay[:, hd, :], decay[:, hd, :], ACT.Exp, scale=-1.0).then_inc(sem("decay_ready"), 1)
            qk_out(2)
            splits_to(2 * C_V + 3)
            qk_out(3)
            splits_to(2 * C_V + 7)

            def mem_exps(layer):
                act.wait_ge(sem("mem_bias"), layer + 1)
                for hd in range(MH):
                    for t in range(TB):
                        c = t * MH + hd
                        ins = act.activation(pm(t, hd), B[hd][:, t * S:(t + 1) * S], ACT.Exp,
                                             bias=msmall[:, 1, c:c + 1], scale=msmall[:, 0, c:c + 1],
                                             accum_out=msmall[:, 2, c:c + 1])
                    ins.then_inc(sem("mem_probs"), 1)

            def mem_turned(layer, pmT):
                for hd in range(MH):
                    act.wait_ge(sem("mem_pT_psum"), MH * layer + hd + 1)
                    act.activation(pmT(hd), B[hd][:, :], ACT.Copy).then_inc(sem("mem_pT"), 1)

            def values_out(t):
                whole(C_V + 2 * t + 2)
                for tb in range(TB):
                    ins = act.activation(vA[:, tb, 2 * t:2 * t + 2, 0:LD],
                                         tile_bank(1 + t, tb)[:, 0:384].rearrange("p (h d) -> p h d", h=2), ACT.Copy)
                ins.then_inc(sem("tile_evacuated"), 1)

            def gates_out(t):
                whole(C_V + 4 + 2 * t + 2)
                for tb in range(TB):
                    ins = act.activation(og[:, tb, 384 * t:384 * t + 384], tile_bank(3 + t, tb)[:, 0:384], ACT.Sigmoid)
                ins.then_inc(sem("tile_evacuated"), 1)

            mem_exps(0)
            values_out(0)
            splits_to(2 * C_V + 9)
            mem_turned(0, pmT_0)
            splits_to(2 * C_V + 11)
            for q in range(4):
                act.wait_ge(sem("conv_done"), q + 1)
                act.activation(qkT[:, 4 * q:4 * q + 4, :], qkT[:, 4 * q:4 * q + 4, :], ACT.Silu).then_inc(sem("qk_silu"), 1)
            values_out(1)
            splits_to(2 * C_V + 15)
            act.wait_ge(sem("mem_out_psum"), 1)
            gates_out(0)
            splits_to(2 * C_OUT0 + 1)
            act.wait_ge(sem("mnum_psum"), LH)
            for hd in range(LH):
                for t in range(TB):
                    c = t * LH + hd
                    ins = act.activation(flat3(decay[:, :, :])[:, c * LD:(c + 1) * LD], B[hd][:, t * S:t * S + LD],
                                         ACT.Square, accum_out=stat[:, 0, c:c + 1])
                ins.then_inc(sem("head_sumsq"), 1)
            splits_to(2 * C_OUT0 + 3)
            gates_out(1)
            high_T(KD, 8, None)
            splits_to(2 * C_OUT0 + 7)
            act.wait_ge(sem("angles_ready"), 1)
            act.activation(sin[:, :, :], angle[:, 2, :, :], ACT.Sin).then_inc(sem("rope_ready"), 1)
            act.activation(cos[:, :, :], angle[:, 3, :, :], ACT.Sin).then_inc(sem("rope_ready"), 1)
            splits_to(2 * C_FFN + 3)

            norm_rows(("tile_evacuated", (copied(TILE_OUT0),) * TB))
            high_T(KD, 12, G["ffn0"])

            def silu_gate(c, more, n):
                act.wait_ge(piece_used, 2 * (c + more))
                if not isinstance(n, int) or n > 0:
                    act.wait_ge(sem("act_done"), n)
                for b in range(2):
                    ins = act.activation(silu_g[:, b * 512:(b + 1) * 512], B[b][:, :], ACT.Silu)
                ins.then_inc(sem("silu_done"), 1)

            def high_act(c, more, n):
                act.wait_ge(sem("act_done"), n + 1)
                act.wait_ge(piece_used, 2 * (c + more))
                act.activation(aT_hi[:, :, :].rearrange("p q s -> p (q s)"), act_f[:, :], ACT.Copy).then_inc(
                    sem("aT_hi_ready"), 1)

            def ffn_body(i, next_shape):
                c, more = C_FFN + 4, 6 * i

                def pieces(a, b):
                    for j in range(a, b):
                        split_high(2 * c + j, DOWN if 8 <= j < 12 else UP if j < 8 else next_shape, more, i)

                pieces(4, 6)
                high_act(c, more, i)
                pieces(6, 9)
                silu_gate(c + 2, more, i + 1)
                pieces(9, 16)

            p0 = 2 * C_FFN
            for j in (4, 5):
                split_high(p0 + j, UP)
            silu_gate(C_FFN + 2, 0, 0)
            for j in range(6, 12):
                split_high(p0 + j, UP)
            with act.Fori(0, NF - 2) as i:
                ffn_body(i, UP)
            ffn_body(NF - 2, DOWN)
            high_act(C_FFN + 40, 0, NF - 1)
            done[0] = 2 * C_IN1
            splits_to(2 * C_IN1 + 1)

            norm_rows(("half_added", (1, 2)))
            splits_to(2 * C_IN1 + 3)
            high_T(KD, 16, G["mix1"])
            splits_to(2 * C_IN1 + 7)
            act.wait_ge(piece_used, 2 * (C_IN1 + 2))
            for tb in range(TB):
                ins = act.activation(c1[:, tb, :], tile_bank(TILE_IN1, tb)[:, :], ACT.Copy)
            ins.then_inc(sem("tile_evacuated"), 1)
            splits_to(2 * (C_UQ + 1) + 1)
            act.wait_ge(piece_used, 2 * (C_IN1 + 4))
            for tb in range(TB):
                ins = act.activation(c2[:, tb, :], tile_bank(TILE_IN1 + 1, tb)[:, 0:320], ACT.Copy)
            ins.then_inc(sem("tile_evacuated"), 1)
            high_T(4, 20, G["cq"])
            splits_to(2 * C_UQ + 5)

            def uq_out(t):
                whole(C_UQ + t + 1)
                for tb in range(TB):
                    ins = act.activation(qS[:, tb, 2 * t:2 * t + 2, :].rearrange("p h d -> p (h d)"),
                                         tile_bank(TILE_IN1 + 2 + t, tb)[:, 0:384], ACT.Copy)
                ins.then_inc(sem("tile_evacuated"), 1)

            def ukv_out(t):
                whole(C_UKV + t + 1)
                for tb in range(TB):
                    src = tile_bank(TILE_IN1 + 5 + t, tb)[:, :].rearrange("p (h d) -> p h d", h=2)
                    act.activation(kS[:, tb, 2 * t:2 * t + 2, :], src[:, :, 0:NOPE], ACT.Copy)
                    ins = act.activation(vS[:, tb, 2 * t:2 * t + 2, :], src[:, :, NOPE:], ACT.Copy)
                ins.then_inc(sem("tile_evacuated"), 1)

            for t in range(3):
                uq_out(t)
                splits_to(2 * (C_UKV + t) + 1)
            mem_exps(1)
            for t in range(3):
                ukv_out(t)
            mem_turned(1, pmT_1)
            splits_to(2 * C_OUT1 + 5)

            for b in range(3):
                act.wait_ge(sem("headsT_psum"), b + 1)
                act.activation(qT[:, 2 * b:2 * b + 2, :].rearrange("p h s -> p (h s)"), B[b][:, :], ACT.Copy,
                               scale=small[:, 60:61]).then_inc(sem("headsT_ready"), 1)

            def pairs(dst, b0, n):
                act.wait_ge(sem("headsT_psum"), n + 1)
                act.activation(dst[:, 0:2, :].rearrange("p h s -> p (h s)"), B[b0][:, :], ACT.Copy).then_inc(
                    sem("headsT_ready"), 1)
                act.wait_ge(sem("headsT_psum"), n + 2)
                act.activation(dst[:, 2, :], B[b0 + 1][:, 0:S], ACT.Copy).then_inc(sem("headsT_ready"), 1)

            pairs(qrT, 3, 3)
            for b in range(3):
                act.wait_ge(sem("headsT_psum"), 5 + b + 1)
                act.activation(kT[:, 2 * b:2 * b + 2, :].rearrange("p h s -> p (h s)"), B[5 + b][:, :], ACT.Copy).then_inc(
                    sem("headsT_ready"), 1)
            pairs(krT, 0, 8)
            def probs_turned(hd):
                act.wait_ge(sem("pT_psum"), hd + 1)
                act.activation(pT[:, hd, :], B[(6 + hd) % 8][:, 0:384], ACT.Copy).then_inc(sem("pT_ready"), 1)

            for hd in range(AH):
                act.wait_ge(sem("score_bias"), hd + 1)
                for t in range(TB):
                    c = t * AH + hd
                    part_s = scr[:, hd, 0:P] if t == 0 else scr[:, hd, P:P + S]
                    ins = act.activation(part_s, part_s, ACT.Exp, bias=small[:, 12 + c:13 + c], scale=small[:, c:c + 1],
                                         accum_out=small[:, 24 + c:25 + c])
                ins.then_inc(sem("probs_ready"), 1)
                if hd:
                    probs_turned(hd - 1)
            probs_turned(AH - 1)
            high_T(KD, 22, None)
            splits_to(2 * (C_MOE + 1) + 1)

            norm_rows(("tile_evacuated", (copied(TILE_OUT1),) * TB))
            high_T(KD, 26, G["ffn1"])
            act.wait_ge(sem("rows_normed"), 10)
            for t in range(TB):
                act.activation(xr_hi[:, t, :], xr[:, t, :], ACT.Copy).then_inc(sem("xr_hi_ready"), 1)
            act.wait_ge(sem("top_diff"), 1)
            act.activation(rt[:, 8, :, 0:1], rt[:, 7, :, 0:1], ACT.Exp).then_inc(sem("top_exp"), 1)

            def gathered(u):
                for b in range(2):
                    act.wait_ge(sem("gather_psum"), 2 * u + b + 1)
                    for kk in range(4):
                        k = 4 * b + kk
                        ins = act.activation(xT_hi[:, k, 0:P], B[b][:, kk * P:(kk + 1) * P], ACT.Copy,
                                             scale=gains[:, G["ffn1"] + k:G["ffn1"] + k + 1])
                    ins.then_inc(sem("gather_hi"), 1)

            def e_silu(c, more, n):
                act.wait_ge(piece_used, 2 * (c + more))
                if n is not None:
                    act.wait_ge(sem("eact_done"), n)
                act.activation(silu_g[:, 0:FC], B[0][:, :], ACT.Silu).then_inc(sem("esilu_done"), 1)

            def e_high(n):
                act.wait_ge(sem("eaT_psum"), n + 1)
                act.activation(aT_hi[:, :, 0:P], B[2][:, :].rearrange("p (q s) -> p q s", q=FB), ACT.Copy).then_inc(
                    sem("eaT_hi"), 1)

            def unit(u, last=False):
                more, lap, n0, p0 = FFN_CHUNKS * u, NF * u, NF * u, 2 * C_MOE

                for j in (4, 5):
                    split_high(p0 + j, UP, more, lap)
                e_silu(C_MOE + 2, more, None)
                for j in (6, 7):
                    split_high(p0 + j, UP, more, lap)
                act.wait_ge(sem("turn_psum"), u + 1)
                act.activation(onehotT[:, :], B[3][:, 0:S], ACT.Copy)
                act.activation(gslot[:, :], B[3][:, S:S + 1], ACT.Copy).then_inc(sem("turned"), 1)
                for j in range(8, 12):
                    split_high(p0 + j, UP, more, lap)

                def e_step(i, next_shape):
                    c, m, lp = C_MOE + 4, more + 6 * i, lap + i

                    def pieces(a, b):
                        for j in range(a, b):
                            split_high(2 * c + j, DOWN if 8 <= j < 12 else UP if j < 8 else next_shape, m, lp)

                    pieces(4, 9)
                    e_high(n0 + i)
                    e_silu(c + 2, m, n0 + i + 1)
                    pieces(9, 16)

                with act.Fori(0, NF - 2) as i:
                    e_step(i, UP)
                e_step(NF - 2, DOWN)
                e_high(n0 + NF - 1)
                if not last:
                    for j in (0, 1):
                        split_high(p0 + 2 * FFN_CHUNKS + j, UP, more, lap)
                    gathered(u + 1)
                    for j in (2, 3):
                        split_high(p0 + 2 * FFN_CHUNKS + j, UP, more, lap)
                act.wait_ge(piece_used, 2 * (C_MOE + FFN_CHUNKS + more))
                for half in range(2):
                    act.activation(ys_hi[:, half * 512:(half + 1) * 512], B[4 + half][:, :], ACT.Copy,
                                   scale=gslot[:, 0:1]).then_inc(sem("ys_hi"), 1)

            gathered(0)
            with act.Fori(0, NE - 1) as u:
                unit(u)
            unit(NE - 1, last=True)
            act.wait_ge(sem("units_known"), 1)
            for j in range(NU_MAX):
                n_over = act.value_load(unit_i[0:1, 3:4], min_val=0, max_val=NU_MAX)
                with act.If(n_over > j):
                    for i in range(4):
                        split_high(2 * C_MOE + i, UP, FFN_CHUNKS * (NE + j), NF * (NE + j))
                    gathered(NE + j)
                    unit(NE + j, last=True)

        @block.vector
        def _(dve):
            steps = [0]

            def step(ins):
                steps[0] += 1
                ins.then_inc(sem("dve_step"), 1)

            def settle():
                dve.wait_ge(sem("dve_step"), steps[0])

            def chain(ins):
                step(ins)
                settle()

            done = [0]

            def split_low(p, shape, more=0):
                c, half = p // 2, p % 2
                dve.wait_ge(hi_ready, p + 1 + 2 * more)
                dve.tensor_tensor(split_piece(w_lo, c, shape, half), raw_piece(c, shape, half),
                                  F(split_piece(w_hi, c, shape, half)), ALU.subtract).then_inc(lo_ready, 1)

            def splits_to(p):
                while done[0] <= p:
                    split_low(done[0], shape_of(done[0] // 2))
                    done[0] += 1

            def variance(n, width, c0=0):
                chain(dve.tensor_scalar(stat[:, 1, c0:c0 + n], stat[:, 0, c0:c0 + n], 1.0 / width, EPS, ALU.mult, ALU.add))

            def rsqrt(n, c0=0):
                v, t, r = stat[:, 1, c0:c0 + n], stat[:, 2, c0:c0 + n], stat[:, 4, c0:c0 + n]
                chain(dve.tensor_scalar(t.bitcast(I32), v.bitcast(I32), 1, None, ALU.logical_shift_right))
                chain(dve.tensor_scalar(r.bitcast(I32), t.bitcast(I32), -1.0, RSQRT_BITS, ALU.mult, ALU.add))
                for i in range(3):
                    chain(dve.tensor_tensor(t, r, r, ALU.mult))
                    chain(dve.scalar_tensor_tensor(out=t, in0=t, scalar=0.25 ** i, in1=v, op0=ALU.mult, op1=ALU.mult))
                    chain(dve.scalar_tensor_tensor(out=r, in0=t, scalar=-3.0, in1=r, op0=ALU.add, op1=ALU.mult))
                chain(dve.tensor_scalar(r, r, -0.125, None, ALU.mult))

            sums = [2 * TB]

            def norm_rows():
                sums[0] += 2 * TB
                dve.wait_ge(sem("sumsq_ready"), sums[0])
                chain(dve.tensor_reduce(stat[:, 3, 0:TB], stat[:, 0, 0:2 * TB].rearrange("p (t a) -> p t a", t=TB), AX, ALU.add))
                chain(dve.tensor_scalar(stat[:, 1, 0:TB], stat[:, 3, 0:TB], 1.0 / D, EPS, ALU.mult, ALU.add))
                rsqrt(TB)
                for t in range(TB):
                    dve.tensor_scalar(xr[:, t, :], h[:, t, :], stat[:, 4, t:t + 1], None, ALU.mult).then_inc(
                        sem("rows_normed"), 1)

            def low_T(nk, base, gain, bank0=0):
                for b in range(nk // 2):
                    dve.wait_ge(sem("xT_hi_ready"), base + b + 1)
                    for kk in range(2):
                        k = 2 * b + kk
                        ins = dve.scalar_tensor_tensor(
                            out=xT_lo[:, k, :], in0=B[bank0 + b][:, kk * S:(kk + 1) * S],
                            scalar=1.0 if gain is None else gains[:, gain + k:gain + k + 1],
                            in1=F(xT_hi[:, k, :]), op0=ALU.mult, op1=ALU.subtract)
                    ins.then_inc(sem("xT_ready"), 1)

            for n in range(2):
                dve.wait_ge(sem("sumsq_ready"), TB * (n + 1))
                variance(TB, D, n * TB)
                rsqrt(TB, n * TB)
                for t in range(TB):
                    src, dst = (mem_rows[t], mem_rows[t]) if n == 0 else (h[:, t, :], xr[:, t, :])
                    dve.tensor_scalar(dst, src, stat[:, 4, n * TB + t:n * TB + t + 1], None, ALU.mult).then_inc(
                        sem("rows_normed"), 1)
            dve.wait_ge(sem("gains_ready"), 2)
            low_T(KD, 0, G["mem"])
            splits_to(2 * C_GM + 1)
            low_T(KD, 4, G["mix0"], bank0=4)
            splits_to(2 * C_GM + 3)
            for t in range(TB):
                dve.wait_ge(sem("vm_copied"), t + 1)
                ins = dve.tensor_copy(km[:, t, :], B[t][:, 0:MEMW])
            ins.then_inc(sem("mem_copied"), 1)
            splits_to(2 * C_QK + 1)
            dve.wait_ge(sem("mem_copied"), 1)

            def head_sums(src, dst, scratch):
                chain(dve.tensor_tensor(scratch, src, src, ALU.mult))
                chain(dve.tensor_reduce(dst, scratch, AX, ALU.add))

            kmv = km[:, :, :].rearrange("p t (h d) -> p (t h) d", h=MH)
            head_sums(kmv, stat[:, 0, 0:TB * MH], og[:, 0, 0:TB * MEMW].rearrange("p (n d) -> p n d", n=TB * MH))
            dve.wait_ge(sem("tile_evacuated"), 1)
            head_sums(gm[:, :, 2 * LH:].rearrange("p t (h d) -> p t h d", h=MH),
                      stat[:, 0, 8:16].rearrange("p (t h) -> p t h", t=TB),
                      og[:, 1, 0:TB * MEMW].rearrange("p (t h d) -> p t h d", t=TB, h=MH))
            variance(16, MD)
            rsqrt(16)
            step(dve.tensor_copy(msmall[:, 0, :], stat[:, 4, 8:16]))
            dve.tensor_tensor(kmv, kmv, stat[:, 4, 0:TB * MH].unsqueeze(2).to_broadcast([P, TB * MH, MD]),
                              ALU.mult).then_inc(sem("km_normed"), 1)
            splits_to(2 * C_QK + 3)

            dve.wait_ge(sem("bias_here"), 16 * 3)
            dve.wait_ge(sem("gates_psum"), 1)
            step(dve.tensor_scalar(gr[:, 0, :], B[6][0:LH, 0:S], gate_bias[:, 0:1], None, ALU.add))
            chain(dve.tensor_scalar(gr[:, 2, :], B[6][0:LH, S:2 * S], gate_bias[:, 1:2], None, ALU.add))
            dve.scalar_tensor_tensor(out=gr[:, 1, :], in0=gr[:, 2, :], scalar=-1.0, in1=gr[:, 2, :], op0=ALU.mult,
                                     op1=ALU.max).then_inc(sem("gate_abs"), 1)
            step(dve.tensor_scalar(gr[:, 2, :], gr[:, 2, :], 0.0, None, ALU.min))
            dve.wait_ge(sem("qmT_psum"), 1)
            step(dve.tensor_copy(qmT[:, :, :].rearrange("p a s -> p (a s)"), B[7][:, :]))
            splits_to(2 * C_QK + 7)
            dve.wait_ge(sem("gate_ln"), 1)
            settle()
            chain(dve.tensor_tensor(gr[:, 2, :], gr[:, 2, :], gr[:, 1, :], ALU.subtract))
            dve.wait_ge(sem("consts_ready"), 1)
            chain(dve.memset(gr[:, 7, :], 1.0))
            chain(dve.tensor_tensor_scan(gr[:, 6, :], gr[:, 7, :], gr[:, 2, :], 0.0, ALU.mult, ALU.add))
            chain(dve.tensor_tensor(gr[:, 3, :], gr[:, 0, :], gr[:, 6, :], ALU.subtract))
            chain(dve.tensor_tensor_scan(gr[:, 4, :], gr[:, 7, :], gr[:, 3, :], 0.0, ALU.mult, ALU.max))
            dve.tensor_tensor(gr[:, 5, :], gr[:, 6, :], gr[:, 4, :], ALU.add).then_inc(sem("gate_m"), 1)

            def conv(t):
                dve.wait_ge(sem("qk_copied"), t + 1)
                for tap in range(TAPS - 2, -1, -1):
                    if tap < TAPS - 2:
                        settle()
                    for q in range(4):
                        b = 4 * t + q
                        ins = dve.scalar_tensor_tensor(
                            out=qkT[:, b, :], in0=qk_in[:, t % 2, q, tap:tap + S],
                            scalar=convw[:, tap * QKB + b:tap * QKB + b + 1], in1=qkT[:, b, :],
                            op0=ALU.mult, op1=ALU.add)
                        if tap == 0 and q == 3:
                            ins.then_inc(sem("conv_done"), 1)
                        else:
                            step(ins)

            conv(0)
            splits_to(2 * C_QK + 11)
            dve.wait_ge(sem("gate_cols_psum"), 1)
            chain(dve.tensor_copy(small[:, 0:2 * TB * LH], B[5][:, 0:2 * TB * LH]))
            conv(1)
            splits_to(2 * C_QK + 13)
            dve.wait_ge(sem("peak_psum"), 1)
            for hd in range(LH):
                peak = B[6 + hd // 2][:, (hd % 2) * S:(hd % 2 + 1) * S]
                step(dve.tensor_scalar(decay[:, hd, 0:S], peak, small[:, hd:hd + 1], 0.0, ALU.subtract, ALU.max))
                dve.tensor_scalar(decay[:, hd, S:S + P], peak[:, P:S], small[:, LH + hd:LH + hd + 1], 0.0, ALU.subtract,
                                  ALU.max).then_inc(sem("decay_exp"), 1)
            splits_to(2 * C_QK + 15)
            conv(2)
            splits_to(2 * C_V + 3)
            chain(dve.tensor_tensor(small[:, 40:41], gains[:, G_MQ[0]:G_MQ[0] + 1], gains[:, G_MK[0]:G_MK[0] + 1], ALU.mult))
            dve.wait_ge(sem("kmT_ready"), 1)
            dve.tensor_scalar(kmTs_0, kmT[:, :, :], small[:, 40:41], float(MD) ** -0.5, ALU.mult, ALU.mult).then_inc(
                sem("mem_ops_ready"), 1)
            for hd in range(LH):
                dve.wait_ge(sem("decay_ready"), hd + 1)
                diag = decay[:, hd, :].rearrange("p (b c) -> p b c", b=3)[:, 0:3:2, :]
                step(dve.tensor_tensor(diag, diag, upto[:, :, :], ALU.mult))
            conv(3)

            def mem_max(layer):
                for hd in range(MH):
                    dve.wait_ge(sem("mem_scores"), MH * layer + hd + 1)
                    step(dve.tensor_reduce(msmall[:, 3, hd:hd + MH + 1:MH],
                                           B[hd][:, :].rearrange("p (t s) -> p t s", t=TB), AX, ALU.max))
                settle()
                dve.scalar_tensor_tensor(out=msmall[:, 1, :], in0=msmall[:, 3, :], scalar=-1.0, in1=msmall[:, 0, :],
                                         op0=ALU.mult, op1=ALU.mult).then_inc(sem("mem_bias"), 1)

            def mem_out(layer):
                dve.wait_ge(sem("mem_probs"), MH * (layer + 1))
                chain(dve.reciprocal(msmall[:, 3, :], msmall[:, 2, :]))
                dve.wait_ge(sem("mem_out_psum"), layer + 1)
                dve.tensor_tensor(
                    y[:, :, MAIN:].rearrange("p t (h d) -> p t h d", h=MH),
                    B[0][:, :].rearrange("p (t h d) -> p t h d", t=TB, h=MH),
                    msmall[:, 3, :].rearrange("p (t h) -> p t h", t=TB).unsqueeze(3).to_broadcast([P, TB, MH, MD]),
                    ALU.mult).then_inc(sem("mem_added"), 1)

            mem_max(0)
            splits_to(2 * C_V + 9)
            splits_to(2 * C_V + 11)
            mem_out(0)
            splits_to(2 * C_V + 13)
            for hd in range(LH):
                dve.wait_ge(sem("mscores_psum"), hd + 1)
                if hd == 0:
                    settle()
                dve.scalar_tensor_tensor(out=decay[:, hd, :], in0=B[hd][:, 0:384], scalar=float(LD) ** -0.5,
                                         in1=decay[:, hd, :], op0=ALU.mult, op1=ALU.mult).then_inc(
                    sem("mweights_ready"), 1)
            splits_to(2 * C_V + 15)
            ogv = og[:, :, :].rearrange("p t (h d) -> p t h d", h=LH)

            def gate_gain(t):
                dve.wait_ge(sem("tile_evacuated"), 4 + t)
                for tb in range(TB):
                    step(dve.tensor_tensor(ogv[:, tb, 2 * t:2 * t + 2, :], ogv[:, tb, 2 * t:2 * t + 2, :],
                                           hnorm_bc[:, :].unsqueeze(1).to_broadcast([P, 2, LD]), ALU.mult))

            gate_gain(0)
            splits_to(2 * C_OUT0 + 1)
            rec = small[:, 16:24].rearrange("p (t h) -> p t h", t=TB)
            for hd in range(LH):
                dve.wait_ge(sem("head_sumsq"), hd + 1)
                den = B[hd][:, LD:LD + S + 1:S]
                step(dve.tensor_scalar(small[:, 24 + hd:24 + hd + LH + 1:LH], den, -1.0, None, ALU.mult))
                settle()
                step(dve.tensor_tensor(rec[:, :, hd], small[:, 24 + hd:24 + hd + LH + 1:LH], den, ALU.max))
            settle()
            chain(dve.tensor_tensor(small[:, 16:24], small[:, 16:24], small[:, 8:16], ALU.max))
            chain(dve.reciprocal(small[:, 16:24], small[:, 16:24]))
            chain(dve.tensor_tensor(stat[:, 0, 0:8], stat[:, 0, 0:8], small[:, 16:24], ALU.mult))
            chain(dve.tensor_tensor(stat[:, 0, 0:8], stat[:, 0, 0:8], small[:, 16:24], ALU.mult))
            variance(8, LD)
            rsqrt(8)
            chain(dve.tensor_tensor(small[:, 24:32], small[:, 16:24], stat[:, 4, 0:8], ALU.mult))

            def heads_out(pair):
                for hd in (2 * pair, 2 * pair + 1):
                    for t in range(TB):
                        c = t * LH + hd
                        ins = dve.scalar_tensor_tensor(out=y[:, t, hd * LD:(hd + 1) * LD], in0=B[hd][:, t * S:t * S + LD],
                                                       scalar=small[:, 24 + c:25 + c], in1=ogv[:, t, hd, :], op0=ALU.mult,
                                                       op1=ALU.mult)
                        if hd < LH - 1 or t < TB - 1:
                            step(ins)
                ins.then_inc(sem("y_ready"), 1) if pair else None

            heads_out(0)
            gate_gain(1)
            settle()
            heads_out(1)
            splits_to(2 * C_OUT0 + 3)
            low_T(KD, 8, None)
            splits_to(2 * C_OUT0 + 7)
            dve.wait_ge(sem("tables_here"), 16 * 4)
            chain(dve.tensor_copy(small[:, 0:TB], pos_i[:, :]))
            for t in range(TB):
                step(dve.tensor_scalar(angle[:, 0, t, :], angle[:, 0, t, :], small[:, t:t + 1], None, ALU.mult))
            settle()
            for i, shift in ((2, 0.0), (3, 0.25)):
                chain(dve.tensor_scalar(angle[:, 1], angle[:, 0], INV_2PI, shift, ALU.mult, ALU.add))
                chain(dve.tensor_scalar(angle[:, 1], angle[:, 1], MAGIC, None, ALU.add))
                chain(dve.tensor_scalar(angle[:, 1], angle[:, 1], MAGIC, None, ALU.subtract))
                chain(dve.scalar_tensor_tensor(out=angle[:, i], in0=angle[:, 1], scalar=-TWO_PI[0], in1=angle[:, 0],
                                               op0=ALU.mult, op1=ALU.add))
                for part_c in TWO_PI[1:]:
                    chain(dve.scalar_tensor_tensor(out=angle[:, i], in0=angle[:, 1], scalar=-part_c, in1=angle[:, i],
                                                   op0=ALU.mult, op1=ALU.add))
                if shift:
                    chain(dve.tensor_scalar(angle[:, i], angle[:, i], HALF_PI, None, ALU.add))
                chain(dve.tensor_scalar(angle[:, i], angle[:, i], PI_BOUND, -PI_BOUND, ALU.min, ALU.max))
            chain(dve.tensor_copy(wr_hi[:, :, :], w_router[:, :, :]))
            dve.tensor_tensor(wr_lo[:, :, :], w_router[:, :, :], F(wr_hi[:, :, :]), ALU.subtract).then_inc(
                sem("angles_ready"), 1)

            first_rows = [0]

            def add_tile(t, c, half):
                for tb in range(TB):
                    if half and tb == 0:
                        first_rows[0] += 1
                        dve.wait_ge(sem("first_rows"), first_rows[0])
                    else:
                        dve.wait_ge(piece_used, 2 * (c + 2))
                    ins = dve.tensor_tensor(h[:, tb, half * 512:(half + 1) * 512], tile_bank(t, tb)[:, :],
                                            h[:, tb, half * 512:(half + 1) * 512], ALU.add)
                    if half:
                        ins.then_inc(sem("rows_added"), 1)
                if not half:
                    ins.then_inc(sem("tile_evacuated"), 1)

            add_tile(TILE_OUT0, C_OUT0, 0)
            splits_to(2 * C_FFN + 3)
            add_tile(TILE_OUT0 + 1, C_OUT0 + 2, 1)

            norm_rows()
            low_T(KD, 12, G["ffn0"])

            def product(c, more, n, first=False):
                dve.wait_ge(sem("silu_done"), n + 1)
                dve.wait_ge(piece_used, 2 * (c + more))
                if not first:
                    dve.wait_ge(sem("aT_ready"), n)
                for b in range(2):
                    ins = dve.tensor_tensor(act_f[:, b * 512:(b + 1) * 512], B[2 + b][:, :],
                                            silu_g[:, b * 512:(b + 1) * 512], ALU.mult)
                ins.then_inc(sem("act_done"), 1)

            def low_act(n):
                dve.wait_ge(sem("aT_hi_ready"), n + 1)
                dve.tensor_tensor(aT_lo[:, :, :].rearrange("p q s -> p (q s)"), act_f[:, :],
                                  F(aT_hi[:, :, :]).rearrange("p q s -> p (q s)"), ALU.subtract).then_inc(sem("aT_ready"), 1)

            def ffn_body(i, next_shape):
                c, more = C_FFN + 4, 6 * i

                def pieces(a, b):
                    for j in range(a, b):
                        split_low(2 * c + j, DOWN if 8 <= j < 12 else UP if j < 8 else next_shape, more)

                pieces(4, 6)
                low_act(i)
                pieces(6, 13)
                product(c + 4, more, i + 1)
                pieces(13, 16)

            p0 = 2 * C_FFN
            for j in range(4, 8):
                split_low(p0 + j, UP)
            product(C_FFN + 4, 0, 0, first=True)
            for j in range(8, 12):
                split_low(p0 + j, UP)
            with dve.Fori(0, NF - 2) as i:
                ffn_body(i, UP)
            ffn_body(NF - 2, DOWN)
            low_act(NF - 1)
            done[0] = 2 * C_IN1
            splits_to(2 * C_IN1 + 1)
            for t in range(TB):
                for half in range(2):
                    if (t, half) == (TB - 1, 1):
                        dve.wait_ge(piece_used, 2 * C_IN1)
                    else:
                        dve.wait_ge(sem("ffn_out"), 2 * t + half + 1)
                    dve.tensor_tensor(h[:, t, half * 512:(half + 1) * 512], B[4 + 2 * t + half][:, :],
                                      h[:, t, half * 512:(half + 1) * 512], ALU.add).then_inc(
                        sem("rows_added" if half else "half_added"), 1)

            norm_rows()
            splits_to(2 * C_IN1 + 3)
            low_T(KD, 16, G["mix1"])
            splits_to(2 * C_IN1 + 7)
            dve.wait_ge(sem("tile_evacuated"), copied(TILE_IN1))
            lora = scr[:, 0:4, :].rearrange("p a b -> p (a b)")[:, 0:TB * 512].rearrange("p (t n) -> p t n", t=TB)
            chain(dve.tensor_tensor(lora, c1[:, :, :], c1[:, :, :], ALU.mult))
            step(dve.tensor_reduce(stat[:, 0, 0:TB], lora[:, :, 0:QL], AX, ALU.add))
            chain(dve.tensor_reduce(stat[:, 0, TB:2 * TB], lora[:, :, QL:], AX, ALU.add))
            variance(TB, QL, 0)
            variance(TB, P, TB)
            rsqrt(2 * TB)
            for t in range(TB):
                step(dve.tensor_scalar(c1[:, t, 0:QL], c1[:, t, 0:QL], stat[:, 4, t:t + 1], None, ALU.mult))
                ins = dve.tensor_scalar(c1[:, t, QL:], c1[:, t, QL:], stat[:, 4, TB + t:TB + t + 1], None, ALU.mult)
                if t == TB - 1:
                    ins.then_inc(sem("lora_normed"), 1)
            splits_to(2 * C_UQ + 3)
            low_T(4, 20, G["cq"])
            step(dve.tensor_tensor(small[:, 60:61], gains[:, G_QN:G_QN + 1], gains[:, G_KN:G_KN + 1], ALU.mult))
            step(dve.tensor_tensor(small[:, 61:62], gains[:, G_MQ[1]:G_MQ[1] + 1], gains[:, G_MK[1]:G_MK[1] + 1], ALU.mult))
            dve.wait_ge(sem("tile_evacuated"), copied(TILE_IN1 + 1))
            head_sums(c2[:, :, ROPE:].rearrange("p t (h d) -> p t h d", h=MH),
                      stat[:, 0, 0:8].rearrange("p (t h) -> p t h", t=TB),
                      flat3(scr[:, :, :])[:, 0:TB * MEMW].rearrange("p (t h d) -> p t h d", t=TB, h=MH))
            variance(8, MD)
            rsqrt(8)
            step(dve.tensor_copy(msmall[:, 0, :], stat[:, 4, 0:8]))
            dve.wait_ge(sem("qmT_psum"), 2)
            step(dve.tensor_copy(qmT[:, :, :].rearrange("p a s -> p (a s)"), B[2][:, :]))
            settle()
            dve.tensor_scalar(kmTs_1, kmT[:, :, :], small[:, 61:62], float(MD) ** -0.5, ALU.mult, ALU.mult).then_inc(
                sem("mem_ops_ready"), 1)
            splits_to(2 * C_UQ + 5)
            dve.wait_ge(sem("rope_ready"), 2)
            k_r = c2[:, :, 0:ROPE]
            step(dve.tensor_tensor(kr[:, 0], k_r, k_r, ALU.mult))
            chain(dve.tensor_tensor(kr[:, 1], k_r, krope_bc[:, :].unsqueeze(1).to_broadcast([P, TB, ROPE]), ALU.mult))
            step(dve.tensor_reduce(stat[:, 0, 32:34], kr[:, 0], AX, ALU.add))

            def halves(ap):
                return (ap[:, :, 0:HALF], ap[:, :, HALF:ROPE]) if len(ap.shape) == 3 else (
                    ap[:, :, :, 0:HALF], ap[:, :, :, HALF:ROPE])

            def rotate(dst, src, t1, t2, c, s):
                (a, b), (da, db) = halves(src), halves(dst)
                step(dve.tensor_tensor(t1, a, c, ALU.mult))
                chain(dve.tensor_tensor(t2, b, s, ALU.mult))
                chain(dve.tensor_tensor(da, t1, t2, ALU.subtract))
                step(dve.tensor_tensor(t1, b, c, ALU.mult))
                chain(dve.tensor_tensor(t2, a, s, ALU.mult))
                return dve.tensor_tensor(db, t1, t2, ALU.add)

            step(rotate(kr[:, 2], kr[:, 1], kr[:, 3, :, 0:HALF], kr[:, 3, :, HALF:], cos[:, :, :], sin[:, :, :]))
            splits_to(2 * C_UKV + 3)
            mem_max(1)
            splits_to(2 * C_UKV + 5)
            dve.wait_ge(sem("tile_evacuated"), copied(TILE_IN1 + 4))
            H12 = TB * AH
            sq = scr[:, :, :].rearrange("p a b -> p (a b)")
            qv = qS[:, :, :, :].rearrange("p t h d -> p (t h) d")
            kv = kS[:, :, :, :].rearrange("p t h d -> p (t h) d")
            head_sums(qv, stat[:, 0, 0:H12], sq[:, 0:H12 * QKD].rearrange("p (h d) -> p h d", h=H12))
            chain(dve.tensor_tensor(rotq[:, :, :, :].rearrange("p t h d -> p (t h) d"), qv[:, :, NOPE:],
                                    qrope_bc[:, :].unsqueeze(1).to_broadcast([P, H12, ROPE]), ALU.mult))
            q0 = sq[:, 0:H12 * ROPE].rearrange("p (t h d) -> p t h d", t=TB, h=AH)
            chain(dve.tensor_copy(q0, rotq[:, :, :, :]))
            cb = cos[:, :, :].unsqueeze(2).to_broadcast([P, TB, AH, HALF])
            sbb = sin[:, :, :].unsqueeze(2).to_broadcast([P, TB, AH, HALF])
            t1, t2 = (sq[:, (2 + i) * H12 * HALF:(3 + i) * H12 * HALF].rearrange("p (t h d) -> p t h d", t=TB, h=AH)
                      for i in range(2))
            rotate(rotq[:, :, :, :], q0, t1, t2, cb, sbb).then_inc(sem("q_ready"), 1)
            dve.wait_ge(sem("q_ready"), 1)
            mem_out(1)
            dve.wait_ge(sem("tile_evacuated"), copied(TILE_IN1 + 7))
            head_sums(kv, stat[:, 0, H12:2 * H12], sq[:, 0:H12 * NOPE].rearrange("p (h d) -> p h d", h=H12))
            kss = stat[:, 0, H12:2 * H12].rearrange("p (t h) -> p t h", t=TB)
            chain(dve.tensor_tensor(kss, kss, stat[:, 0, 32:34].unsqueeze(2).to_broadcast([P, TB, AH]), ALU.add))
            variance(2 * H12, QKD)
            rsqrt(2 * H12)
            rk = stat[:, 4, H12:2 * H12]
            step(dve.tensor_tensor(kv, kv, rk.unsqueeze(2).to_broadcast([P, H12, NOPE]), ALU.mult))
            rkv = rk.rearrange("p (t h) -> p t h", t=TB)
            for t in range(TB):
                step(dve.tensor_tensor(rotk[:, t], kr[:, 2, t, :].unsqueeze(1).to_broadcast([P, AH, ROPE]),
                                       rkv[:, t].unsqueeze(2).to_broadcast([P, AH, ROPE]), ALU.mult))
            settle()
            dve.tensor_scalar(small[:, 0:H12], stat[:, 4, 0:H12], float(QKD) ** -0.5, None, ALU.mult).then_inc(
                sem("k_ready"), 1)
            splits_to(2 * C_OUT1 + 1)
            for hd in range(AH):
                dve.wait_ge(sem("scores_psum"), hd + 1)
                chain(dve.tensor_tensor(scr[:, hd, :].rearrange("p (b c) -> p b c", b=3),
                                       B[hd][:, 0:384].rearrange("p (b c) -> p b c", b=3), negmask[:, :, :], ALU.add))
                top = stat[:, 3, 3 * hd:3 * hd + 3]
                chain(dve.tensor_reduce(top, scr[:, hd, :].rearrange("p (b c) -> p b c", b=3), AX, ALU.max))
                chain(dve.tensor_tensor(top[:, 1:2], top[:, 1:2], top[:, 2:3], ALU.max))
                dve.scalar_tensor_tensor(out=small[:, 12 + hd:12 + hd + AH + 1:AH], in0=top[:, 0:2], scalar=-1.0,
                                         in1=small[:, hd:hd + AH + 1:AH], op0=ALU.mult, op1=ALU.mult).then_inc(
                    sem("score_bias"), 1)
            splits_to(2 * C_OUT1 + 5)
            dve.wait_ge(sem("probs_ready"), AH)
            chain(dve.reciprocal(small[:, 36:48], small[:, 24:36]))
            dve.wait_ge(sem("heads_psum"), 1)
            rs = small[:, 36:48].rearrange("p (t h) -> p t h", t=TB)
            for t in range(TB):
                step(dve.tensor_tensor(y[:, t, 0:4 * VD].rearrange("p (h d) -> p h d", h=4),
                                       B[4 + t][:, :].rearrange("p (h d) -> p h d", h=4),
                                       rs[:, t, 0:4].unsqueeze(2).to_broadcast([P, 4, VD]), ALU.mult))
                ins = dve.tensor_tensor(y[:, t, 4 * VD:MAIN].rearrange("p (h d) -> p h d", h=2),
                                        B[6][:, t * 2 * VD:(t + 1) * 2 * VD].rearrange("p (h d) -> p h d", h=2),
                                        rs[:, t, 4:6].unsqueeze(2).to_broadcast([P, 2, VD]), ALU.mult)
                ins.then_inc(sem("heads_out"), 1)
            low_T(KD, 22, None)
            splits_to(2 * (C_OUT1 + 3) + 1)
            add_tile(TILE_OUT1, C_OUT1, 0)
            splits_to(2 * (C_MOE + 1) + 1)
            add_tile(TILE_OUT1 + 1, C_OUT1 + 2, 1)

            norm_rows()
            low_T(KD, 26, G["ffn1"])
            for t in range(TB):
                dve.wait_ge(sem("xr_hi_ready"), t + 1)
                step(dve.tensor_tensor(xr_lo[:, t, :], xr[:, t, :], F(xr_hi[:, t, :]), ALU.subtract))
            dve.wait_ge(sem("logits_psum"), 1)
            dve.tensor_copy(lgT[:, :], B[4][0:NE, 0:S]).then_inc(sem("logits_copied"), 1)
            dve.wait_ge(sem("logits_psum"), 2)
            chain(dve.tensor_copy(lg[:, :, :].rearrange("p t e -> p (t e)"), B[5][:, S:S + TB * NE]))
            for t in range(TB):
                own = lg[:, t, :].unsqueeze(2).to_broadcast([P, NE, NE])
                other = lg[:, t, :].unsqueeze(1).to_broadcast([P, NE, NE])
                step(dve.tensor_tensor(cmp[:, 0, t], other, own, ALU.is_gt))
                step(dve.tensor_tensor(cmp[:, 1, t], other, own, ALU.is_equal))
            settle()
            for t in range(TB):
                step(dve.tensor_tensor(cmp[:, 1, t], cmp[:, 1, t], earlier[:, :, :], ALU.mult))
            settle()
            chain(dve.tensor_tensor(cmp[:, 2], cmp[:, 0], cmp[:, 1], ALU.add))
            chain(dve.tensor_reduce(rt[:, 0], cmp[:, 2], AX, ALU.add))
            step(dve.tensor_scalar(rt[:, 1], rt[:, 0], 0.0, None, ALU.is_equal))
            step(dve.tensor_scalar(rt[:, 2], rt[:, 0], 1.0, None, ALU.is_equal))
            settle()
            step(dve.tensor_tensor(rt[:, 3], rt[:, 1], lg[:, :, :], ALU.mult))
            step(dve.tensor_tensor(rt[:, 4], rt[:, 2], lg[:, :, :], ALU.mult))
            dve.tensor_tensor(rt[:, 5], rt[:, 1], rt[:, 2], ALU.add).then_inc(sem("routed"), 1)
            settle()
            chain(dve.tensor_tensor(rt[:, 6], rt[:, 4], rt[:, 3], ALU.subtract))
            dve.tensor_reduce(rt[:, 7, :, 0], rt[:, 6], AX, ALU.add).then_inc(sem("top_diff"), 1)
            dve.wait_ge(sem("top_exp"), 1)
            chain(dve.tensor_scalar(rt[:, 9, :, 0:1], rt[:, 8, :, 0:1], 1.0, None, ALU.add))
            chain(dve.reciprocal(rt[:, 9, :, 0:1], rt[:, 9, :, 0:1]))
            chain(dve.tensor_tensor(rt[:, 10, :, 0:1], rt[:, 8, :, 0:1], rt[:, 9, :, 0:1], ALU.mult))
            for t in range(TB):
                step(dve.tensor_scalar(rt[:, 11, t, :], rt[:, 1, t, :], rt[:, 9, t, 0:1], None, ALU.mult))
            settle()
            for t in range(TB):
                step(dve.scalar_tensor_tensor(out=rt[:, 12, t, :], in0=rt[:, 2, t, :], scalar=rt[:, 10, t, 0:1],
                                              in1=rt[:, 11, t, :], op0=ALU.mult, op1=ALU.add))
            dve.wait_ge(sem("slots_psum"), 1)
            chain(dve.tensor_copy(posc[:, :, :].rearrange("p t e -> p (t e)"), B[5][:, 0:3 * NE]))
            for n, src in enumerate((posc[:, 0:TB, :], rt[:, 5], rt[:, 12])):
                step(dve.tensor_copy(tab[:, 0:NE, n, :].rearrange("p e t -> p t e"), src))
            def mark(u):
                dve.tensor_copy(cur[:, :, :].unsqueeze(1), tab[:, bass.ds(u, 1), :, :]).then_inc(sem("cur_ready"), 1)
                dve.wait_ge(sem("cur_ready"), u + 1)
                for t in range(TB):
                    ins = dve.tensor_scalar(onehot[:, t, :], iota[:, :], cur[:, 0, t:t + 1], cur[:, 1, t:t + 1],
                                            ALU.is_equal, ALU.mult)
                ins.then_inc(sem("onehot_ready"), 1)

            settle()
            mark(0)
            chain(dve.tensor_scalar(over[:, 0, :], posc[:, TB, :], float(P), None, ALU.is_gt))
            chain(dve.tensor_tensor_scan(over[:, 1, :], ones[:, 0:NE], over[:, 0, :], 0.0, ALU.mult, ALU.add))
            step(dve.tensor_scalar(rt[:, 13], posc[:, 0:TB, :], -float(P), None, ALU.add))
            step(dve.tensor_copy(unit_f[:, 3:4], over[0:1, 1, NE - 1:NE]))
            for j in range(NU_MAX):
                chain(dve.tensor_scalar(over[:, 2, :], over[:, 1, :], float(j + 1), None, ALU.is_equal))
                chain(dve.tensor_tensor(over[:, 2, :], over[:, 2, :], over[:, 0, :], ALU.mult))
                sel = over[:, 2, :].unsqueeze(1).to_broadcast([P, TB, NE])
                for n, src in enumerate((rt[:, 13], rt[:, 5], rt[:, 12])):
                    chain(dve.tensor_tensor(rt[:, 14], src, sel, ALU.mult))
                    chain(dve.tensor_reduce(tab[:, NE + j, n, :], rt[:, 14], AX, ALU.add))
                chain(dve.tensor_tensor(over[:, 3, :], over[:, 2, :], iota[:, 0:NE], ALU.mult))
                chain(dve.tensor_reduce(unit_f[:, j:j + 1], over[0:1, 3, :], AX, ALU.add))
            dve.tensor_copy(unit_i[:, :], unit_f[:, :]).then_inc(sem("units_known"), 1)

            def gathered(u):
                for b in range(2):
                    dve.wait_ge(sem("gather_hi"), 2 * u + b + 1)
                    for kk in range(4):
                        k = 4 * b + kk
                        ins = dve.scalar_tensor_tensor(
                            out=xT_lo[:, k, 0:P], in0=B[b][:, kk * P:(kk + 1) * P],
                            scalar=gains[:, G["ffn1"] + k:G["ffn1"] + k + 1], in1=F(xT_hi[:, k, 0:P]),
                            op0=ALU.mult, op1=ALU.subtract)
                    ins.then_inc(sem("gather_ready"), 1)

            def scaled(u):
                dve.wait_ge(sem("turned"), u + 1)
                for half in range(2):
                    dve.wait_ge(sem("ys_hi"), 2 * u + half + 1)
                    dve.scalar_tensor_tensor(out=ys_lo[:, half * 512:(half + 1) * 512], in0=B[4 + half][:, :],
                                             scalar=gslot[:, 0:1], in1=F(ys_hi[:, half * 512:(half + 1) * 512]),
                                             op0=ALU.mult, op1=ALU.subtract).then_inc(sem("ys_ready"), 1)

            def added(u):
                for t in range(TB):
                    for half in range(2):
                        dve.wait_ge(sem("back_psum"), 4 * u + 2 * t + half + 1)
                        dve.tensor_tensor(h[:, t, half * 512:(half + 1) * 512], B[6 + half][:, :],
                                          h[:, t, half * 512:(half + 1) * 512], ALU.add).then_inc(sem("h_added"), 1)

            def e_product(c, more, n):
                dve.wait_ge(sem("esilu_done"), n + 1)
                dve.wait_ge(piece_used, 2 * (c + more))
                dve.tensor_tensor(act_f[:, 0:FC], B[1][:, :], silu_g[:, 0:FC], ALU.mult).then_inc(sem("eact_done"), 1)

            def e_low(n):
                dve.wait_ge(sem("eaT_hi"), n + 1)
                dve.tensor_tensor(aT_lo[:, :, 0:P], B[2][:, :].rearrange("p (q s) -> p q s", q=FB),
                                  F(aT_hi[:, :, 0:P]), ALU.subtract).then_inc(sem("eaT_ready"), 1)

            def unit(u, last=False):
                more, n0, p0 = FFN_CHUNKS * u, NF * u, 2 * C_MOE

                for j in (6, 7):
                    split_low(p0 + j, UP, more)
                e_product(C_MOE + 4, more, n0)
                for j in range(8, 12):
                    split_low(p0 + j, UP, more)

                def e_step(i, next_shape):
                    c, m = C_MOE + 4, more + 6 * i

                    def pieces(a, b):
                        for j in range(a, b):
                            split_low(2 * c + j, DOWN if 8 <= j < 12 else UP if j < 8 else next_shape, m)

                    pieces(4, 9)
                    e_low(n0 + i)
                    pieces(9, 12)
                    e_product(c + 4, m, n0 + i + 1)
                    pieces(12, 16)

                with dve.Fori(0, NF - 2) as i:
                    e_step(i, UP)
                if not last:
                    mark(u + 1)
                e_step(NF - 2, DOWN)
                e_low(n0 + NF - 1)
                if last:
                    scaled(u)
                    added(u)
                    return
                for j in (0, 1):
                    split_low(p0 + 2 * FFN_CHUNKS + j, UP, more)
                gathered(u + 1)
                for j in (2, 3):
                    split_low(p0 + 2 * FFN_CHUNKS + j, UP, more)
                scaled(u)
                for j in (4, 5):
                    split_low(p0 + 2 * FFN_CHUNKS + j, UP, more)
                added(u)

            gathered(0)
            for j in (4, 5):
                split_low(2 * C_MOE + j, UP)
            with dve.Fori(0, NE - 1) as u:
                unit(u)
            unit(NE - 1, last=True)
            for j in range(NU_MAX):
                n_over = dve.value_load(unit_i[0:1, 3:4], min_val=0, max_val=NU_MAX)
                with dve.If(n_over > j):
                    mark(NE + j)
                    more = FFN_CHUNKS * (NE + j)
                    for i in range(4):
                        split_low(2 * C_MOE + i, UP, more)
                    gathered(NE + j)
                    for i in (4, 5):
                        split_low(2 * C_MOE + i, UP, more)
                    unit(NE + j, last=True)
            dve.drain().then_inc(sem("h_final"), 1)


_INS = [
    "x", "mem", "positions", "mem_norm", "w_mem_kv",
    "ln_mix0", "w_in0", "conv_w0", "b_i0", "b_f0", "h_norm0", "mq_norm0", "mk_norm0", "w_out0",
    "ln_ffn0", "w_gate0", "w_up0", "w_down0",
    "ln_mix1", "w_in1", "cq_norm1", "ckv_norm1", "w_uq1", "w_ukv1", "q_norm1", "k_norm1", "mq_norm1", "mk_norm1", "w_out1",
    "ln_ffn1", "w_router1", "we_gate1", "we_up1", "we_down1",
]


def kernel(**inputs):
    import numpy as _np
    import concourse.bacc as _bacc
    from concourse import mybir as _mybir
    from concourse.bass_utils import run_bass_kernel_spmd as _run

    nc = _bacc.Bacc("TRN2", target_bir_lowering=False, num_devices=1)
    arrays, args = {}, []
    for name in _INS:
        a = _np.ascontiguousarray(inputs[name])
        arrays[f"in_{name}_dram"] = a
        args.append(nc.dram_tensor(f"in_{name}_dram", a.shape, _mybir.dt.from_np(a.dtype), kind="ExternalInput").ap())
    shape = tuple(inputs["x"].shape)
    args.append(nc.dram_tensor("out_0_dram", shape, _mybir.dt.float32, kind="ExternalOutput").ap())
    hybrid_trunk(nc, *args)
    r = _run(nc, [arrays], core_ids=[0])
    return r.results[0]["out_0_dram"]
```
